# Optimizing a Trainium2 kernel written in Bass

```python
import jax, jax.numpy as jnp
from jax import lax
import numpy as np
import math

D_MODEL = 1024
BATCH = 1
SEQ = 256
DEPTH = 1

HEAD_DIM = 64
SB_HEADS = 8
DIL_GROUPS = ((128, 1), (512, 4), (2048, 16))
DIL_HEADS_PER_GROUP = 4
N_DIL_GROUPS = len(DIL_GROUPS)
DIL_HEADS = DIL_HEADS_PER_GROUP * N_DIL_GROUPS
SB_WIDTH = SB_HEADS * HEAD_DIM
DIL_WIDTH = DIL_HEADS * HEAD_DIM
DIL_OUT_WIDTH = DIL_HEADS_PER_GROUP * HEAD_DIM
IN_COLS = 3 * SB_WIDTH + 3 * DIL_WIDTH + 2 * D_MODEL
Q_BLOCK = 128
ROPE_THETA = 10000.0
PEER_HEADS = 8
PEER_NKEYS = 128
PEER_EXPERTS = PEER_NKEYS * PEER_NKEYS
PEER_QDIM = 256
PEER_HALF = PEER_QDIM // 2
PEER_TOPK = 16
PEER_TOKEN_CHUNK = 128
N_MOD = 6
EPS = 1e-6


def rms_norm(x, g):
    xf = x.astype(jnp.float32)
    y = xf * lax.rsqrt(jnp.mean(xf * xf, axis=-1, keepdims=True) + EPS)
    return (y * g.astype(jnp.float32)).astype(x.dtype)

def modulate(h, shift, scale):
    return h * (1.0 + scale[:, None, :]) + shift[:, None, :]

def rope(x, pos):
    half = HEAD_DIM // 2
    inv = ROPE_THETA ** (-jnp.arange(half, dtype=jnp.float32) / half)
    ang = pos.astype(jnp.float32)[:, None] * inv[None, :]
    cos = jnp.cos(ang)[None, :, None, :]
    sin = jnp.sin(ang)[None, :, None, :]
    xf = x.astype(jnp.float32)
    x1, x2 = xf[..., :half], xf[..., half:]
    return jnp.concatenate([x1 * cos - x2 * sin, x1 * sin + x2 * cos], axis=-1).astype(x.dtype)

def stick_breaking_attention(q, k, v):
    S = q.shape[1]
    scale = HEAD_DIM ** -0.5
    outs = []
    for blk in range(S // Q_BLOCK):
        t0 = blk * Q_BLOCK
        kl = t0 + Q_BLOCK
        qb, kb, vb = q[:, t0:kl], k[:, :kl], v[:, :kl]
        z = jnp.einsum('bqhd,bkhd->bhqk', qb, kb).astype(jnp.float32) * scale
        t_idx = t0 + jnp.arange(Q_BLOCK)
        s_idx = jnp.arange(kl)
        mask = s_idx[None, :] < t_idx[:, None]
        log_1m_beta = jnp.where(mask, jax.nn.log_sigmoid(-z), 0.0)
        after = lax.cumsum(log_1m_beta, axis=3, reverse=True) - log_1m_beta
        a = jnp.where(mask, jnp.exp(jax.nn.log_sigmoid(z) + after), 0.0)
        outs.append(jnp.einsum('bhqk,bkhd->bqhd', a.astype(v.dtype), vb))
    return jnp.concatenate(outs, axis=1)

def dilated_attention(q, k, v):
    B, S = q.shape[:2]
    scale = HEAD_DIM ** -0.5
    n_blocks = S // Q_BLOCK

    def block(blk):
        t = blk * Q_BLOCK + jnp.arange(Q_BLOCK)
        qb = lax.dynamic_slice_in_dim(q, blk * Q_BLOCK, Q_BLOCK, axis=1)
        outs, lses = [], []
        for g, (w, r) in enumerate(DIL_GROUPS):
            n = w // r + 1
            idx = t[:, None] - r * jnp.arange(n)[None, :]
            valid = idx >= 0
            idx_c = jnp.maximum(idx, 0)
            kg = jnp.take(k[:, :, g], idx_c, axis=1)
            vg = jnp.take(v[:, :, g], idx_c, axis=1)
            z = jnp.einsum('bqhd,bqnhd->bhqn', qb[:, :, g], kg).astype(jnp.float32) * scale
            z = jnp.where(valid[None, None], z, -jnp.inf)
            lse = jax.nn.logsumexp(z, axis=-1)
            p = jnp.exp(z - lse[..., None])
            outs.append(jnp.einsum('bhqn,bqnhd->bqhd', p.astype(vg.dtype), vg).astype(jnp.float32))
            lses.append(lse)
        wts = jax.nn.softmax(jnp.stack(lses, axis=0), axis=0)
        wts = jnp.transpose(wts, (0, 1, 3, 2))[..., None]
        return jnp.sum(wts * jnp.stack(outs, axis=0), axis=0).astype(q.dtype)

    out = lax.map(block, jnp.arange(n_blocks))
    return jnp.transpose(out, (1, 0, 2, 3, 4)).reshape(B, S, DIL_HEADS_PER_GROUP, HEAD_DIM)

def peer_ffn(h, w_pq, peer_keys, peer_u, peer_v):
    B, S, D = h.shape
    T = B * S
    ht = h.reshape(T, D)
    q = (ht @ w_pq).reshape(T, PEER_HEADS, 2, PEER_HALF)
    sub = jnp.einsum('thpc,hpnc->thpn', q, peer_keys).astype(jnp.float32)
    s_top, i_top = lax.top_k(sub, PEER_TOPK)
    cand_s = (s_top[:, :, 0, :, None] + s_top[:, :, 1, None, :]).reshape(T, PEER_HEADS, PEER_TOPK * PEER_TOPK)
    cand_i = (i_top[:, :, 0, :, None] * PEER_NKEYS + i_top[:, :, 1, None, :]).reshape(T, PEER_HEADS, PEER_TOPK * PEER_TOPK)
    best_s, pos = lax.top_k(cand_s, PEER_TOPK)
    expert = jnp.take_along_axis(cand_i, pos, axis=-1)
    gate = jax.nn.softmax(best_s, axis=-1)
    hk = PEER_HEADS * PEER_TOPK
    n_chunks = T // PEER_TOKEN_CHUNK

    def chunk(args):
        xc, ec, gc = args
        u = jnp.take(peer_u, ec, axis=0)
        act = jax.nn.gelu(jnp.einsum('cd,ckd->ck', xc, u))
        vv = jnp.take(peer_v, ec, axis=0)
        return jnp.einsum('ck,ckd->cd', gc.astype(xc.dtype) * act, vv)

    out = lax.map(chunk, (ht.reshape(n_chunks, PEER_TOKEN_CHUNK, D),
                          expert.reshape(n_chunks, PEER_TOKEN_CHUNK, hk),
                          gate.reshape(n_chunks, PEER_TOKEN_CHUNK, hk)))
    return out.reshape(B, S, D)

def first_inputs(seed: int = 0) -> dict:
    key = jax.random.key(seed)
    ks = jax.random.split(key, 16)
    D = D_MODEL
    f = jnp.float32
    nrm = lambda k, shape, s: jax.random.normal(k, shape, f) * s
    return {
        "x": nrm(ks[0], (BATCH, SEQ, D), 1.0),
        "c": nrm(ks[1], (BATCH, D), 1.0),
        "w_ada": nrm(ks[2], (DEPTH, D, N_MOD * D), 0.5 * D ** -0.5),
        "b_ada": nrm(ks[3], (DEPTH, N_MOD * D), 0.01),
        "g_mix": 1.0 + nrm(ks[4], (DEPTH, D), 0.02),
        "w_in": nrm(ks[5], (DEPTH, D, IN_COLS), D ** -0.5),
        "w_sb_o": nrm(ks[6], (DEPTH, SB_WIDTH, D), SB_WIDTH ** -0.5),
        "w_dil_o": nrm(ks[7], (DEPTH, DIL_OUT_WIDTH, D), DIL_OUT_WIDTH ** -0.5),
        "w_out": nrm(ks[8], (DEPTH, D, D), D ** -0.5),
        "g_ffn": 1.0 + nrm(ks[9], (DEPTH, D), 0.02),
        "w_pq": nrm(ks[10], (DEPTH, D, PEER_HEADS * PEER_QDIM), D ** -0.5),
        "peer_keys": nrm(ks[11], (DEPTH, PEER_HEADS, 2, PEER_NKEYS, PEER_HALF), PEER_HALF ** -0.5),
        "peer_u": nrm(ks[12], (DEPTH, PEER_EXPERTS, D), D ** -0.5),
        "peer_v": nrm(ks[13], (DEPTH, PEER_EXPERTS, D), PEER_HEADS ** -0.5),
        "g_final": 1.0 + nrm(ks[14], (D,), 0.02),
    }

def first_block(x, c, w_ada, b_ada, g_mix, w_in, w_sb_o, w_dil_o, w_out, g_ffn, w_pq,
              peer_keys, peer_u, peer_v, g_final):
    B, S, D = x.shape
    pos = jnp.arange(S)
    splits = np.cumsum([SB_WIDTH] * 3 + [DIL_WIDTH] * 3 + [D_MODEL]).tolist()
    for layer in range(DEPTH):
        mod = jax.nn.silu(c) @ w_ada[layer] + b_ada[layer]
        sh1, sc1, gt1, sh2, sc2, gt2 = jnp.split(mod, N_MOD, axis=-1)

        h = modulate(rms_norm(x, g_mix[layer]), sh1, sc1)
        proj = h @ w_in[layer]
        q_sb, k_sb, v_sb, q_d, k_d, v_d, gate_sb, gate_d = jnp.split(proj, splits, axis=-1)

        hs = (B, S, SB_HEADS, HEAD_DIM)
        o_sb = stick_breaking_attention(q_sb.reshape(hs), k_sb.reshape(hs), v_sb.reshape(hs))

        hd = (B, S, DIL_HEADS, HEAD_DIM)
        gd = (B, S, N_DIL_GROUPS, DIL_HEADS_PER_GROUP, HEAD_DIM)
        q_dr = rope(q_d.reshape(hd), pos).reshape(gd)
        k_dr = rope(k_d.reshape(hd), pos).reshape(gd)
        o_d = dilated_attention(q_dr, k_dr, v_d.reshape(gd))

        br_sb = o_sb.reshape(B, S, SB_WIDTH) @ w_sb_o[layer]
        br_d = o_d.reshape(B, S, DIL_OUT_WIDTH) @ w_dil_o[layer]
        merged = jax.nn.sigmoid(gate_sb) * br_sb + jax.nn.sigmoid(gate_d) * br_d
        x = x + gt1[:, None, :] * (merged @ w_out[layer])

        h2 = modulate(rms_norm(x, g_ffn[layer]), sh2, sc2)
        x = x + gt2[:, None, :] * peer_ffn(h2, w_pq[layer], peer_keys[layer], peer_u[layer], peer_v[layer])
    return rms_norm(x, g_final)


PLE_DIM = 256
SGU_CHUNK = 128
SGU_GROUPS = 8
SGU_WIDTH = D_MODEL
SGU_GROUP_DIM = SGU_WIDTH // SGU_GROUPS
ATT_HEADS = 16
ATT_WIDTH = ATT_HEADS * HEAD_DIM
MOBA_BLOCK = 256
MOBA_TOPK = 3
Q_CHUNK = 64
REL_BUCKETS = 32
REL_MAX_DIST = 1024
D_FF = 4 * D_MODEL
SPLITS = (SGU_WIDTH, SGU_WIDTH, ATT_WIDTH, ATT_WIDTH, ATT_WIDTH, D_MODEL, D_MODEL)
IN_COLS_2 = sum(SPLITS)


def rms_norm_2(x, g):
    xf = x.astype(jnp.float32)
    y = xf * lax.rsqrt(jnp.mean(xf * xf, axis=-1, keepdims=True) + EPS)
    return (y * g.astype(jnp.float32)).astype(x.dtype)

def layer_norm(x, g, b):
    xf = x.astype(jnp.float32)
    mu = jnp.mean(xf, axis=-1, keepdims=True)
    xc = xf - mu
    y = xc * lax.rsqrt(jnp.mean(xc * xc, axis=-1, keepdims=True) + EPS)
    return (y * g.astype(jnp.float32) + b.astype(jnp.float32)).astype(x.dtype)

def rel_bucket(dist):
    n = jnp.maximum(dist, 0)
    max_exact = REL_BUCKETS // 2
    nf = jnp.maximum(n, max_exact).astype(jnp.float32)
    large = max_exact + (jnp.log(nf / max_exact) / math.log(REL_MAX_DIST / max_exact)
                         * (REL_BUCKETS - max_exact)).astype(jnp.int32)
    large = jnp.minimum(large, REL_BUCKETS - 1)
    return jnp.where(n < max_exact, n, large)

def sgu_mixer(u, v, w_s, b_s, ln_g, ln_b):
    B, S, _ = u.shape
    nc = S // SGU_CHUNK
    v = layer_norm(v, ln_g, ln_b)
    vg = v.reshape(B, nc, SGU_CHUNK, SGU_GROUPS, SGU_GROUP_DIM)
    causal = jnp.tril(jnp.ones((SGU_CHUNK, SGU_CHUNK), dtype=bool))
    w = jnp.where(causal, w_s, 0).astype(v.dtype)
    mixed = jnp.einsum('gts,bnsgc->bntgc', w, vg) + b_s.T[None, None, :, :, None].astype(v.dtype)
    return u * mixed.reshape(B, S, SGU_WIDTH)

_gather_blocks = jax.vmap(jax.vmap(lambda blocks, idx: blocks[idx]))

def moba_attention(q, k, v, rel_bias):
    B, H, S, dh = q.shape
    nb = S // MOBA_BLOCK
    topk = min(MOBA_TOPK, nb)
    kb = k.reshape(B, H, nb, MOBA_BLOCK, dh)
    vb = v.reshape(B, H, nb, MOBA_BLOCK, dh)
    k_mean = jnp.mean(kb.astype(jnp.float32), axis=3).astype(k.dtype)
    scale = dh ** -0.5
    table = rel_bias.T
    h_idx = jnp.arange(H)[None, :, None, None, None]
    pos_in_block = jnp.arange(MOBA_BLOCK)
    n_chunks = S // Q_CHUNK
    q_chunks = q.reshape(B, H, n_chunks, Q_CHUNK, dh).transpose(2, 0, 1, 3, 4)
    n_sel = topk * MOBA_BLOCK

    def one_chunk(args):
        c, q_c = args
        q_pos = c * Q_CHUNK + jnp.arange(Q_CHUNK)
        own = (c * Q_CHUNK) // MOBA_BLOCK
        gate = jnp.einsum('bhqd,bhnd->bhqn', q_c, k_mean).astype(jnp.float32)
        gate = jnp.where(jnp.arange(nb) < own, gate, -jnp.inf)
        _, sel = lax.top_k(gate, topk)
        sel_valid = sel < own
        k_sel = _gather_blocks(kb, sel)
        v_sel = _gather_blocks(vb, sel)
        s_sel = jnp.einsum('bhqd,bhqkmd->bhqkm', q_c, k_sel).astype(jnp.float32) * scale
        k_pos_sel = sel[..., None] * MOBA_BLOCK + pos_in_block
        dist_sel = q_pos[:, None, None] - k_pos_sel
        s_sel = s_sel + table[h_idx, rel_bucket(dist_sel)].astype(jnp.float32)
        s_sel = jnp.where(sel_valid[..., None], s_sel, -jnp.inf)
        k_own = lax.dynamic_index_in_dim(kb, own, axis=2, keepdims=False)
        v_own = lax.dynamic_index_in_dim(vb, own, axis=2, keepdims=False)
        s_own = jnp.einsum('bhqd,bhmd->bhqm', q_c, k_own).astype(jnp.float32) * scale
        dist_own = q_pos[:, None] - (own * MOBA_BLOCK + pos_in_block)[None, :]
        s_own = s_own + table[:, rel_bucket(dist_own)].astype(jnp.float32)
        s_own = jnp.where(dist_own >= 0, s_own, -jnp.inf)
        s_all = jnp.concatenate([s_sel.reshape(B, H, Q_CHUNK, n_sel), s_own], axis=-1)
        probs = jax.nn.softmax(s_all, axis=-1).astype(v.dtype)
        p_sel = probs[..., :n_sel].reshape(B, H, Q_CHUNK, topk, MOBA_BLOCK)
        p_own = probs[..., n_sel:]
        return (jnp.einsum('bhqkm,bhqkmd->bhqd', p_sel, v_sel)
                + jnp.einsum('bhqm,bhmd->bhqd', p_own, v_own))

    out = lax.map(one_chunk, (jnp.arange(n_chunks), q_chunks))
    return out.transpose(1, 2, 0, 3, 4).reshape(B, H, S, dh)

def second_inputs(seed: int = 0) -> dict:
    key = jax.random.key(seed)
    ks = jax.random.split(key, 20)
    f32 = jnp.float32
    nrm = lambda k, shape, s: jax.random.normal(k, shape, f32) * s
    L = DEPTH
    return {
        "x": nrm(ks[0], (BATCH, SEQ, D_MODEL), 1.0),
        "p": nrm(ks[1], (DEPTH, BATCH, SEQ, PLE_DIM), 1.0),
        "norm_mix_g": 1.0 + nrm(ks[2], (L, D_MODEL), 0.05),
        "w_in": nrm(ks[3], (L, D_MODEL, IN_COLS_2), D_MODEL ** -0.5),
        "w_sgu_spatial": nrm(ks[4], (L, SGU_GROUPS, SGU_CHUNK, SGU_CHUNK), SGU_CHUNK ** -0.5),
        "b_sgu_spatial": 1.0 + nrm(ks[5], (L, SGU_GROUPS, SGU_CHUNK), 0.1),
        "ln_v_g": 1.0 + nrm(ks[6], (L, SGU_WIDTH), 0.05),
        "ln_v_b": nrm(ks[7], (L, SGU_WIDTH), 0.02),
        "rel_bias": nrm(ks[8], (REL_BUCKETS, ATT_HEADS), 0.5),
        "w_out": nrm(ks[9], (L, D_MODEL, D_MODEL), D_MODEL ** -0.5),
        "norm_ffn_g": 1.0 + nrm(ks[10], (L, D_MODEL), 0.05),
        "w_ff1": nrm(ks[11], (L, D_MODEL, D_FF), D_MODEL ** -0.5),
        "w_ff2": nrm(ks[12], (L, D_FF, D_MODEL), D_FF ** -0.5),
        "norm_ple_g": 1.0 + nrm(ks[13], (L, D_MODEL), 0.05),
        "w_ple_gate": nrm(ks[14], (L, D_MODEL, D_MODEL), D_MODEL ** -0.5),
        "w_ple_proj": nrm(ks[15], (L, PLE_DIM, D_MODEL), PLE_DIM ** -0.5),
        "norm_final_g": 1.0 + nrm(ks[16], (D_MODEL,), 0.05),
    }

def second_block(x, p, norm_mix_g, w_in, w_sgu_spatial, b_sgu_spatial, ln_v_g, ln_v_b, rel_bias,
              w_out, norm_ffn_g, w_ff1, w_ff2, norm_ple_g, w_ple_gate, w_ple_proj, norm_final_g):
    B, S, _ = x.shape
    offsets = np.cumsum(SPLITS)[:-1].tolist()
    for i in range(DEPTH):
        h = rms_norm_2(x, norm_mix_g[i])
        proj = h @ w_in[i]
        za_u, za_v, q, k, v_att, g_a, g_b = jnp.split(proj, offsets, axis=-1)
        y_a = sgu_mixer(jax.nn.gelu(za_u), jax.nn.gelu(za_v), w_sgu_spatial[i], b_sgu_spatial[i],
                        ln_v_g[i], ln_v_b[i])
        heads = lambda t: t.reshape(B, S, ATT_HEADS, HEAD_DIM).transpose(0, 2, 1, 3)
        y_b = moba_attention(heads(q), heads(k), heads(v_att), rel_bias)
        y_b = y_b.transpose(0, 2, 1, 3).reshape(B, S, ATT_WIDTH)
        merged = jax.nn.sigmoid(g_a) * y_a + jax.nn.sigmoid(g_b) * y_b
        x = x + merged @ w_out[i]
        h = rms_norm_2(x, norm_ffn_g[i])
        x = x + jnp.square(jax.nn.relu(h @ w_ff1[i])) @ w_ff2[i]
        gate = jax.nn.sigmoid(rms_norm_2(x, norm_ple_g[i]) @ w_ple_gate[i])
        x = x + gate * (p[i] @ w_ple_proj[i])
    return rms_norm_2(x, norm_final_g)


def setup_inputs(seed=0):
    out = dict(first_inputs(seed))
    for name, value in second_inputs(seed + 1).items():
        if name != "x":
            out[name + "_2"] = value
    return out


def reference(
    x, c, w_ada, b_ada, g_mix, w_in, w_sb_o, w_dil_o, w_out, g_ffn, w_pq, peer_keys, peer_u,
    peer_v, g_final, p_2, norm_mix_g_2, w_in_2, w_sgu_spatial_2, b_sgu_spatial_2, ln_v_g_2,
    ln_v_b_2, rel_bias_2, w_out_2, norm_ffn_g_2, w_ff1_2, w_ff2_2, norm_ple_g_2, w_ple_gate_2,
    w_ple_proj_2, norm_final_g_2,
):
    x = first_block(
        x, c, w_ada, b_ada, g_mix, w_in, w_sb_o, w_dil_o, w_out, g_ffn, w_pq, peer_keys, peer_u,
        peer_v, g_final,
    )
    return second_block(
        x, p_2, norm_mix_g_2, w_in_2, w_sgu_spatial_2, b_sgu_spatial_2, ln_v_g_2, ln_v_b_2,
        rel_bias_2, w_out_2, norm_ffn_g_2, w_ff1_2, w_ff2_2, norm_ple_g_2, w_ple_gate_2,
        w_ple_proj_2, norm_final_g_2,
    )


_drawn_inputs = setup_inputs


def setup_inputs(seed=0):
    import zlib

    import numpy as np

    out = dict(_drawn_inputs(seed))
    spreads = {}
    factors = {'b_ada': 5.446,
     'g_mix': 8.0,
     'g_ffn': 6.124,
     'ln_v_g_2': 4.943,
     'ln_v_b_2': 8.0,
     'norm_ple_g_2': 26.278}
    for name, (base, spread) in spreads.items():
        noise = np.random.default_rng([zlib.crc32(name.encode()), seed]).standard_normal(out[name].shape)
        drawn = base * np.exp(spread * noise) if base else spread * noise
        out[name] = __import__('jax').numpy.asarray(drawn.astype(out[name].dtype))
    for name, factor in factors.items():
        out[name] = (out[name] * factor).astype(out[name].dtype)
    return out
```

```python
from contextlib import ExitStack

import numpy as np

import concourse.bass as bass
from concourse import mybir

F32 = mybir.dt.float32
U32 = mybir.dt.uint32
ALU = mybir.AluOpType
ACT = mybir.ActivationFunctionType
AX = mybir.AxisListType

P = 128
T, D = 256, 1024
TT, KC = T // P, D // P
HD = 64
SBW, DILW = 512, 768
SB_PAIRS = SBW // P
DIL_G, DIL_HP = 3, 2
DIL_RATE = (1, 4, 16)
DIL_WIN = (128, 512, 2048)
NH, NK, TOPK = 8, 128, 16
NU = TT * NH
DFF = 4096
AH = 16
NBUCK = 32
PLE = 256
EPS = 1e-6
SCALE = HD ** -0.5
GELU_A, GELU_C = 0.044715, float(np.sqrt(2.0 / np.pi))
NEG = -1e30
LOWEST = -3.0e38
RMAX = 512

RING = 12
TILES = {
    "stick": (12, 1, list(range(12)), [1] * 12),
    "dilated": (9, 2, list(range(9)), [1] * 9),
    "gates": (12, 2, [4 * j + b for j in range(4) for b in (0, 1, 3)], [1, 1, 2] * 4),
    "out1": (8, 1, list(range(8)), [1] * 8),
    "query": (8, 2, list(range(8)), [1] * 8),
    "sgu_v": (8, 1, list(range(8)), [1] * 8),
    "mix": (12, 4, list(range(12)), [1] * 12),
    "out2": (8, 1, list(range(8)), [1] * 8),
    "ff1": (8, 4, list(range(8)), [1] * 8),
    "ff2": (8, 4, [0] * 4 + [1] * 4, [1] * 8),
    "ple": (8, 2, list(range(8)), [1] * 8),
}
USES = {
    "init": (1, {"T0": 3, "T1": 2, "S1": 4}),
    "norm1": (1, {"SA": 1}),
    "stick": (1, {"M0": 6, "M1": 6, "SA": 4, "S0": 4, "S1": 8, "T0": 4, "T1": 4, "OT": 4}),
    "extra": (1, {"T0": 4, "T1": 3, "SA": 1}),
    "dilated": (2, {"M0": 5, "M1": 4, "T0": 7, "T1": 5, "SA": 2, "S0": 2, "OT": 1}),
    "gates": (2, {"M0": 8, "M1": 8}),
    "out1": (1, {"M0": 4, "M1": 4}),
    "norm2": (1, {"SA": 1}),
    "query": (2, {"M0": 4, "M1": 4}),
    "rows": (1, {"T0": 2, "T1": 2}),
    "sub": (1, {"SA": 4, "S0": 4}),
    "experts": (8, {"S0": 1, "T0": 1}),
    "back": (1, {"T0": 2, "T1": 2}),
    "norm3": (1, {"SA": 1}),
    "norm4": (1, {"SA": 1}),
    "sgu_v": (1, {"M0": 4, "M1": 4}),
    "mix": (4, {"M0": 6, "M1": 6, "SA": 2, "S0": 2, "S1": 2, "T0": 2, "T1": 2, "OT": 2}),
    "out2": (1, {"M0": 4, "M1": 4}),
    "norm5": (1, {"SA": 1}),
    "ff1": (4, {"M0": 4, "M1": 4}),
    "ff2": (4, {"M0": 1, "M1": 1}),
    "norm6": (1, {"SA": 1}),
    "ple": (2, {"M0": 4, "M1": 4}),
    "norm7": (1, {"SA": 1}),
    "final": (1, {"T0": 2, "T1": 2}),
}
BANKS = ("M0", "M1", "SA", "S0", "S1", "T0", "T1", "OT")


def prior(bank, stage, k, i=0):
    n = 0
    for name, (bodies, per) in USES.items():
        if name == stage:
            return i * per[bank] + (n + k)
        n += bodies * per.get(bank, 0)
    raise KeyError(stage)


def tile_loads(slot, stage):
    n = 0
    for name, (tiles, bodies, _, dmas) in TILES.items():
        if name == stage:
            return n
        if slot < tiles:
            n += bodies * dmas[slot]
    raise KeyError(stage)


def tile_ready(stage, t, i=0):
    dmas = TILES[stage][3][t]
    return i * (16 * dmas) + 16 * (tile_loads(t, stage) + dmas)


def last_user(slot, stage):
    found = None
    for name, (tiles, bodies, free_after, _) in TILES.items():
        if name == stage:
            return found
        if slot < tiles:
            k = free_after[slot]
            found = (f"M{k % 2}", prior(f"M{k % 2}", name, k // 2, bodies - 1) + 1)
    raise KeyError(stage)


class Steps:

    def __init__(self, sem):
        self.sem, self.n, self.reg, self.per, self.at = sem, 0, None, 0, 0

    def tick(self):
        self.n += 1
        return self.sem

    def now(self):
        return self.n if self.reg is None else self.reg * self.per + self.n

    def enter(self, reg, per):
        self.reg, self.per, self.at = reg, per, self.n

    def leave(self, bodies):
        assert self.n - self.at == self.per, (self.n - self.at, self.per)
        self.n, self.reg = self.at + bodies * self.per, None


def build(nc, A, K, rel_rows, out):
    with ExitStack() as ctx:
        def sb(name, shape, dt=F32):
            return ctx.enter_context(nc.sbuf_tensor(name, shape, dt))

        def sem(name):
            return ctx.enter_context(nc.semaphore(name))

        ident = sb("ident", [P, P])
        ones = sb("ones", [P, P])
        eps = sb("eps", [P, 1])
        xT = sb("xT", [P, KC, T])
        hT = sb("hT", [P, KC, T])
        tmp = sb("tmp", [P, KC, T])
        merged = sb("merged", [P, KC, T])
        rt = sb("rt", [P, T])
        rstd = sb("rstd", [P, T])
        ring = sb("ring", [P, RING, KC, P])
        NVEC = 8 * KC
        vec_rows = sb("vec_rows", [NVEC + 6 * KC, P])
        vecT = sb("vecT", [P, NVEC + 6 * KC])
        names = ("c", "g_mix", "g_ffn", "g_final", "norm_mix_g_2", "norm_ffn_g_2", "norm_ple_g_2",
                 "norm_final_g_2")
        col = {n: vecT[:, KC * i:KC * (i + 1)] for i, n in enumerate(names)}
        b_ada_col = vecT[:, NVEC:NVEC + 6 * KC]
        silu_c = sb("silu_c", [P, 2, KC])
        modT = sb("modT", [P, 6 * KC])
        mod = [modT[:, KC * i:KC * (i + 1)] for i in range(6)]
        gain = sb("gain", [P, 2, KC])
        keysT = sb("keysT", [P, 2 * NH, NK])
        sguT = sb("sguT", [P, KC, P])
        pT = sb("pT", [P, 2, T])
        iota = sb("iota", [P, TOPK])[:, :]
        arena = sb("arena", [P, 27300])
        carved = [0]

        def carve(*shape, dt=F32, parts=P):
            n = int(np.prod(shape))
            ap = arena[0:parts, carved[0]:carved[0] + n]
            carved[0] += n
            assert carved[0] <= 27300, carved[0]
            if dt is not F32:
                ap = ap.bitcast(dt)
            if len(shape) == 2:
                ap = ap.rearrange("p (a b) -> p a b", b=shape[1])
            elif len(shape) == 3:
                ap = ap.rearrange("p (a b c) -> p a b c", b=shape[1], c=shape[2])
            return ap

        ada = carve(2, KC, 512)
        ada_sum = carve(2, 512)
        tri = carve(P)
        rot = carve(P)
        cosT, sinT = carve(T), carve(T)
        stick_neg = carve(384)
        dil_neg = carve(DIL_G * 384)
        osb = carve(SB_PAIRS, T)
        odl = carve(DIL_HP, T)
        qs, ks, vs = carve(T), carve(T), carve(TT, P)
        zm, ez, sp = carve(2, 384), carve(2, 384), carve(2, 384)
        gate_a, gate_b, br_a, br_b = carve(T), carve(T), carve(T), carve(T)
        mark = carved[0]
        x_rows = carve(TT, D)
        key_rows = carve(2 * NH, P)
        sgu_rows = carve(KC, P)
        sgu_mask = carve(P)
        p_rows = carve(TT, PLE)
        rel_tab = carve(AH, parts=NBUCK)
        rel_hot = carve(RMAX, parts=NBUCK)
        rel_neg = carve(RMAX, parts=AH)
        rel_row = tmp[0:AH, 0:2, :].rearrange("p a t -> p (a t)")
        carved[0] = mark
        raw = carve(DIL_G, 2, T)
        roped = carve(DIL_G, 2, T)
        rope_a, rope_b = carve(2, T), carve(2, T)
        vd = carve(DIL_G, TT, P)
        sd = carve(2, DIL_G * 384)
        pt = carve(2, DIL_G, 384)
        sm_max, sm_sum, sm_inv = carve(2, 2), carve(2, 2), carve(2, 2)
        carved[0] = 0
        sub = carve(TT * 2 * NH * NK)
        h_rows = carve(TT * D)
        y_rows = carve(TT * D)
        v_ring = carve(8, D)
        mark = carved[0]
        qT = carve(2 * NH, T)
        carved[0] = mark
        u_ring = carve(8, D)
        dg = carve(8, P)
        dot_junk = [tmp[:, c:c + 4, :].rearrange("p a t -> p (a t)") for c in (0, 4)]
        s16 = carve(2, TOPK)
        i16 = carve(2, TOPK, dt=U32)
        i16f = carve(2, TOPK)
        sub_w = carve(2, NK)
        cand, cand_w = carve(TOPK, TOPK), carve(TOPK * TOPK)
        best = carve(TOPK)
        pos = carve(TOPK, dt=U32)
        pos_ab = carve(2, TOPK, dt=U32)
        pos_f = carve(2, TOPK)
        hot = merged[:, 0:2, :].rearrange("p a t -> p (a t)").rearrange("p (k a) -> p k a", a=TOPK)
        pick = carve(2, TOPK)
        expert_f = carve(TOPK)
        expert = carve(2, TOPK, dt=U32)
        gate_w, gate_n = carve(2, TOPK), carve(2, 1)
        gate_s, gate_r = carve(2, 1), carve(2, 1)
        act_x, act_a, act_b, act_t = carve(2, TOPK), carve(2, TOPK), carve(2, TOPK), carve(2, TOPK)
        wgt = carve(2, TOPK)
        carved[0] = 0
        rel = carve(AH * T)
        bs_rows = carve(KC * P)
        ln_g, ln_b = carve(D), carve(D)
        zv = carve(TT, D)
        zsq = carve(D)
        ln_s, ln_m, ln_q, ln_r, ln_i = carve(2, 1), carve(2, 1), carve(2, 1), carve(2, 1), carve(2, 1)
        g_raw, g_sq, g_th, u_act = carve(T), carve(T), carve(T), carve(T)
        vst = carve(TT, P)
        q2, k2, v2 = carve(T), carve(T), carve(TT, P)
        s2, p2 = carve(2, 384), carve(2, 384)
        ga, gb, ya = carve(T), carve(T), carve(T)
        mx2, sm2, iv2 = carve(2, 2), carve(2, 2), carve(2, 2)
        mark = carved[0]
        carved[0] = 0
        ffT = carve(DFF // P, T)
        relu = carve(2, T)
        gate_p, prod_p = carve(2, T), carve(2, T)
        o_rows = carve(TT, D)

        ps = {b: None for b in BANKS}
        for b in ("M0", "M1", "SA"):
            ps[b] = ctx.enter_context(nc.psum_tensor(f"ps_{b}", [P, 512], F32))[:, :]
        wide = ctx.enter_context(nc.psum_tensor("ps_S", [P, 1024], F32))
        ps["S0"], ps["S1"] = wide[:, 0:512], wide[:, 512:1024]
        twin = ctx.enter_context(nc.psum_tensor("ps_T", [P, 1024], F32))
        ps["T0"], ps["T1"] = twin[:, 0:512], twin[:, 512:1024]
        ps["OT"] = ctx.enter_context(nc.psum_tensor("ps_OT", [P, 512], F32))[:, :]

        done = {b: sem(f"done_{b}") for b in BANKS}
        free = {b: sem(f"free_{b}") for b in BANKS}
        tile_in = [sem(f"tile_in{s}") for s in range(RING)]
        vec_in, ident_in, x_in, key_in, sgu_in, p_in, rel_in, const_in = (
            sem(n) for n in ("vec_in", "ident_in", "x_in", "key_in", "sgu_in", "p_in", "rel_in", "const_in"))
        ada_in = [sem(f"ada_in{s}") for s in range(2)]
        ada_used, ada_ready, mod_ready = sem("ada_used"), sem("ada_ready"), sem("mod_ready")
        setup_done, silu_half = sem("setup_done"), sem("silu_half")
        rel_out, rel_back, layer2_in = sem("rel_out"), sem("rel_back"), sem("layer2_in")
        x_ready = sem("x_ready")
        sq_ready, root_ready, scaled, h_ready = sem("sq_ready"), sem("root_ready"), sem("scaled"), sem("h_ready")
        stick_sp, stick_ln, stick_p = sem("stick_sp"), sem("stick_ln"), sem("stick_p")
        qkv_ready = sem("qkv_ready")
        roped_ready = sem("roped_ready")
        soft_max, soft_exp, soft_p, pt_ready = sem("soft_max"), sem("soft_exp"), sem("soft_p"), sem("pt_ready")
        gate_ready, merged_ready = sem("gate_ready"), sem("merged_ready")
        q_ready, rows_ready, sub_ready = sem("q_ready"), sem("rows_ready"), sem("sub_ready")
        idx_ready, best_ready, gate_exp = sem("idx_ready"), sem("best_ready"), sem("gate_exp")
        u_in = [sem(f"u_in{s}") for s in range(8)]
        v_in = [sem(f"v_in{s}") for s in range(8)]
        u_used, v_used, issued = sem("u_used"), sem("v_used"), sem("issued")
        act_arg, act_tanh, wgt_ready, diag_ready = sem("act_arg"), sem("act_tanh"), sem("wgt_ready"), sem("diag_ready")
        y_ready = sem("y_ready")
        zv_raw, zv_arg, zv_tanh, zv_ready = sem("zv_raw"), sem("zv_arg"), sem("zv_tanh"), sem("zv_ready")
        ln_c, ln_sq, ln_root, vn_ready, vst_ready = (
            sem("ln_c"), sem("ln_sq"), sem("ln_root"), sem("vn_ready"), sem("vst_ready"))
        u_raw, u_arg, u_tanh = sem("u_raw"), sem("u_arg"), sem("u_tanh")
        relu_ready, ff_ready = sem("relu_ready"), sem("ff_ready")
        out_done = sem("out_done")
        dve_step, act_step = sem("dve_step"), sem("act_step")
        slots_freed, route_step = sem("slots_freed"), sem("route_step")

        block = ctx.enter_context(nc.Block())

        w_in, w_in2 = A["w_in"][0], A["w_in_2"][0]

        def rows8(w):
            return w.rearrange("(c p) n -> p c n", p=P)

        w_in_v, w_in2_v = rows8(w_in), rows8(w_in2)
        w_ada_v = rows8(A["w_ada"][0])
        w_sbo_v, w_dlo_v = rows8(A["w_sb_o"][0]), rows8(A["w_dil_o"][0])
        w_out_v, w_pq_v, w_out2_v = rows8(A["w_out"][0]), rows8(A["w_pq"][0]), rows8(A["w_out_2"][0])
        w_ff1_v = rows8(A["w_ff1_2"][0])
        w_ff2_v = A["w_ff2_2"][0].rearrange("(q c p) n -> q p c n", p=P, c=KC)
        w_plg_v, w_plp_v = rows8(A["w_ple_gate_2"][0]), rows8(A["w_ple_proj_2"][0])

        @block.sync
        def _(eng):
            for i, n in enumerate(names):
                src = A[n] if len(A[n].shape) == 1 else A[n][0]
                eng.dma_start(vec_rows[KC * i:KC * (i + 1), :],
                              src.rearrange("(c p) -> c p", p=P)).then_inc(vec_in, 16)
            eng.dma_start(vec_rows[NVEC:NVEC + 6 * KC, :],
                          A["b_ada"][0].rearrange("(c p) -> c p", p=P)).then_inc(vec_in, 16)
            eng.dma_start(ident[:, :], K["ident"]).then_inc(ident_in, 16)
            eng.dma_start(x_rows, A["x"][0].rearrange("(t p) d -> p t d", p=P)).then_inc(x_in, 16)

            def tile(stage, t, i, *parts):
                if isinstance(i, int) and i == 0:
                    user = last_user(t, stage)
                    if user is not None:
                        eng.wait_ge(done[user[0]], user[1])
                else:
                    k = TILES[stage][2][t]
                    b = f"M{k % 2}"
                    eng.wait_ge(done[b], prior(b, stage, k // 2, i - 1) + 1)
                    eng.sem_inc(slots_freed, 1)
                for lo, hi, src in parts:
                    eng.dma_start(ring[:, t, lo:hi, :], src).then_inc(tile_in[t], 16)

            def cols(view, start):
                return (0, KC, view[:, :, bass.ds(start, P)])

            def stick_tiles(i):
                for j in range(SB_PAIRS):
                    for s in range(3):
                        tile("stick", 3 * j + s, i, cols(w_in_v, s * SBW + j * P))

            def dilated_tiles(i):
                for g in range(DIL_G):
                    for s in range(3):
                        tile("dilated", 3 * g + s, i, cols(w_in_v, i * P + (3 * SBW + s * DILW + g * 256)))

            def gate_tiles(i):
                for j in range(4):
                    n = i * (4 * P) + j * P
                    g0 = 3 * SBW + 3 * DILW
                    tile("gates", 3 * j, i, cols(w_in_v, n + g0))
                    tile("gates", 3 * j + 1, i, cols(w_in_v, n + (g0 + D)))
                    tile("gates", 3 * j + 2, i, (0, 4, w_sbo_v[:, :, bass.ds(n, P)]),
                         (4, 6, w_dlo_v[:, :, bass.ds(n, P)]))

            def plain_tiles(stage, view, base=0):
                def body(i):
                    for t in range(8):
                        tile(stage, t, i, cols(view, i * (8 * P) + (base + t * P)))
                return body

            def mix_tiles(i):
                for j in range(2):
                    for t, base in enumerate((2 * D, 3 * D, 4 * D, 0, 5 * D, 6 * D)):
                        tile("mix", 6 * j + t, i, cols(w_in2_v, i * (2 * P) + (base + j * P)))

            def ff2_tiles(i):
                for j in range(2):
                    for q in range(4):
                        tile("ff2", 4 * j + q, i, (0, KC, w_ff2_v[q][:, :, bass.ds(i * (2 * P) + j * P, P)]))

            def ple_tiles(i):
                for j in range(4):
                    n = i * (4 * P) + j * P
                    tile("ple", 2 * j, i, cols(w_plg_v, n))
                    tile("ple", 2 * j + 1, i, (0, 2, w_plp_v[:, :, bass.ds(n, P)]))

            def stream(stage, body):
                body(0)
                bodies = TILES[stage][1]
                if bodies > 1:
                    with eng.Fori(1, bodies) as i:
                        body(i)

            stream("stick", stick_tiles)
            for dst, n in ((tri, "tri"), (rot, "rot"), (cosT, "cos"), (sinT, "sin"),
                           (stick_neg, "stick_neg"), (dil_neg, "dil_neg"), (iota[:, :], "iota")):
                eng.dma_start(dst, K[n]).then_inc(const_in, 16)
            eng.dma_start(key_rows, A["peer_keys"][0].rearrange("h s n c -> n (h s) c")).then_inc(key_in, 16)
            eng.dma_start(sgu_rows, A["w_sgu_spatial_2"][0].rearrange("g t s -> t g s")).then_inc(sgu_in, 16)
            eng.dma_start(sgu_mask, K["sgu_mask"]).then_inc(sgu_in, 16)
            eng.dma_start(p_rows, A["p_2"][0, 0].rearrange("(t p) d -> p t d", p=P)).then_inc(p_in, 16)
            eng.dma_start(rel_tab, A["rel_bias_2"]).then_inc(rel_in, 16)
            eng.dma_start(rel_hot, K["rel_hot"]).then_inc(rel_in, 16)
            eng.dma_start(rel_neg, K["rel_neg"]).then_inc(rel_in, 16)
            eng.wait_ge(rel_out, 1)
            eng.dma_start(rel_rows, rel_row.unsqueeze(1).broadcast_to([AH, P, RMAX])).then_inc(rel_back, 16)
            stream("dilated", dilated_tiles)
            stream("gates", gate_tiles)
            stream("out1", plain_tiles("out1", w_out_v))
            stream("query", plain_tiles("query", w_pq_v))
            stream("sgu_v", plain_tiles("sgu_v", w_in2_v, D))
            eng.wait_ge(x_ready, 3)
            eng.wait_ge(rel_back, 16)
            eng.dma_start(rel.rearrange("p (h k) -> p h k", k=T),
                          bass.AP(rel_rows.tensor, P - 1, [[RMAX - 1, P], [P * RMAX, AH], [1, T]])).then_inc(layer2_in, 16)
            eng.dma_start(bs_rows, A["b_sgu_spatial_2"][0].rearrange("g t -> (g t)").partition_broadcast(P))\
                .then_inc(layer2_in, 16)
            eng.dma_start(ln_g, A["ln_v_g_2"][0].partition_broadcast(P)).then_inc(layer2_in, 16)
            eng.dma_start(ln_b, A["ln_v_b_2"][0].partition_broadcast(P)).then_inc(layer2_in, 16)
            stream("mix", mix_tiles)
            stream("out2", plain_tiles("out2", w_out2_v))
            stream("ff1", plain_tiles("ff1", w_ff1_v))
            stream("ff2", ff2_tiles)
            stream("ple", ple_tiles)
            for t in range(TT):
                for b in ("T0", "T1"):
                    eng.wait_ge(free[b], prior(b, "final", t) + 1)
                eng.dma_start(out[0, t * P:(t + 1) * P, :], o_rows[:, t, :]).then_inc(out_done, 16)
            eng.wait_ge(out_done, 16 * TT)

        @block.gpsimd
        def _(pool):
            nc.gpsimd.memset(ones[:, :], 1.0).then_inc(setup_done, 1)
            nc.gpsimd.memset(eps[:, :], EPS).then_inc(setup_done, 1)
            for ch in range(12):
                if ch >= 2:
                    pool.wait_ge(ada_used, ch - 1)
                pool.dma_start(ada[:, ch % 2], w_ada_v[:, :, ch * 512:(ch + 1) * 512]).then_inc(ada_in[ch % 2], 16)

            def gather(ring_buf, table, sems, used, s, u):
                for k in range(TOPK):
                    pool.wait_ge(used, u * TOPK + (k + 1))
                    pool.sem_inc(issued, 1)
                    pool.indirect_dma_start(ring_buf[:, k % 8, :], None, table,
                                            bass.IndirectOffsetOnAxis(ap=expert[:, s, k:k + 1], axis=0))\
                        .then_inc(sems[k % 8], 16)

            with pool.Fori(0, NU // 2) as i:
                for s in range(2):
                    u = i * 2 + s
                    pool.wait_ge(idx_ready, u + 1)
                    gather(u_ring, A["peer_u"][0], u_in, u_used, s, u)
                    gather(v_ring, A["peer_v"][0], v_in, v_used, s, u)

        @block.tensor
        def _(pe):
            mm = nc.tensor.matmul

            def claim(bank, stage, k, i=0):
                n = prior(bank, stage, k, i)
                if not isinstance(n, int) or n > 0:
                    pe.wait_ge(free[bank], n)

            def norm(n):
                pe.wait_ge(sq_ready, n)
                claim("SA", f"norm{n}", 0)
                for c in range(KC):
                    m = mm(ps["SA"][:, 0:T], ones[:, :], tmp[:, c, :], start=c == 0, stop=c == KC - 1)
                m.then_inc(done["SA"], 1)

            def block_t(stage, t, k, i, src=None, chunks=(0, KC)):
                bank = f"M{k % 2}"
                claim(bank, stage, k // 2, i)
                pe.wait_ge(tile_in[t], tile_ready(stage, t, i))
                lo, hi = chunks
                for c in range(lo, hi):
                    rhs = hT[:, c, :] if src is None else src(c)
                    m = mm(ps[bank][:, 0:T], ring[:, t, c, :], rhs, start=c == lo, stop=c == hi - 1)
                m.then_inc(done[bank], 1)

            def block_r(stage, t, k, i):
                bank = f"M{k % 2}"
                claim(bank, stage, k // 2, i)
                pe.wait_ge(tile_in[t], tile_ready(stage, t, i))
                for tt in range(TT):
                    for c in range(KC):
                        m = mm(ps[bank][:, tt * P:(tt + 1) * P], hT[:, c, tt * P:(tt + 1) * P], ring[:, t, c, :],
                               start=c == 0, stop=c == KC - 1)
                m.then_inc(done[bank], 1)

            def turn(stage, group, sources, width=P):
                bank = f"T{group % 2}"
                claim(bank, stage, group // 2)
                for n, src in enumerate(sources):
                    m = nc.tensor.transpose(ps[bank][:, n * P:n * P + width], src, ident[0:width, 0:width])
                m.then_inc(done[bank], 1)

            def ada_columns(stage, k):
                pe.wait_ge(ada_ready, k + 1 if stage == "init" else k + 5)
                claim("S1", stage, k)
                for b in range(4):
                    m = mm(ps["S1"][:, b:b + 1], ada_sum[:, k % 2, b * P:(b + 1) * P], ones[:, 0:1],
                           start=True, stop=True)
                m.then_inc(done["S1"], 1)

            pe.wait_ge(setup_done, 2)
            pe.wait_ge(ident_in, 16)
            pe.wait_ge(vec_in, 9 * 16)
            turn("init", 0, [vec_rows[:, :]], width=NVEC + 6 * KC)
            pe.wait_ge(x_in, 16)
            for g in range(4):
                turn("init", 1 + g, [x_rows[:, tt, c * P:(c + 1) * P] for c in (2 * g, 2 * g + 1) for tt in range(TT)])
            for k in range(4):
                ada_columns("init", k)
            norm(1)
            pe.wait_ge(h_ready, 1)
            pe.wait_ge(const_in, 7 * 16)
            for j in range(SB_PAIRS):
                block_t("stick", 3 * j, 3 * j, 0)
                block_t("stick", 3 * j + 1, 3 * j + 1, 0)
                pe.wait_ge(qkv_ready, 3 * j + 2)
                for h, bank in enumerate(("SA", "S0")):
                    r = slice(HD * h, HD * h + HD)
                    claim(bank, "stick", j)
                    mm(ps[bank][:, 0:T], ks[r, 0:P], qs[r, :], start=True, stop=True)
                    mm(ps[bank][:, T:384], ks[r, P:T], qs[r, P:T], start=True, stop=True).then_inc(done[bank], 1)
                block_r("stick", 3 * j + 2, 3 * j + 2, 0)
                if j > 0:
                    for k in (2 * j - 2, 2 * j - 1):
                        ada_columns("stick", k)
                for h in range(2):
                    bank = f"T{h}"
                    pe.wait_ge(stick_sp, 2 * j + h + 1)
                    claim(bank, "stick", j)
                    mm(ps[bank][:, 0:384], tri, sp[:, h, :], start=True, stop=False)
                    mm(ps[bank][:, P:T], ones[:, :], sp[:, h, T:384], start=False, stop=True).then_inc(done[bank], 1)
                pe.wait_ge(qkv_ready, 3 * j + 3)
                claim("OT", "stick", j)
                for h in range(2):
                    r = slice(HD * h, HD * h + HD)
                    pe.wait_ge(stick_p, 2 * j + h + 1)
                    mm(ps["OT"][r, 0:T], vs[:, 0, r], ez[:, h, 0:T], start=True, stop=False)
                    m = mm(ps["OT"][r, P:T], vs[:, 1, r], ez[:, h, T:384], start=False, stop=True)
                m.then_inc(done["OT"], 1)

            for k in (6, 7):
                ada_columns("stick", k)

            pe.wait_ge(key_in, 16)
            for g in range(4):
                turn("extra", g, [key_rows[:, 4 * g + n, :] for n in range(4)])
            pe.wait_ge(sgu_in, 32)
            for g in range(2):
                turn("extra", 4 + g, [sgu_rows[:, 4 * g + n, :] for n in range(4)])
            pe.wait_ge(p_in, 16)
            turn("extra", 6, [p_rows[:, tt, c * P:(c + 1) * P] for c in range(2) for tt in range(TT)])
            pe.wait_ge(rel_in, 48)
            claim("SA", "extra", 0)
            mm(ps["SA"][0:AH, 0:RMAX], rel_tab, rel_hot, start=True, stop=True).then_inc(done["SA"], 1)
            pe.wait_ge(free["S1"], prior("S1", "stick", 8))

            with pe.Fori(0, DIL_HP) as i:
                for g in range(DIL_G):
                    block_t("dilated", 3 * g, 3 * g, i)
                    block_t("dilated", 3 * g + 1, 3 * g + 1, i)
                    block_r("dilated", 3 * g + 2, 3 * g + 2, i)
                    for s in range(2):
                        bank = f"T{s}"
                        pe.wait_ge(qkv_ready, i * 9 + (12 + 3 * g + s + 1))
                        claim(bank, "dilated", g, i)
                        mm(ps[bank][:, 0:T], rot, raw[:, g, s, :], start=True, stop=True).then_inc(done[bank], 1)
                pe.wait_ge(roped_ready, i * 3 + 3)
                for h in range(2):
                    r = slice(HD * h, HD * h + HD)
                    claim("SA", "dilated", h, i)
                    for g in range(DIL_G):
                        m = mm(ps["SA"][:, g * P:(g + 1) * P], roped[r, g, 0, 0:P], roped[r, g, 1, 0:P],
                               start=True, stop=True)
                    m.then_inc(done["SA"], 1)
                    claim("S0", "dilated", h, i)
                    for g in range(DIL_G):
                        m = mm(wide[:, g * T:(g + 1) * T], roped[r, g, 0, P:T], roped[r, g, 1, :],
                               start=True, stop=True)
                    m.then_inc(done["S0"], 1)
                pe.wait_ge(qkv_ready, i * 9 + 21)
                claim("OT", "dilated", 0, i)
                for h in range(2):
                    r = slice(HD * h, HD * h + HD)
                    pe.wait_ge(soft_p, i * 4 + (2 * h + 2))
                    for g in range(DIL_G):
                        bank = f"T{g % 2}"
                        claim(bank, "dilated", 3 + 2 * h + g // 2 if g % 2 == 0 else 3 + h, i)
                        at = DIL_G * P + g * T
                        for n, lo in enumerate((g * P, at, at + P)):
                            m = nc.tensor.transpose(ps[bank][:, n * P:(n + 1) * P], sd[:, h, lo:lo + P], ident[:, :])
                        m.then_inc(done[bank], 1)
                    pe.wait_ge(pt_ready, i * 6 + (3 * h + 3))
                    for g in range(DIL_G):
                        mm(ps["OT"][r, 0:T], vd[:, g, 0, r], pt[:, h, g, 0:T], start=g == 0, stop=False)
                        m = mm(ps["OT"][r, P:T], vd[:, g, 1, r], pt[:, h, g, T:384], start=False, stop=g == 2)
                m.then_inc(done["OT"], 1)

            pe.wait_ge(free["OT"], prior("OT", "dilated", 1, DIL_HP - 1))
            with pe.Fori(0, 2) as i:
                for j in range(4):
                    block_t("gates", 3 * j, 4 * j, i)
                    block_t("gates", 3 * j + 1, 4 * j + 1, i)
                    block_t("gates", 3 * j + 2, 4 * j + 2, i, lambda c: osb[:, c, :], (0, 4))
                    block_t("gates", 3 * j + 2, 4 * j + 3, i, lambda c: odl[:, c - 4, :], (4, 6))
            pe.wait_ge(merged_ready, 8)
            for t in range(KC):
                block_t("out1", t, t, 0, lambda c: merged[:, c, :])

            norm(2)
            pe.wait_ge(h_ready, 2)
            with pe.Fori(0, 2) as i:
                for t in range(8):
                    block_t("query", t, t, i)
            for g in range(4):
                turn("rows", g, [hT[:, 4 * (g % 2) + n, (g // 2) * P:(g // 2 + 1) * P] for n in range(4)])
            pe.wait_ge(q_ready, 16)
            for g in range(8):
                bank = ("SA", "S0")[g % 2]
                tt, h4 = g // 4, g % 4
                claim(bank, "sub", g // 2)
                for n in range(4):
                    m = mm(ps[bank][:, n * P:(n + 1) * P], qT[:, 4 * h4 + n, tt * P:(tt + 1) * P],
                           keysT[:, 4 * h4 + n, :], start=True, stop=True)
                m.then_inc(done[bank], 1)

            pe.sem_inc(v_used, 8)
            with pe.Fori(0, NU // 2) as i:
                for s in range(2):
                    u = i * 2 + s
                    acc = wide if s == 0 else twin
                    bank = "S0" if s == 0 else "T0"
                    claim(bank, "experts", 0, i)
                    for k in range(TOPK):
                        pe.wait_ge(diag_ready, u * TOPK + (k + 1))
                        pe.wait_ge(v_in[k % 8], u * 32 + 16 * (k // 8 + 1))
                        mm(acc[:, 0:512], dg[:, k % 8, :], v_ring[:, k % 8, 0:512], start=k == 0, stop=k == TOPK - 1)
                        mm(acc[:, 512:1024], dg[:, k % 8, :], v_ring[:, k % 8, 512:1024],
                           start=k == 0, stop=k == TOPK - 1).then_inc(v_used, 1)
                    pe.wait_ge(v_used, u * TOPK + (TOPK + 8))
                    pe.sem_inc(done[bank], 1)
            pe.wait_ge(y_ready, NU)
            for g in range(4):
                turn("back", g, [y_rows[:, tt * D + c * P:tt * D + (c + 1) * P]
                                 for c in (2 * g, 2 * g + 1) for tt in range(TT)])
            norm(3)
            norm(4)

            pe.wait_ge(h_ready, 3)
            for t in range(8):
                block_r("sgu_v", t, t, 0)
            with pe.Fori(0, 4) as i:
                for j in range(2):
                    k0 = 6 * j
                    block_t("mix", k0, k0, i)
                    block_t("mix", k0 + 1, k0 + 1, i)
                    pe.wait_ge(qkv_ready, i * 6 + (30 + 3 * j + 2))
                    for h, bank in enumerate(("SA", "S0")):
                        r = slice(HD * h, HD * h + HD)
                        claim(bank, "mix", j, i)
                        mm(ps[bank][:, 0:P], q2[r, 0:P], k2[r, 0:P], start=True, stop=True)
                        mm(ps[bank][:, P:384], q2[r, P:T], k2[r, :], start=True, stop=True).then_inc(done[bank], 1)
                    block_r("mix", k0 + 2, k0 + 2, i)
                    block_t("mix", k0 + 3, k0 + 3, i)
                    for h in range(2):
                        bank = f"T{h}"
                        pe.wait_ge(soft_p, i * 8 + (8 + 4 * j + 2 * h + 2))
                        claim(bank, "mix", j, i)
                        for n in range(3):
                            m = nc.tensor.transpose(ps[bank][:, n * P:(n + 1) * P], s2[:, h, n * P:(n + 1) * P],
                                                    ident[:, :])
                        m.then_inc(done[bank], 1)
                    block_t("mix", k0 + 4, k0 + 4, i)
                    pe.wait_ge(qkv_ready, i * 6 + (30 + 3 * j + 3))
                    claim("OT", "mix", j, i)
                    for h in range(2):
                        r = slice(HD * h, HD * h + HD)
                        pe.wait_ge(pt_ready, i * 4 + (12 + 2 * j + h + 1))
                        mm(ps["OT"][r, 0:T], v2[:, 0, r], p2[:, h, 0:T], start=True, stop=False)
                        m = mm(ps["OT"][r, P:T], v2[:, 1, r], p2[:, h, T:384], start=False, stop=True)
                    m.then_inc(done["OT"], 1)
                    pe.wait_ge(vst_ready, i * 2 + (j + 1))
                    claim("S1", "mix", j, i)
                    for tt in range(TT):
                        m = mm(ps["S1"][:, tt * P:(tt + 1) * P], vst[:, tt, :],
                               sguT[:, bass.ds(i * 2 + j, 1), :].rearrange("p a b -> p (a b)"), start=True, stop=True)
                    m.then_inc(done["S1"], 1)
                    block_t("mix", k0 + 5, k0 + 5, i)
            pe.wait_ge(merged_ready, 16)
            for t in range(KC):
                block_t("out2", t, t, 0, lambda c: merged[:, c, :])
            norm(5)
            pe.wait_ge(h_ready, 4)
            with pe.Fori(0, 4) as i:
                for t in range(8):
                    block_t("ff1", t, t, i)
            pe.wait_ge(ff_ready, DFF // P + 2)
            with pe.Fori(0, 4) as i:
                for j in range(2):
                    bank = f"M{j}"
                    claim(bank, "ff2", 0, i)
                    for q in range(4):
                        pe.wait_ge(tile_in[4 * j + q], tile_ready("ff2", 4 * j + q, i))
                        for c in range(KC):
                            m = mm(ps[bank][:, 0:T], ring[:, 4 * j + q, c, :], ffT[:, q * KC + c, :],
                                   start=q + c == 0, stop=q == 3 and c == KC - 1)
                    m.then_inc(done[bank], 1)
            norm(6)
            pe.wait_ge(h_ready, 5)
            with pe.Fori(0, 2) as i:
                for j in range(4):
                    block_t("ple", 2 * j, 2 * j, i)
                    block_t("ple", 2 * j + 1, 2 * j + 1, i, lambda c: pT[:, c, :], (0, 2))
            norm(7)
            pe.wait_ge(h_ready, 6)
            for g in range(4):
                turn("final", g, [hT[:, 4 * (g % 2) + n, (g // 2) * P:(g // 2 + 1) * P] for n in range(4)])

        @block.scalar
        def _(act):
            st = Steps(act_step)
            F = nc.scalar.activation

            def take(bank, stage, k, i=0):
                act.wait_ge(done[bank], prior(bank, stage, k, i) + 1)

            def norm(n, x_count):
                act.wait_ge(x_ready, x_count)
                F(tmp[:, :, :], xT[:, :, :], ACT.Square).then_inc(sq_ready, 1)
                take("SA", f"norm{n}", 0)
                F(rt[:, :], ps["SA"][:, 0:T], ACT.Sqrt, bias=eps[:, :], scale=1.0 / D).then_inc(free["SA"], 1)

            def shifted(n, shift):
                for c in range(KC):
                    act.wait_ge(scaled, KC * n + c + 1)
                    m = F(hT[:, c, :], tmp[:, c, :], ACT.Identity, bias=shift[:, c:c + 1])
                m.then_inc(h_ready, 1)

            take("T0", "init", 0)
            F(vecT[:, :], ps["T0"][:, 0:NVEC + 6 * KC], ACT.Copy).then_inc(free["T0"], 1)
            act.wait_ge(free["T0"], 1)
            F(silu_c[:, 0, :], col["c"], ACT.Tanh, scale=0.5).then_inc(silu_half, 1)
            for g in range(4):
                bank = f"T{(1 + g) % 2}"
                take(bank, "init", (1 + g) // 2)
                F(xT[:, 2 * g:2 * g + 2, :].rearrange("p c t -> p (c t)"), ps[bank], ACT.Copy).then_inc(free[bank], 1)
            for b in ("T0", "T1"):
                act.wait_ge(free[b], 3 if b == "T0" else 2)
            act.sem_inc(x_ready, 1)
            norm(1, 1)
            act.wait_ge(mod_ready, 4)
            shifted(0, mod[0])
            for j in range(SB_PAIRS):
                for k, dst in ((0, qs), (1, ks)):
                    b = f"M{(3 * j + k) % 2}"
                    take(b, "stick", (3 * j + k) // 2)
                    F(dst, ps[b][:, 0:T], ACT.Copy).then_inc(free[b], 1)
                    act.wait_ge(free[b], prior(b, "stick", (3 * j + k) // 2) + 1)
                    act.sem_inc(qkv_ready, 1)
                for h, bank in enumerate(("SA", "S0")):
                    act.wait_ge(free[bank], prior(bank, "stick", j) + 1)
                    F(ez[:, h, :], zm[:, h, :], ACT.Abs).then_inc(st.tick(), 1)
                for h in range(2):
                    act.wait_ge(st.sem, 4 * j + 1 + h)
                    F(ez[:, h, :], ez[:, h, :], ACT.Exp, scale=-1.0).then_inc(st.tick(), 1)
                for h in range(2):
                    act.wait_ge(st.sem, 4 * j + 3 + h)
                    F(ez[:, h, :], ez[:, h, :], ACT.Ln, bias=ones[:, 0:1]).then_inc(stick_ln, 1)
                b = f"M{(3 * j + 2) % 2}"
                take(b, "stick", (3 * j + 2) // 2)
                F(vs.rearrange("p t n -> p (t n)"), ps[b][:, 0:T], ACT.Copy).then_inc(free[b], 1)
                act.wait_ge(free[b], prior(b, "stick", (3 * j + 2) // 2) + 1)
                act.sem_inc(qkv_ready, 1)
                for h in range(2):
                    act.wait_ge(free[f"T{h}"], prior(f"T{h}", "stick", j) + 1)
                    F(ez[:, h, :], zm[:, h, :], ACT.Exp).then_inc(stick_p, 1)
                take("OT", "stick", j)
                F(osb[:, j, :], ps["OT"][:, 0:T], ACT.Copy).then_inc(free["OT"], 1)

            for g in range(4):
                bank = f"T{g % 2}"
                take(bank, "extra", g // 2)
                F(keysT[:, 4 * g:4 * g + 4, :].rearrange("p a b -> p (a b)"), ps[bank], ACT.Copy).then_inc(free[bank], 1)
            take("T0", "extra", 3)
            F(pT[:, :, :].rearrange("p c t -> p (c t)"), ps["T0"], ACT.Copy).then_inc(free["T0"], 1)

            def soft_exp_of(buf, lo, hi, h, part, mx, sm, value):
                act.wait_ge(soft_max, value)
                F(buf[:, h, lo:hi], buf[:, h, lo:hi], ACT.Exp, bias=mx[:, h, part:part + 1],
                  accum_out=sm[:, h, part:part + 1]).then_inc(soft_exp, 1)

            with act.Fori(0, DIL_HP) as i:
                for g in range(DIL_G):
                    for s, dst in enumerate((raw[:, g, 0, :], raw[:, g, 1, :],
                                             vd[:, g].rearrange("p t n -> p (t n)"))):
                        k = 3 * g + s
                        b = f"M{k % 2}"
                        take(b, "dilated", k // 2, i)
                        F(dst, ps[b][:, 0:T], ACT.Copy).then_inc(free[b], 1)
                        act.wait_ge(free[b], prior(b, "dilated", k // 2, i) + 1)
                        act.sem_inc(qkv_ready, 1)
                for h in range(2):
                    soft_exp_of(sd, 0, 384, h, 0, sm_max, sm_sum, i * 4 + (2 * h + 1))
                    soft_exp_of(sd, 384, 1152, h, 1, sm_max, sm_sum, i * 4 + (2 * h + 2))
                for h in range(2):
                    for g in range(DIL_G):
                        bank = f"T{g % 2}"
                        n = 3 + 2 * h + g // 2 if g % 2 == 0 else 3 + h
                        take(bank, "dilated", n, i)
                        F(pt[:, h, g, :], ps[bank][:, 0:384], ACT.Copy).then_inc(free[bank], 1)
                        act.wait_ge(free[bank], prior(bank, "dilated", n, i) + 1)
                        act.sem_inc(pt_ready, 1)
                take("OT", "dilated", 0, i)
                F(odl[:, bass.ds(i, 1), :].rearrange("p a t -> p (a t)"), ps["OT"][:, 0:T], ACT.Copy)\
                    .then_inc(free["OT"], 1)

            with act.Fori(0, 2) as i:
                for j in range(4):
                    for s, dst in enumerate((gate_a, gate_b)):
                        take(f"M{s}", "gates", 2 * j, i)
                        F(dst, ps[f"M{s}"][:, 0:T], ACT.Tanh, scale=0.5).then_inc(free[f"M{s}"], 1)

            act.wait_ge(rel_back, 16)
            norm(2, 2)
            act.wait_ge(mod_ready, 12)
            shifted(1, mod[3])
            with act.Fori(0, 2) as i:
                for t in range(8):
                    b = f"M{t % 2}"
                    take(b, "query", t // 2, i)
                    F(qT[:, bass.ds(i * 8 + t, 1), :].rearrange("p a t -> p (a t)"), ps[b][:, 0:T], ACT.Copy)\
                        .then_inc(free[b], 1)
            for b in ("M0", "M1"):
                act.wait_ge(free[b], prior(b, "query", 4, 1))
            act.sem_inc(q_ready, 16)
            for g in range(4):
                bank = f"T{g % 2}"
                take(bank, "rows", g // 2)
                F(h_rows[:, g * 512:(g + 1) * 512], ps[bank], ACT.Copy).then_inc(free[bank], 1)
            for g in range(8):
                bank = ("SA", "S0")[g % 2]
                take(bank, "sub", g // 2)
                F(sub[:, g * 512:(g + 1) * 512], ps[bank], ACT.Copy).then_inc(free[bank], 1)
                act.wait_ge(free[bank], prior(bank, "sub", g // 2) + 1)
                act.sem_inc(sub_ready, 1)

            with act.Fori(0, NU // 2) as i:
                for s in range(2):
                    u = i * 2 + s
                    act.wait_ge(best_ready, u + 1)
                    F(gate_w[:, s, :], best, ACT.Exp, bias=gate_n[:, s, :], accum_out=gate_s[:, s, :])\
                        .then_inc(gate_exp, 1)
                    act.wait_ge(act_arg, u + 1)
                    F(act_t[:, s, :], act_b[:, s, :], ACT.Tanh, scale=GELU_C).then_inc(act_tanh, 1)
                    act.wait_ge(wgt_ready, u + 1)
                    for k in range(TOPK):
                        act.wait_ge(v_used, u * TOPK + (k + 1))
                        F(dg[:, k % 8, :], ident[:, :], ACT.Copy, scale=wgt[:, s, k:k + 1]).then_inc(diag_ready, 1)

            norm(3, 3)
            norm(4, 4)
            for t in range(8):
                b = f"M{t % 2}"
                take(b, "sgu_v", t // 2)
                if t > 0:
                    act.wait_ge(zv_ready, t)
                F(g_raw, ps[b][:, 0:T], ACT.Copy).then_inc(free[b], 1)
                act.wait_ge(free[b], prior(b, "sgu_v", t // 2) + 1)
                F(g_sq, g_raw, ACT.Square).then_inc(zv_raw, 1)
                act.wait_ge(zv_arg, t + 1)
                F(g_th, g_sq, ACT.Tanh, scale=GELU_C).then_inc(zv_tanh, 1)
            for tt in range(TT):
                act.wait_ge(ln_c, tt + 1)
                F(zsq, zv[:, tt, :], ACT.Square, accum_out=ln_q[:, tt, :]).then_inc(ln_sq, 1)
                act.wait_ge(ln_sq, tt + 1)
                F(ln_r[:, tt, :], ln_q[:, tt, :], ACT.Sqrt, bias=eps[:, :], scale=1.0 / D).then_inc(ln_root, 1)

            with act.Fori(0, 4) as i:
                for j in range(2):
                    k0 = 6 * j

                    def copy(k, dst):
                        b = f"M{k % 2}"
                        take(b, "mix", k // 2, i)
                        F(dst, ps[b][:, 0:T], ACT.Copy).then_inc(free[b], 1)
                        act.wait_ge(free[b], prior(b, "mix", k // 2, i) + 1)

                    copy(k0, q2)
                    act.sem_inc(qkv_ready, 1)
                    copy(k0 + 1, k2)
                    act.sem_inc(qkv_ready, 1)
                    for h in range(2):
                        soft_exp_of(s2, 0, P, h, 0, mx2, sm2, i * 8 + (8 + 4 * j + 2 * h + 1))
                        soft_exp_of(s2, P, 384, h, 1, mx2, sm2, i * 8 + (8 + 4 * j + 2 * h + 2))
                    copy(k0 + 2, v2.rearrange("p t n -> p (t n)"))
                    act.sem_inc(qkv_ready, 1)
                    act.wait_ge(merged_ready, i * 2 + (KC + j))
                    copy(k0 + 3, g_raw)
                    F(g_sq, g_raw, ACT.Square).then_inc(u_raw, 1)
                    for h in range(2):
                        take(f"T{h}", "mix", j, i)
                        F(p2[:, h, :], ps[f"T{h}"][:, 0:384], ACT.Copy).then_inc(free[f"T{h}"], 1)
                        act.wait_ge(free[f"T{h}"], prior(f"T{h}", "mix", j, i) + 1)
                        act.sem_inc(pt_ready, 1)
                    act.wait_ge(u_arg, i * 2 + (j + 1))
                    F(g_th, g_sq, ACT.Tanh, scale=GELU_C).then_inc(u_tanh, 1)
                    for s, dst in enumerate((ga, gb)):
                        b = f"M{s}"
                        take(b, "mix", (k0 + 4 + s) // 2, i)
                        F(dst, ps[b][:, 0:T], ACT.Tanh, scale=0.5).then_inc(free[b], 1)

            norm(5, 5)
            with act.Fori(0, 4) as i:
                for t in range(8):
                    b = f"M{t % 2}"
                    take(b, "ff1", t // 2, i)
                    act.wait_ge(ff_ready, i * 8 + (t + 1))
                    F(relu[:, t % 2, :], ps[b][:, 0:T], ACT.Relu).then_inc(free[b], 1)
            norm(6, 6)
            with act.Fori(0, 2) as i:
                for j in range(4):
                    take("M0", "ple", j, i)
                    act.wait_ge(free["M1"], prior("M1", "ple", j, i))
                    F(gate_p[:, 0, :], ps["M0"][:, 0:T], ACT.Tanh, scale=0.5).then_inc(free["M0"], 1)
            norm(7, 7)
            for g in range(4):
                bank = f"T{g % 2}"
                take(bank, "final", g // 2)
                F(o_rows[:, g // 2, (g % 2) * 512:(g % 2 + 1) * 512], ps[bank], ACT.Copy).then_inc(free[bank], 1)

        @block.vector
        def _(dve):
            st = Steps(dve_step)
            V = nc.vector

            def take(bank, stage, k, i=0):
                dve.wait_ge(done[bank], prior(bank, stage, k, i) + 1)

            def own():
                dve.wait_ge(st.sem, st.now())

            def norm(n, gains, dst, signal):
                dve.wait_ge(free["SA"], prior("SA", f"norm{n}", 0) + 1)
                V.reciprocal(rstd[:, :], rt[:, :]).then_inc(st.tick(), 1)
                own()
                for c in range(KC):
                    m = V.scalar_tensor_tensor(dst[:, c, :], xT[:, c, :], gains[:, c:c + 1], rstd[:, :],
                                               ALU.mult, ALU.mult)
                    if signal is scaled:
                        m.then_inc(scaled, 1)
                if signal is not scaled:
                    m.then_inc(signal, 1)

            def ada_chunk(ch):
                a = ada_sum[:, ch % 2, :]
                dve.wait_ge(ada_in[ch % 2], 16 * (ch // 2 + 1))
                if ch >= 2:
                    dve.wait_ge(mod_ready, ch - 1)
                for c in range(KC):
                    w = ada[:, ch % 2, c, :]
                    if c == 0:
                        m = V.tensor_scalar(a, w, silu_c[:, 1, 0:1], None, ALU.mult)
                    else:
                        own()
                        m = V.scalar_tensor_tensor(a, w, silu_c[:, 1, c:c + 1], a, ALU.mult, ALU.add)
                    if c < KC - 1:
                        m.then_inc(st.tick(), 1)
                m.then_inc(ada_ready, 1)
                dve.wait_ge(ada_ready, ch + 1)
                dve.sem_inc(ada_used, 1)

            def ada_bias(ch, stage, k):
                take("S1", stage, k)
                V.tensor_tensor(modT[:, 4 * ch:4 * ch + 4], ps["S1"][:, 0:4], b_ada_col[:, 4 * ch:4 * ch + 4], ALU.add)\
                    .then_inc(free["S1"], 1)
                dve.wait_ge(free["S1"], prior("S1", stage, k) + 1)
                dve.sem_inc(mod_ready, 1)

            dve.wait_ge(silu_half, 1)
            V.tensor_scalar(silu_c[:, 0, :], silu_c[:, 0, :], 0.5, 0.5, ALU.mult, ALU.add).then_inc(st.tick(), 1)
            own()
            V.tensor_tensor(silu_c[:, 1, :], silu_c[:, 0, :], col["c"], ALU.mult).then_inc(st.tick(), 1)
            own()
            for ch in range(4):
                ada_chunk(ch)
                ada_bias(ch, "init", ch)
            dve.wait_ge(mod_ready, 4)
            V.scalar_tensor_tensor(gain[:, 0, :], mod[1], 1.0, col["g_mix"], ALU.add, ALU.mult).then_inc(st.tick(), 1)
            norm(1, gain[:, 0, :], tmp, scaled)
            dve.wait_ge(const_in, 7 * 16)
            for j in range(SB_PAIRS):
                for h, bank in enumerate(("SA", "S0")):
                    take(bank, "stick", j)
                    V.scalar_tensor_tensor(zm[:, h, :], ps[bank][:, 0:384], SCALE, stick_neg, ALU.mult, ALU.add)\
                        .then_inc(free[bank], 1)
                if j > 0:
                    for k in (2 * j - 2, 2 * j - 1):
                        ada_bias(4 + k, "stick", k)
                for h in range(2):
                    dve.wait_ge(stick_ln, 2 * j + h + 1)
                    V.scalar_tensor_tensor(sp[:, h, :], zm[:, h, :], 0.0, ez[:, h, :], ALU.max, ALU.add)\
                        .then_inc(stick_sp, 1)
                for h in range(2):
                    take(f"T{h}", "stick", j)
                    V.tensor_tensor(zm[:, h, :], zm[:, h, :], ps[f"T{h}"][:, 0:384], ALU.subtract)\
                        .then_inc(free[f"T{h}"], 1)
                for k in (2 * j, 2 * j + 1):
                    ada_chunk(4 + k)
            for k in (6, 7):
                ada_bias(4 + k, "stick", k)
            V.scalar_tensor_tensor(gain[:, 1, :], mod[4], 1.0, col["g_ffn"], ALU.add, ALU.mult).then_inc(st.tick(), 1)

            for g in range(2):
                bank = f"T{g}"
                take(bank, "extra", 2)
                V.tensor_tensor(sguT[:, 4 * g:4 * g + 4, :], ps[bank].rearrange("p (a b) -> p a b", b=P),
                                sgu_mask.unsqueeze(1).broadcast_to([P, 4, P]), ALU.mult).then_inc(free[bank], 1)
            take("SA", "extra", 0)
            V.tensor_tensor(rel_row, ps["SA"][0:AH, 0:RMAX], rel_neg, ALU.add).then_inc(free["SA"], 1)
            dve.wait_ge(free["SA"], prior("SA", "extra", 0) + 1)
            dve.sem_inc(rel_out, 1)

            def soft_norm(buf, splits, h, sm, iv, value):
                dve.wait_ge(soft_exp, value)
                V.reciprocal(iv[:, h, :], sm[:, h, :]).then_inc(st.tick(), 1)
                own()
                for part, (lo, hi) in enumerate(splits):
                    V.tensor_scalar(buf[:, h, lo:hi], buf[:, h, lo:hi], iv[:, h, part:part + 1], None, ALU.mult)\
                        .then_inc(soft_p, 1)

            with dve.Fori(0, DIL_HP) as i:
                st.enter(i, 8)
                for g in range(DIL_G):
                    if g > 0:
                        dve.wait_ge(roped_ready, i * DIL_G + g)
                    for s in range(2):
                        take(f"T{s}", "dilated", g, i)
                        V.tensor_tensor(rope_b[:, s, :], ps[f"T{s}"][:, 0:T], sinT, ALU.mult).then_inc(free[f"T{s}"], 1)
                        V.tensor_tensor(rope_a[:, s, :], raw[:, g, s, :], cosT, ALU.mult).then_inc(st.tick(), 1)
                    own()
                    dve.wait_ge(free["T1"], prior("T1", "dilated", g, i) + 1)
                    V.tensor_tensor(roped[:, g], rope_a, rope_b, ALU.add).then_inc(roped_ready, 1)
                for h in range(2):
                    take("SA", "dilated", h, i)
                    V.scalar_tensor_tensor(sd[:, h, 0:384], ps["SA"][:, 0:384], SCALE, dil_neg[:, 0:384],
                                           ALU.mult, ALU.add).then_inc(free["SA"], 1)
                    take("S0", "dilated", h, i)
                    V.scalar_tensor_tensor(sd[:, h, 384:1152], wide[:, 0:768], SCALE, dil_neg[:, 384:1152],
                                           ALU.mult, ALU.add).then_inc(free["S0"], 1)
                    dve.wait_ge(free["S0"], prior("S0", "dilated", h, i) + 1)
                    V.tensor_reduce(sm_max[:, h, 0:1], sd[:, h, 0:384], AX.X, ALU.max, negate=True).then_inc(soft_max, 1)
                    V.tensor_reduce(sm_max[:, h, 1:2], sd[:, h, 384:1152], AX.X, ALU.max, negate=True)\
                        .then_inc(soft_max, 1)
                for h in range(2):
                    soft_norm(sd, ((0, 384), (384, 1152)), h, sm_sum, sm_inv, i * 4 + (2 * h + 2))
                st.leave(DIL_HP)

            with dve.Fori(0, 2) as i:
                st.enter(i, 8)
                for j in range(4):
                    for s, (g, br) in enumerate(((gate_a, br_a), (gate_b, br_b))):
                        dve.wait_ge(free[f"M{s}"], prior(f"M{s}", "gates", 2 * j, i) + 1)
                        V.tensor_scalar(g, g, 0.5, 0.5, ALU.mult, ALU.add).then_inc(st.tick(), 1)
                        take(f"M{s}", "gates", 2 * j + 1, i)
                        own()
                        V.tensor_tensor(br, g, ps[f"M{s}"][:, 0:T], ALU.mult).then_inc(free[f"M{s}"], 1)
                    for s in range(2):
                        dve.wait_ge(free[f"M{s}"], prior(f"M{s}", "gates", 2 * j + 1, i) + 1)
                    V.tensor_tensor(merged[:, bass.ds(i * 4 + j, 1), :].rearrange("p a t -> p (a t)"), br_a, br_b, ALU.add)\
                        .then_inc(merged_ready, 1)
                st.leave(2)
            for t in range(KC):
                b = f"M{t % 2}"
                take(b, "out1", t // 2)
                V.scalar_tensor_tensor(xT[:, t, :], ps[b][:, 0:T], mod[2][:, t:t + 1], xT[:, t, :], ALU.mult, ALU.add)\
                    .then_inc(free[b], 1)
            for b in ("M0", "M1"):
                dve.wait_ge(free[b], prior(b, "out1", 4))
            dve.sem_inc(x_ready, 1)
            norm(2, gain[:, 1, :], tmp, scaled)

            def top16(vals, idx, src, work):
                own()
                dve.sem_inc(route_step, 1)
                V.max(vals[:, 0:8], src).then_inc(st.tick(), 1)
                own()
                dve.sem_inc(route_step, 1)
                V.max_index(idx[:, 0:8], vals[:, 0:8], src).then_inc(st.tick(), 1)
                V.match_replace(work, vals[:, 0:8], src, LOWEST).then_inc(st.tick(), 1)
                own()
                dve.sem_inc(route_step, 1)
                V.max(vals[:, 8:16], work).then_inc(st.tick(), 1)
                own()
                dve.sem_inc(route_step, 1)
                V.max_index(idx[:, 8:16], vals[:, 8:16], work).then_inc(st.tick(), 1)

            def route(u, s):
                V.tensor_copy(sub_w.rearrange("p a b -> p (a b)"), sub[:, bass.ds(u * (2 * NK), 2 * NK)])\
                    .then_inc(st.tick(), 1)
                for half in range(2):
                    top16(s16[:, half, :], i16[:, half, :], sub_w[:, half, :], cand_w[:, half * NK:(half + 1) * NK])
                own()
                V.tensor_copy(i16f, i16).then_inc(st.tick(), 1)
                V.tensor_tensor(cand, s16[:, 0, :].unsqueeze(2).broadcast_to([P, TOPK, TOPK]),
                                s16[:, 1, :].unsqueeze(1).broadcast_to([P, TOPK, TOPK]), ALU.add).then_inc(st.tick(), 1)
                top16(best, pos, cand.rearrange("p a b -> p (a b)"), cand_w)
                own()
                V.tensor_scalar(gate_n[:, s, :], best[:, 0:1], -1.0, None, ALU.mult).then_inc(best_ready, 1)
                V.tensor_scalar(pos_ab[:, 0, :], pos, 4, None, ALU.logical_shift_right).then_inc(st.tick(), 1)
                V.tensor_scalar(pos_ab[:, 1, :], pos, 15, None, ALU.bitwise_and).then_inc(st.tick(), 1)
                own()
                V.tensor_copy(pos_f, pos_ab).then_inc(st.tick(), 1)
                own()
                V.tensor_tensor(hot, pos_f.rearrange("p a k -> p (a k)").unsqueeze(2).broadcast_to([P, 2 * TOPK, TOPK]),
                                iota.unsqueeze(1).broadcast_to([P, 2 * TOPK, TOPK]), ALU.is_equal).then_inc(st.tick(), 1)
                own()
                for half in range(2):
                    part = hot[:, half * TOPK:(half + 1) * TOPK, :]
                    V.tensor_tensor(part, part, i16f[:, half, :].unsqueeze(1).broadcast_to([P, TOPK, TOPK]), ALU.mult)\
                        .then_inc(st.tick(), 1)
                own()
                V.tensor_reduce(pick.rearrange("p a k -> p (a k)"), hot, AX.X, ALU.add).then_inc(st.tick(), 1)
                own()
                V.scalar_tensor_tensor(expert_f, pick[:, 0, :], float(NK), pick[:, 1, :], ALU.mult, ALU.add)\
                    .then_inc(st.tick(), 1)
                own()
                V.tensor_copy(expert[:, s, :], expert_f).then_inc(idx_ready, 1)
            ROUTE_STEPS = 26

            def tile_of(u):
                return u // NH if isinstance(u, int) else (u >> 3) & (TT - 1)

            def dots(u, s):
                for k in range(TOPK):
                    dve.wait_ge(u_in[k % 8], u * 32 + 16 * (k // 8 + 1))
                    if k >= 2 or not isinstance(u, int) or u > 0:
                        dve.wait_ge(u_used, u * TOPK + (k + 7))
                    V.scalar_tensor_tensor(dot_junk[k % 2], u_ring[:, k % 8, :], 1.0, h_rows[:, bass.ds(tile_of(u) * D, D)],
                                           ALU.mult, ALU.mult, accum_out=act_x[:, s, k:k + 1]).then_inc(u_used, 1)
                dve.wait_ge(u_used, u * TOPK + (TOPK + 8))
                x = act_x[:, s, :]
                V.tensor_tensor(act_a[:, s, :], x, x, ALU.mult).then_inc(st.tick(), 1)
                own()
                V.tensor_scalar(act_a[:, s, :], act_a[:, s, :], GELU_A, 1.0, ALU.mult, ALU.add).then_inc(st.tick(), 1)
                own()
                V.tensor_tensor(act_b[:, s, :], act_a[:, s, :], x, ALU.mult).then_inc(act_arg, 1)
                dve.wait_ge(gate_exp, u + 1)
                V.reciprocal(gate_r[:, s, :], gate_s[:, s, :]).then_inc(st.tick(), 1)
                own()
                V.tensor_scalar(gate_w[:, s, :], gate_w[:, s, :], gate_r[:, s, :], 0.5, ALU.mult, ALU.mult)\
                    .then_inc(st.tick(), 1)
                dve.wait_ge(act_tanh, u + 1)
                V.scalar_tensor_tensor(act_a[:, s, :], act_t[:, s, :], 1.0, x, ALU.add, ALU.mult).then_inc(st.tick(), 1)
                own()
                V.tensor_tensor(wgt[:, s, :], act_a[:, s, :], gate_w[:, s, :], ALU.mult).then_inc(wgt_ready, 1)

            DOT_STEPS = 5

            def add_y(u, s, i):
                bank, acc = ("S0", wide) if s == 0 else ("T0", twin)
                take(bank, "experts", 0, i)
                y = y_rows[:, bass.ds(tile_of(u) * D, D)]
                V.tensor_tensor(y, y, acc[:, :], ALU.add).then_inc(free[bank], 1)
                dve.wait_ge(free[bank], prior(bank, "experts", 0, i) + 1)
                dve.sem_inc(y_ready, 1)

            V.memset(y_rows, 0.0).then_inc(st.tick(), 1)
            dve.wait_ge(sub_ready, 8)
            own()
            route(0, 0)
            dve.sem_inc(u_used, 8)
            dots(0, 0)
            route(1, 1)

            def unit(u, s, before):
                dots(u, s)
                add_y(u - 1, 1 - s, before)
                dve.wait_ge(v_used, u * TOPK + 8)
                route(u + 1, 1 - s)

            with dve.Fori(0, NU // 2 - 1) as i:
                st.enter(i, 2 * (ROUTE_STEPS + DOT_STEPS))
                unit(i * 2 + 1, 1, i)
                unit(i * 2 + 2, 0, i)
                st.leave(NU // 2 - 1)
            dots(NU - 1, 1)
            add_y(NU - 2, 0, NU // 2 - 1)
            add_y(NU - 1, 1, NU // 2 - 1)
            for g in range(4):
                bank = f"T{g % 2}"
                take(bank, "back", g // 2)
                for n in range(2):
                    c = 2 * g + n
                    m = V.scalar_tensor_tensor(xT[:, c, :], ps[bank][:, n * T:(n + 1) * T], mod[5][:, c:c + 1], xT[:, c, :],
                                               ALU.mult, ALU.add)
                m.then_inc(free[bank], 1)
            for b in ("T0", "T1"):
                dve.wait_ge(free[b], prior(b, "back", 2))
            dve.sem_inc(x_ready, 1)
            norm(3, col["g_final"], xT, x_ready)

            norm(4, col["norm_mix_g_2"], hT, h_ready)

            def gelu_arg(ready, value, signal):
                dve.wait_ge(ready, value)
                V.tensor_scalar(g_sq, g_sq, GELU_A, 1.0, ALU.mult, ALU.add).then_inc(st.tick(), 1)
                own()
                V.tensor_tensor(g_sq, g_sq, g_raw, ALU.mult).then_inc(signal, 1)

            def gelu_half(ready, value):
                dve.wait_ge(ready, value)
                V.tensor_scalar(g_th, g_th, 0.5, 0.5, ALU.mult, ALU.add).then_inc(st.tick(), 1)
                own()

            for t in range(8):
                gelu_arg(zv_raw, t + 1, zv_arg)
                gelu_half(zv_tanh, t + 1)
                V.tensor_tensor(zv[:, :, t * P:(t + 1) * P], g_th.rearrange("p (t n) -> p t n", n=P),
                                g_raw.rearrange("p (t n) -> p t n", n=P), ALU.mult).then_inc(zv_ready, 1)
            dve.wait_ge(zv_ready, 8)
            for tt in range(TT):
                V.tensor_reduce(ln_s[:, tt, :], zv[:, tt, :], AX.X, ALU.add).then_inc(st.tick(), 1)
                own()
                V.tensor_scalar(ln_m[:, tt, :], ln_s[:, tt, :], 1.0 / D, None, ALU.mult).then_inc(st.tick(), 1)
                own()
                V.tensor_scalar(zv[:, tt, :], zv[:, tt, :], ln_m[:, tt, :], None, ALU.subtract).then_inc(ln_c, 1)
            for tt in range(TT):
                dve.wait_ge(ln_root, tt + 1)
                V.reciprocal(ln_i[:, tt, :], ln_r[:, tt, :]).then_inc(st.tick(), 1)
                own()
                V.tensor_scalar(zv[:, tt, :], zv[:, tt, :], ln_i[:, tt, :], None, ALU.mult).then_inc(vn_ready, 1)
            dve.wait_ge(vn_ready, 2)
            dve.wait_ge(layer2_in, 64)

            MIX_STEPS = 12
            with dve.Fori(0, 4) as i:
                st.enter(i, 2 * MIX_STEPS)
                for j in range(2):
                    jj = i * 2 + j
                    for h, bank in enumerate(("SA", "S0")):
                        take(bank, "mix", j, i)
                        V.scalar_tensor_tensor(s2[:, h, 0:P], ps[bank][:, 0:P], SCALE,
                                               rel[:, bass.ds(i * (4 * T) + ((2 * j + h) * T + P), P)], ALU.mult, ALU.add)\
                            .then_inc(st.tick(), 1)
                        V.scalar_tensor_tensor(s2[:, h, P:384], ps[bank][:, P:384], SCALE,
                                               rel[:, bass.ds(i * (4 * T) + (2 * j + h) * T, T)], ALU.mult, ALU.add)\
                            .then_inc(free[bank], 1)
                        dve.wait_ge(free[bank], prior(bank, "mix", j, i) + 1)
                        own()
                        V.tensor_reduce(mx2[:, h, 0:1], s2[:, h, 0:P], AX.X, ALU.max, negate=True).then_inc(soft_max, 1)
                        V.tensor_reduce(mx2[:, h, 1:2], s2[:, h, P:384], AX.X, ALU.max, negate=True).then_inc(soft_max, 1)
                    for h in range(2):
                        soft_norm(s2, ((0, P), (P, 384)), h, sm2, iv2, i * 8 + (8 + 4 * j + 2 * h + 2))
                    vcols = zv[:, :, bass.ds(jj * P, P)]
                    V.tensor_tensor(vst, vcols, ln_g[:, bass.ds(jj * P, P)].unsqueeze(1).broadcast_to([P, TT, P]),
                                    ALU.mult).then_inc(st.tick(), 1)
                    own()
                    V.tensor_tensor(vst, vst, ln_b[:, bass.ds(jj * P, P)].unsqueeze(1).broadcast_to([P, TT, P]),
                                    ALU.add).then_inc(vst_ready, 1)
                    gelu_arg(u_raw, jj + 1, u_arg)
                    gelu_half(u_tanh, jj + 1)
                    V.tensor_tensor(u_act, g_th, g_raw, ALU.mult).then_inc(st.tick(), 1)
                    take("S1", "mix", j, i)
                    V.tensor_tensor(ya.rearrange("p (t n) -> p t n", n=P),
                                    ps["S1"][:, 0:T].rearrange("p (t n) -> p t n", n=P),
                                    bs_rows[:, bass.ds(jj * P, P)].unsqueeze(1).broadcast_to([P, TT, P]), ALU.add)\
                        .then_inc(free["S1"], 1)
                    dve.wait_ge(free["S1"], prior("S1", "mix", j, i) + 1)
                    own()
                    V.tensor_tensor(ya, ya, u_act, ALU.mult).then_inc(st.tick(), 1)
                    for s, g in enumerate((ga, gb)):
                        b = f"M{s}"
                        dve.wait_ge(free[b], prior(b, "mix", (6 * j + 4 + s) // 2, i) + 1)
                        V.tensor_scalar(g, g, 0.5, 0.5, ALU.mult, ALU.add).then_inc(st.tick(), 1)
                    own()
                    V.tensor_tensor(ya, ya, ga, ALU.mult).then_inc(st.tick(), 1)
                    take("OT", "mix", j, i)
                    V.tensor_tensor(gb, gb, ps["OT"][:, 0:T], ALU.mult).then_inc(free["OT"], 1)
                    dve.wait_ge(free["OT"], prior("OT", "mix", j, i) + 1)
                    own()
                    V.tensor_tensor(merged[:, bass.ds(jj, 1), :].rearrange("p a t -> p (a t)"), ya, gb, ALU.add)\
                        .then_inc(merged_ready, 1)
                st.leave(4)
            for t in range(KC):
                b = f"M{t % 2}"
                take(b, "out2", t // 2)
                V.tensor_tensor(xT[:, t, :], xT[:, t, :], ps[b][:, 0:T], ALU.add).then_inc(free[b], 1)
            for b in ("M0", "M1"):
                dve.wait_ge(free[b], prior(b, "out2", 4))
            dve.sem_inc(x_ready, 1)
            norm(5, col["norm_ffn_g_2"], hT, h_ready)
            dve.sem_inc(ff_ready, 2)
            with dve.Fori(0, 4) as i:
                for t in range(8):
                    b = f"M{t % 2}"
                    dve.wait_ge(free[b], prior(b, "ff1", t // 2, i) + 1)
                    V.tensor_tensor(ffT[:, bass.ds(i * 8 + t, 1), :].rearrange("p a t -> p (a t)"), relu[:, t % 2, :],
                                    relu[:, t % 2, :], ALU.mult).then_inc(ff_ready, 1)
            with dve.Fori(0, 4) as i:
                for j in range(2):
                    b = f"M{j}"
                    take(b, "ff2", 0, i)
                    xs = xT[:, bass.ds(i * 2 + j, 1), :].rearrange("p a t -> p (a t)")
                    V.tensor_tensor(xs, xs, ps[b][:, 0:T], ALU.add).then_inc(free[b], 1)
            for b in ("M0", "M1"):
                dve.wait_ge(free[b], prior(b, "ff2", 1, 3))
            dve.sem_inc(x_ready, 1)
            norm(6, col["norm_ple_g_2"], hT, h_ready)
            with dve.Fori(0, 2) as i:
                st.enter(i, 8)
                for j in range(4):
                    dve.wait_ge(free["M0"], prior("M0", "ple", j, i) + 1)
                    V.tensor_scalar(gate_p[:, 1, :], gate_p[:, 0, :], 0.5, 0.5, ALU.mult, ALU.add).then_inc(st.tick(), 1)
                    take("M1", "ple", j, i)
                    own()
                    V.tensor_tensor(prod_p[:, j % 2, :], gate_p[:, 1, :], ps["M1"][:, 0:T], ALU.mult)\
                        .then_inc(free["M1"], 1)
                    dve.wait_ge(free["M1"], prior("M1", "ple", j, i) + 1)
                    xs = xT[:, bass.ds(i * 4 + j, 1), :].rearrange("p a t -> p (a t)")
                    V.tensor_tensor(xs, xs, prod_p[:, j % 2, :], ALU.add).then_inc(st.tick(), 1)
                st.leave(2)
            own()
            dve.sem_inc(x_ready, 1)
            norm(7, col["norm_final_g_2"], hT, h_ready)


def shape_constants():
    f = np.float32
    p, t = np.arange(P), np.arange(T)
    half = HD // 2
    inv = (f(10000.0) ** (-np.arange(half, dtype=f) / f(half))).astype(f)
    ang = (t.astype(f)[:, None] * inv[None, :]).astype(f)
    K = {"ident": np.eye(P, dtype=f), "tri": (p[:, None] >= p[None, :]).astype(f),
         "cos": np.cos(ang).astype(f).T[p % half], "sin": np.sin(ang).astype(f).T[p % half]}
    rot = np.zeros((P, P), f)
    for j in range(P):
        if j % HD < half:
            rot[j + half, j] = -1
        else:
            rot[j - half, j] = 1
    K["rot"] = rot
    before = np.where(p[:, None] < p[None, :], 0, NEG)
    K["stick_neg"] = np.concatenate([before, np.zeros((P, P)), before], 1).astype(f)
    dist0, dist1 = p[:, None] - p[None, :], P + p[:, None] - t[None, :]
    ok = [[(d >= 0) & (d <= w) & (d % r == 0) for w, r in zip(DIL_WIN, DIL_RATE)] for d in (dist0, dist1)]
    K["dil_neg"] = np.concatenate([np.where(m, 0, NEG) for part in ok for m in part], 1).astype(f)
    K["sgu_mask"] = (p[:, None] <= p[None, :]).astype(f)
    n = np.maximum((T - 1) - np.arange(RMAX), 0)
    exact = NBUCK // 2
    large = exact + (np.log(np.maximum(n, exact).astype(f) / f(exact)) / f(np.log(1024 / exact)) * f(exact)).astype(np.int32)
    bucket = np.where(n < exact, n, np.minimum(large, NBUCK - 1))
    causal = np.arange(RMAX) <= T - 1
    K["rel_hot"] = ((np.arange(NBUCK)[:, None] == bucket[None, :]) & causal[None, :]).astype(f)
    K["rel_neg"] = np.broadcast_to(np.where(causal, 0, NEG), (AH, RMAX)).astype(f)
    K["iota"] = np.broadcast_to(np.arange(TOPK), (P, TOPK)).astype(f)
    return {n: np.ascontiguousarray(a) for n, a in K.items()}


def kernel(**inputs):
    import concourse.bacc as bacc
    from concourse.bass_utils import run_bass_kernel_spmd as run

    nc = bacc.Bacc("TRN2", target_bir_lowering=False, num_devices=1)
    arrays, A, K = {}, {}, {}
    for name, value in inputs.items():
        arrays[f"in_{name}"] = np.ascontiguousarray(value)
        A[name] = nc.dram_tensor(f"in_{name}", arrays[f"in_{name}"].shape, F32, kind="ExternalInput").ap()
    for name, value in shape_constants().items():
        arrays[f"const_{name}"] = value
        K[name] = nc.dram_tensor(f"const_{name}", value.shape, F32, kind="ExternalInput").ap()
    rel_rows = nc.dram_tensor("rel_rows", (AH, P, RMAX), F32).ap()
    out = nc.dram_tensor("out", (1, T, D), F32, kind="ExternalOutput").ap()
    build(nc, A, K, rel_rows, out)
    r = run(nc, [arrays], core_ids=[0])
    return r.results[0]["out"]
```

```python
from contextlib import ExitStack

import numpy as np

import concourse.bass as bass
from concourse import mybir

F32 = mybir.dt.float32
U32 = mybir.dt.uint32
ALU = mybir.AluOpType
ACT = mybir.ActivationFunctionType
AX = mybir.AxisListType

P = 128
T, D = 256, 1024
TT, KC = T // P, D // P
HD = 64
SBW, DILW = 512, 768
SB_PAIRS = SBW // P
DIL_G, DIL_HP = 3, 2
DIL_RATE = (1, 4, 16)
DIL_WIN = (128, 512, 2048)
NH, NK, TOPK = 8, 128, 16
NU = TT * NH
DFF = 4096
AH = 16
NBUCK = 32
PLE = 256
EPS = 1e-6
SCALE = HD ** -0.5
GELU_A, GELU_C = 0.044715, float(np.sqrt(2.0 / np.pi))
NEG = -1e30
LOWEST = -3.0e38
RMAX = 512

RING = 12
TILES = {
    "stick": (12, 1, list(range(12)), [1] * 12),
    "dilated": (9, 2, list(range(9)), [1] * 9),
    "gates": (12, 2, [4 * j + b for j in range(4) for b in (0, 1, 3)], [1, 1, 2] * 4),
    "out1": (8, 1, list(range(8)), [1] * 8),
    "query": (12, 1, list(range(12)), [1] * 12),
    "query2": (4, 1, list(range(4)), [1] * 4),
    "sgu_v": (8, 1, list(range(8)), [1] * 8),
    "mix": (12, 4, list(range(12)), [1] * 12),
    "out2": (8, 1, list(range(8)), [1] * 8),
    "ff1": (8, 4, list(range(8)), [1] * 8),
    "ff2": (8, 4, [0] * 4 + [1] * 4, [1] * 8),
    "ple": (8, 2, list(range(8)), [1] * 8),
}
USES = {
    "init": (1, {"T0": 3, "T1": 2, "S0": 2, "S1": 2}),
    "norm1": (1, {"SA": 1}),
    "stick": (1, {"M0": 6, "M1": 6, "SA": 8, "S0": 4, "S1": 10, "T0": 4, "T1": 4, "OT": 4}),
    "dilated": (2, {"M0": 5, "M1": 4, "T0": 7, "T1": 5, "SA": 2, "S0": 2, "OT": 1}),
    "ada": (1, {"S1": 2}),
    "gates": (2, {"M0": 8, "M1": 8}),
    "out1": (1, {"M0": 4, "M1": 4}),
    "norm2": (1, {"SA": 1}),
    "query": (1, {"M0": 6, "M1": 6}),
    "query2": (1, {"M0": 2, "M1": 2}),
    "rows": (1, {"T0": 2, "T1": 2}),
    "sub": (1, {"SA": 4, "OT": 4}),
    "back": (1, {"T0": 2, "T1": 2}),
    "norm3": (1, {"SA": 1}),
    "norm4": (1, {"SA": 1}),
    "sgu_v": (1, {"M0": 4, "M1": 4}),
    "mix": (4, {"M0": 6, "M1": 6, "SA": 2, "S0": 2, "S1": 2, "T0": 2, "T1": 2, "OT": 2}),
    "out2": (1, {"M0": 4, "M1": 4}),
    "norm5": (1, {"SA": 1}),
    "ff1": (4, {"M0": 4, "M1": 4}),
    "ff2": (4, {"M0": 1, "M1": 1}),
    "norm6": (1, {"SA": 1}),
    "ple": (2, {"M0": 4, "M1": 4}),
    "norm7": (1, {"SA": 1}),
    "final": (1, {"T0": 2, "T1": 2}),
}
DIL_ORDER = [(s, g) for g in range(DIL_G) for s in (0, 1)] + [(2, g) for g in range(DIL_G)]
BANKS = ("M0", "M1", "SA", "S0", "S1", "T0", "T1", "OT")


def prior(bank, stage, k, i=0):
    n = 0
    for name, (bodies, per) in USES.items():
        if name == stage:
            return i * per[bank] + (n + k)
        n += bodies * per.get(bank, 0)
    raise KeyError(stage)


def tile_loads(slot, stage):
    n = 0
    for name, (tiles, bodies, _, dmas) in TILES.items():
        if name == stage:
            return n
        if slot < tiles:
            n += bodies * dmas[slot]
    raise KeyError(stage)


def tile_ready(stage, t, i=0):
    dmas = TILES[stage][3][t]
    return i * (16 * dmas) + 16 * (tile_loads(t, stage) + dmas)


def last_user(slot, stage):
    found = None
    for name, (tiles, bodies, free_after, _) in TILES.items():
        if name == stage:
            return found
        if slot < tiles:
            k = free_after[slot]
            found = (f"M{k % 2}", prior(f"M{k % 2}", name, k // 2, bodies - 1) + 1)
    raise KeyError(stage)


def query_block(k):
    return ("query", k) if k < RING else ("query2", k - RING)


class Steps:

    def __init__(self, sem):
        self.sem, self.n, self.reg, self.per, self.at = sem, 0, None, 0, 0

    def tick(self):
        self.n += 1
        return self.sem

    def now(self):
        return self.n if self.reg is None else self.reg * self.per + self.n

    def enter(self, reg, per):
        self.reg, self.per, self.at = reg, per, self.n

    def leave(self, bodies):
        assert self.n - self.at == self.per, (self.n - self.at, self.per)
        self.n, self.reg = self.at + bodies * self.per, None


def build(nc, A, K, rel_rows, out):
    with ExitStack() as ctx:
        def sb(name, shape, dt=F32):
            return ctx.enter_context(nc.sbuf_tensor(name, shape, dt))

        def sem(name):
            return ctx.enter_context(nc.semaphore(name))

        ident = sb("ident", [P, P])
        ones = sb("ones", [P, P])
        eps = sb("eps", [P, 1])
        xT = sb("xT", [P, KC, T])
        hT = sb("hT", [P, KC, T])
        tmp = sb("tmp", [P, KC, T])
        merged = sb("merged", [P, KC, T])
        rt = sb("rt", [P, T])
        rstd = sb("rstd", [P, T])
        warm = sb("warm", [P, 8])
        ring = sb("ring", [P, RING, KC, P])
        NVEC = 8 * KC
        vec_rows = sb("vec_rows", [NVEC + 6 * KC, P])
        vecT = sb("vecT", [P, NVEC + 6 * KC])
        names = ("c", "g_mix", "g_ffn", "g_final", "norm_mix_g_2", "norm_ffn_g_2", "norm_ple_g_2",
                 "norm_final_g_2")
        col = {n: vecT[:, KC * i:KC * (i + 1)] for i, n in enumerate(names)}
        b_ada_col = vecT[:, NVEC:NVEC + 6 * KC]
        silu_c = sb("silu_c", [P, 2, KC])
        modT = sb("modT", [P, 6 * KC])
        mod = [modT[:, KC * i:KC * (i + 1)] for i in range(6)]
        gain = sb("gain", [P, 2, KC])
        keysT = sb("keysT", [P, 2 * NH, NK])
        sguT = sb("sguT", [P, KC, P])
        pT = sb("pT", [P, 2, T])
        iota = sb("iota", [P, TOPK])[:, :]
        arena = sb("arena", [P, 27300])
        carved = [0]

        def carve(*shape, dt=F32, parts=P):
            n = int(np.prod(shape))
            ap = arena[0:parts, carved[0]:carved[0] + n]
            carved[0] += n
            assert carved[0] <= 27300, carved[0]
            if dt is not F32:
                ap = ap.bitcast(dt)
            if len(shape) == 2:
                ap = ap.rearrange("p (a b) -> p a b", b=shape[1])
            elif len(shape) == 3:
                ap = ap.rearrange("p (a b c) -> p a b c", b=shape[1], c=shape[2])
            return ap

        ada = carve(2, KC, 512)
        ada_sum = carve(2, 512)
        tri = carve(P)
        rot = carve(P)
        cosT, sinT = carve(T), carve(T)
        stick_neg = carve(384)
        dil_neg = carve(DIL_G * 384)
        osb = carve(SB_PAIRS, T)
        odl = carve(DIL_HP, T)
        qs, ks, vs = carve(T), carve(T), carve(TT, P)
        zm, ez, sp = carve(2, 384), carve(2, 384), carve(2, 384)
        gate_a, gate_b, br_a, br_b = carve(T), carve(T), carve(T), carve(T)
        mark = carved[0]
        x_rows = carve(TT, D)
        key_rows = carve(2 * NH, P)
        sgu_rows = carve(KC, P)
        sgu_mask = carve(P)
        p_rows = carve(TT, PLE)
        rel_tab = carve(AH, parts=NBUCK)
        rel_hot = carve(RMAX, parts=NBUCK)
        rel_neg = carve(RMAX, parts=AH)
        rel_row = tmp[0:AH, 0:2, :].rearrange("p a t -> p (a t)")
        carved[0] = mark
        raw = carve(DIL_G, 2, T)
        roped = carve(DIL_G, 2, T)
        rope_a, rope_b = carve(2, T), carve(2, T)
        vd = carve(DIL_G, TT, P)
        sd = carve(2, DIL_G * 384)
        pt = carve(2, DIL_G, 384)
        sm_max, sm_sum, sm_inv = carve(2, 2), carve(2, 2), carve(2, 2)
        carved[0] = 0
        sub = carve(TT * 2 * NH * NK)
        y_rows = sub[:, 0:TT * D]
        h_rows = carve(TT, D)
        v_first = carve(8, D)
        qT = carve(4, T)
        u_ring = carve(8, D)
        dg = carve(8, P)
        dot_junk = tmp[:, 0:4, :].rearrange("p a t -> p (a t)")
        v_ring = [v_first[:, n, :] for n in range(8)] + \
            [b.rearrange("p a t -> p (a t)") for b in (tmp[:, 4:8, :], merged[:, 4:8, :])] + \
            [ring[:, n, :, :].rearrange("p c n -> p (c n)") for n in range(8, RING)] + \
            [b.rearrange("p a t -> p (a t)") for b in (hT[:, 0:4, :], hT[:, 4:8, :])]
        VR = len(v_ring)
        s16 = carve(2, TOPK)
        i16 = carve(2, TOPK, dt=U32)
        i16f = carve(2, TOPK)
        sub_w = carve(2, NK)
        cand, cand_w = carve(TOPK, TOPK), carve(TOPK * TOPK)
        best_2 = carve(2, TOPK)
        pos = carve(TOPK, dt=U32)
        pos_ab = carve(2, TOPK, dt=U32)
        pos_f = carve(2, TOPK)
        hot = merged[:, 0:2, :].rearrange("p a t -> p (a t)").rearrange("p (k a) -> p k a", a=TOPK)
        pick = carve(2, TOPK)
        expert_f = carve(TOPK)
        expert = carve(2, TOPK, dt=U32)
        gate_w, gate_n = carve(2, TOPK), carve(2, 1)
        gate_s, gate_r = carve(2, 1), carve(2, 1)
        act_x, act_a, act_b, act_t = carve(2, TOPK), carve(2, TOPK), carve(2, TOPK), carve(2, TOPK)
        wgt = carve(2, TOPK)
        carved[0] = 0
        rel = carve(AH * T)
        bs_rows = carve(KC * P)
        ln_g, ln_b = carve(D), carve(D)
        zv = carve(TT, D)
        zsq = carve(TT, D)
        ln_part = carve(TT, KC)
        ln_s, ln_m, ln_q, ln_r, ln_i = carve(TT), carve(TT), carve(TT), carve(TT), carve(TT)
        g_raw, g_sq, g_th, u_act = carve(2, T), carve(2, T), carve(2, T), carve(T)
        vst = carve(TT, P)
        q2, k2, v2 = carve(T), carve(T), carve(TT, P)
        s2, p2 = carve(2, 384), carve(2, 384)
        ga, gb, ya = carve(T), carve(T), carve(T)
        mx2, sm2, iv2 = carve(2, 2), carve(2, 2), carve(2, 2)
        mark = carved[0]
        carved[0] = 0
        ffT = carve(DFF // P, T)
        relu = carve(2, T)
        gate_p, prod_p = carve(2, T), carve(2, T)
        o_rows = carve(TT, D)

        ps = {b: None for b in BANKS}
        for b in ("M0", "M1", "SA"):
            ps[b] = ctx.enter_context(nc.psum_tensor(f"ps_{b}", [P, 512], F32))[:, :]
        wide = ctx.enter_context(nc.psum_tensor("ps_S", [P, 1024], F32))
        ps["S0"], ps["S1"] = wide[:, 0:512], wide[:, 512:1024]
        twin = ctx.enter_context(nc.psum_tensor("ps_T", [P, 1024], F32))
        ps["T0"], ps["T1"] = twin[:, 0:512], twin[:, 512:1024]
        ps["OT"] = ctx.enter_context(nc.psum_tensor("ps_OT", [P, 512], F32))[:, :]

        done = {b: sem(f"done_{b}") for b in BANKS}
        free = {b: sem(f"free_{b}") for b in BANKS}
        tile_in = [sem(f"tile_in{s}") for s in range(RING)]
        vec_in, ident_in, x_in, key_in, sgu_in, p_in, rel_in, const_in, const2_in = (
            sem(n) for n in ("vec_in", "ident_in", "x_in", "key_in", "sgu_in", "p_in", "rel_in", "const_in",
                             "const2_in"))
        ada_in = [sem(f"ada_in{s}") for s in range(2)]
        ada_used, ada_ready, mod_ready = sem("ada_used"), sem("ada_ready"), sem("mod_ready")
        setup_done, silu_half, silu_ready = sem("setup_done"), sem("silu_half"), sem("silu_ready")
        rel_out, rel_back, layer2_in = sem("rel_out"), sem("rel_back"), sem("layer2_in")
        x_ready = sem("x_ready")
        sq_ready, root_ready, scaled, h_ready = sem("sq_ready"), sem("root_ready"), sem("scaled"), sem("h_ready")
        stick_sp, stick_ln, stick_p = sem("stick_sp"), sem("stick_ln"), sem("stick_p")
        qkv_ready = sem("qkv_ready")
        roped_ready = sem("roped_ready")
        soft_max, soft_exp, soft_p, pt_ready = sem("soft_max"), sem("soft_exp"), sem("soft_p"), sem("pt_ready")
        gate_ready, merged_ready = sem("gate_ready"), sem("merged_ready")
        sub_ready = sem("sub_ready")
        idx_ready, best_ready, gate_exp = sem("idx_ready"), sem("best_ready"), sem("gate_exp")
        u_in = [sem(f"u_in{s}") for s in range(8)]
        v_in = [sem(f"v_in{s}") for s in range(VR)]
        u_used, v_used, issued = sem("u_used"), sem("v_used"), sem("issued")
        act_arg, act_tanh, wgt_ready, diag_ready = sem("act_arg"), sem("act_tanh"), sem("wgt_ready"), sem("diag_ready")
        y_ready = sem("y_ready")
        zv_raw, zv_arg, zv_tanh, zv_ready = sem("zv_raw"), sem("zv_arg"), sem("zv_tanh"), sem("zv_ready")
        ln_c, ln_sq, ln_root, vst_ready = sem("ln_c"), sem("ln_sq"), sem("ln_root"), sem("vst_ready")
        u_raw, u_arg, u_tanh = sem("u_raw"), sem("u_arg"), sem("u_tanh")
        relu_ready, ff_ready = sem("relu_ready"), sem("ff_ready")
        out_done = sem("out_done")
        dve_step, act_step = sem("dve_step"), sem("act_step")
        slots_freed, route_step = sem("slots_freed"), sem("route_step")

        block = ctx.enter_context(nc.Block())

        w_in, w_in2 = A["w_in"][0], A["w_in_2"][0]

        def rows8(w):
            return w.rearrange("(c p) n -> p c n", p=P)

        w_in_v, w_in2_v = rows8(w_in), rows8(w_in2)
        w_ada_v = rows8(A["w_ada"][0])
        w_sbo_v, w_dlo_v = rows8(A["w_sb_o"][0]), rows8(A["w_dil_o"][0])
        w_out_v, w_pq_v, w_out2_v = rows8(A["w_out"][0]), rows8(A["w_pq"][0]), rows8(A["w_out_2"][0])
        w_ff1_v = rows8(A["w_ff1_2"][0])
        w_ff2_v = A["w_ff2_2"][0].rearrange("(q c p) n -> q p c n", p=P, c=KC)
        w_plg_v, w_plp_v = rows8(A["w_ple_gate_2"][0]), rows8(A["w_ple_proj_2"][0])

        def load_vectors(eng, lo, hi):
            for i in range(lo, hi):
                src = A[names[i]] if len(A[names[i]].shape) == 1 else A[names[i]][0]
                eng.dma_start(vec_rows[KC * i:KC * (i + 1), :],
                              src.rearrange("(c p) -> c p", p=P)).then_inc(vec_in, 16)

        def ada_sums(ch):
            if ch < 4:
                return ("S0", "S1")[ch % 2], "init", ch // 2
            return ("S1", "stick", ch - 4) if ch < 10 else ("S1", "ada", ch - 10)

        @block.sync
        def _(eng):
            load_vectors(eng, 0, 4)
            eng.dma_start(vec_rows[NVEC:NVEC + 6 * KC, :],
                          A["b_ada"][0].rearrange("(c p) -> c p", p=P)).then_inc(vec_in, 16)
            eng.dma_start(ident[:, :], K["ident"]).then_inc(ident_in, 16)
            eng.dma_start(x_rows, A["x"][0].rearrange("(t p) d -> p t d", p=P)).then_inc(x_in, 16)

            def tile(stage, t, i, *parts):
                if isinstance(i, int) and i == 0:
                    user = last_user(t, stage)
                    if user is not None:
                        eng.wait_ge(done[user[0]], user[1])
                else:
                    k = TILES[stage][2][t]
                    b = f"M{k % 2}"
                    eng.wait_ge(done[b], prior(b, stage, k // 2, i - 1) + 1)
                    eng.sem_inc(slots_freed, 1)
                for lo, hi, src in parts:
                    eng.dma_start(ring[:, t, lo:hi, :], src).then_inc(tile_in[t], 16)

            def cols(view, start):
                return (0, KC, view[:, :, bass.ds(start, P)])

            def stick_tiles(i):
                for j in range(SB_PAIRS):
                    for s in range(3):
                        tile("stick", 3 * j + s, i, cols(w_in_v, s * SBW + j * P))

            def dilated_tiles(i):
                for t, (s, g) in enumerate(DIL_ORDER):
                    tile("dilated", t, i, cols(w_in_v, i * P + (3 * SBW + s * DILW + g * 256)))

            def gate_tiles(i):
                for j in range(4):
                    n = i * (4 * P) + j * P
                    g0 = 3 * SBW + 3 * DILW
                    tile("gates", 3 * j, i, cols(w_in_v, n + g0))
                    tile("gates", 3 * j + 1, i, cols(w_in_v, n + (g0 + D)))
                    tile("gates", 3 * j + 2, i, (0, 4, w_sbo_v[:, :, bass.ds(n, P)]),
                         (4, 6, w_dlo_v[:, :, bass.ds(n, P)]))

            def plain_tiles(stage, view, base=0):
                def body(i):
                    for t in range(8):
                        tile(stage, t, i, cols(view, i * (8 * P) + (base + t * P)))
                return body

            def mix_tiles(i):
                for j in range(2):
                    for t, base in enumerate((2 * D, 3 * D, 4 * D, 0, 5 * D, 6 * D)):
                        tile("mix", 6 * j + t, i, cols(w_in2_v, i * (2 * P) + (base + j * P)))

            def ff2_tiles(i):
                for j in range(2):
                    for q in range(4):
                        tile("ff2", 4 * j + q, i, (0, KC, w_ff2_v[q][:, :, bass.ds(i * (2 * P) + j * P, P)]))

            def ple_tiles(i):
                for j in range(4):
                    n = i * (4 * P) + j * P
                    tile("ple", 2 * j, i, cols(w_plg_v, n))
                    tile("ple", 2 * j + 1, i, (0, 2, w_plp_v[:, :, bass.ds(n, P)]))

            def stream(stage, body):
                body(0)
                bodies = TILES[stage][1]
                if bodies > 1:
                    with eng.Fori(1, bodies) as i:
                        body(i)

            for dst, n in ((tri, "tri"), (stick_neg, "stick_neg")):
                eng.dma_start(dst, K[n]).then_inc(const_in, 16)
            eng.wait_ge(ada_in[0], 2 * 16)
            stream("stick", stick_tiles)
            for dst, n in ((rot, "rot"), (cosT, "cos"), (sinT, "sin"), (dil_neg, "dil_neg"), (iota[:, :], "iota")):
                eng.dma_start(dst, K[n]).then_inc(const2_in, 16)
            eng.dma_start(key_rows, A["peer_keys"][0].rearrange("h s n c -> n (h s) c")).then_inc(key_in, 16)
            eng.dma_start(sgu_rows, A["w_sgu_spatial_2"][0].rearrange("g t s -> t g s")).then_inc(sgu_in, 16)
            eng.dma_start(sgu_mask, K["sgu_mask"]).then_inc(sgu_in, 16)
            eng.dma_start(p_rows, A["p_2"][0, 0].rearrange("(t p) d -> p t d", p=P)).then_inc(p_in, 16)
            eng.dma_start(rel_tab, A["rel_bias_2"]).then_inc(rel_in, 16)
            eng.dma_start(rel_hot, K["rel_hot"]).then_inc(rel_in, 16)
            eng.dma_start(rel_neg, K["rel_neg"]).then_inc(rel_in, 16)
            stream("dilated", dilated_tiles)
            stream("gates", gate_tiles)
            stream("out1", plain_tiles("out1", w_out_v))
            for k in range(2 * NH):
                stage, t = query_block(k)
                tile(stage, t, 0, cols(w_pq_v, k * P))
            eng.wait_ge(v_in[VR - 1], 16 * NU)
            stream("sgu_v", plain_tiles("sgu_v", w_in2_v, D))
            stream("mix", mix_tiles)
            stream("out2", plain_tiles("out2", w_out2_v))
            stream("ff1", plain_tiles("ff1", w_ff1_v))
            stream("ff2", ff2_tiles)
            stream("ple", ple_tiles)
            for g in range(4):
                b, t, n = f"T{g % 2}", g % 2, g // 2 * 512
                eng.wait_ge(free[b], prior(b, "final", g // 2) + 1)
                eng.dma_start(out[0, t * P:(t + 1) * P, n:n + 512], o_rows[:, t, n:n + 512]).then_inc(out_done, 16)
            eng.wait_ge(out_done, 16 * 4)

        @block.gpsimd
        def _(pool):
            nc.gpsimd.memset(ones[:, :], 1.0).then_inc(setup_done, 1)
            nc.gpsimd.memset(eps[:, :], EPS).then_inc(setup_done, 1)
            pool.wait_ge(vec_in, 9 * 16)
            for ch in range(12):
                if 2 <= ch < 6:
                    bank, stage, k = ada_sums(ch - 2)
                    pool.wait_ge(done[bank], prior(bank, stage, k) + 1)
                elif ch >= 6:
                    pool.wait_ge(ada_used, ch - 5)
                pool.dma_start(ada[:, ch % 2], w_ada_v[:, :, ch * 512:(ch + 1) * 512]).then_inc(ada_in[ch % 2], 16)

            pool.wait_ge(rel_out, 1)
            pool.dma_start(rel_rows, rel_row.unsqueeze(1).broadcast_to([AH, P, RMAX])).then_inc(rel_back, 16)

            def gather(slots, table, sems, used, s, u):
                for k in range(TOPK):
                    pool.wait_ge(used, u * TOPK + (k + 1))
                    pool.sem_inc(issued, 1)
                    pool.indirect_dma_start(slots[k % len(slots)], None, table,
                                            bass.IndirectOffsetOnAxis(ap=expert[:, s, k:k + 1], axis=0))\
                        .then_inc(sems[k % len(slots)], 16)

            with pool.Fori(0, NU // 2) as i:
                for s in range(2):
                    u = i * 2 + s
                    pool.wait_ge(idx_ready, u + 1)
                    gather([u_ring[:, n, :] for n in range(8)], A["peer_u"][0], u_in, u_used, s, u)
                    gather(v_ring, A["peer_v"][0], v_in, v_used, s, u)
            pool.wait_ge(done["T0"], prior("T0", "back", 2))
            pool.wait_ge(done["T1"], prior("T1", "back", 2))
            pool.wait_ge(rel_back, 16)
            pool.dma_start(rel.rearrange("p (h k) -> p h k", k=T),
                           bass.AP(rel_rows.tensor, P - 1, [[RMAX - 1, P], [P * RMAX, AH], [1, T]])).then_inc(layer2_in, 16)
            pool.dma_start(bs_rows, A["b_sgu_spatial_2"][0].rearrange("g t -> (g t)").partition_broadcast(P))\
                .then_inc(layer2_in, 16)
            pool.dma_start(ln_g, A["ln_v_g_2"][0].partition_broadcast(P)).then_inc(layer2_in, 16)
            pool.dma_start(ln_b, A["ln_v_b_2"][0].partition_broadcast(P)).then_inc(layer2_in, 16)

        @block.tensor
        def _(pe):
            mm = nc.tensor.matmul

            def claim(bank, stage, k, i=0):
                n = prior(bank, stage, k, i)
                if not isinstance(n, int) or n > 0:
                    pe.wait_ge(free[bank], n)

            def norm(n):
                claim("SA", f"norm{n}", 0)
                for c in range(KC):
                    pe.wait_ge(sq_ready, KC * (n - 1) + c + 1)
                    m = mm(ps["SA"][:, 0:T], ones[:, :], tmp[:, c, :], start=c == 0, stop=c == KC - 1)
                m.then_inc(done["SA"], 1)

            def block_t(stage, t, k, i, src=None, chunks=(0, KC), fresh=None):
                bank = f"M{k % 2}"
                claim(bank, stage, k // 2, i)
                pe.wait_ge(tile_in[t], tile_ready(stage, t, i))
                lo, hi = chunks
                for c in range(lo, hi):
                    if fresh is not None:
                        pe.wait_ge(fresh[0], fresh[1] + c + 1)
                    rhs = hT[:, c, :] if src is None else src(c)
                    m = mm(ps[bank][:, 0:T], ring[:, t, c, :], rhs, start=c == lo, stop=c == hi - 1)
                m.then_inc(done[bank], 1)

            def block_r(stage, t, k, i, fresh=None):
                bank = f"M{k % 2}"
                claim(bank, stage, k // 2, i)
                pe.wait_ge(tile_in[t], tile_ready(stage, t, i))
                for tt in range(TT):
                    for c in range(KC):
                        if fresh is not None and tt == 0:
                            pe.wait_ge(fresh[0], fresh[1] + c + 1)
                        m = mm(ps[bank][:, tt * P:(tt + 1) * P], hT[:, c, tt * P:(tt + 1) * P], ring[:, t, c, :],
                               start=c == 0, stop=c == KC - 1)
                m.then_inc(done[bank], 1)

            def turn(stage, group, sources, width=P):
                bank = f"T{group % 2}"
                claim(bank, stage, group // 2)
                for n, src in enumerate(sources):
                    m = nc.tensor.transpose(ps[bank][:, n * P:n * P + width], src, ident[0:width, 0:width])
                m.then_inc(done[bank], 1)

            def ada_columns(ch):
                bank, stage, k = ada_sums(ch)
                claim(bank, stage, k)
                if ch < 4:
                    pe.wait_ge(ada_in[ch % 2], 16 * (ch // 2 + 1))
                    for c in range(KC):
                        mm(ps[bank][:, 0:1], ada[:, ch % 2, c, 0:P], silu_c[:, 1, c:c + 1],
                           start=c == 0, stop=c == KC - 1)
                pe.wait_ge(ada_ready, ch + 1)
                for b in range(1 if ch < 4 else 0, 4):
                    m = mm(ps[bank][:, b:b + 1], ada_sum[:, ch % 2, b * P:(b + 1) * P], ones[:, 0:1],
                           start=True, stop=True)
                m.then_inc(done[bank], 1)

            def extra(e):
                bank, k = ("SA", "S1")[e % 2], (4, 6)[e % 2] + e // 2
                if e < 4:
                    pe.wait_ge(key_in, 16)
                    sources = [key_rows[:, 4 * e + n, :] for n in range(4)]
                elif e < 6:
                    pe.wait_ge(sgu_in, 32)
                    sources = [sgu_rows[:, 4 * (e - 4) + n, :] for n in range(4)]
                elif e == 6:
                    pe.wait_ge(p_in, 16)
                    sources = [p_rows[:, tt, c * P:(c + 1) * P] for c in range(2) for tt in range(TT)]
                claim(bank, "stick", k)
                if e < 7:
                    for n, src in enumerate(sources):
                        m = nc.tensor.transpose(ps[bank][:, n * P:(n + 1) * P], src, ident[:, :])
                else:
                    pe.wait_ge(rel_in, 48)
                    m = mm(ps[bank][0:AH, 0:RMAX], rel_tab, rel_hot, start=True, stop=True)
                m.then_inc(done[bank], 1)

            pe.wait_ge(setup_done, 2)
            pe.wait_ge(ident_in, 16)
            pe.wait_ge(vec_in, 9 * 16)
            turn("init", 0, [vec_rows[:, :]], width=NVEC + 6 * KC)
            pe.wait_ge(x_in, 16)
            for g in range(4):
                turn("init", 1 + g, [x_rows[:, tt, c * P:(c + 1) * P] for c in (2 * g, 2 * g + 1) for tt in range(TT)])
            norm(1)
            pe.wait_ge(silu_ready, 1)
            for ch in range(4):
                ada_columns(ch)
            pe.wait_ge(const_in, 2 * 16)
            block_t("stick", 0, 0, 0, fresh=(h_ready, 0))
            block_t("stick", 1, 1, 0)
            for j in range(SB_PAIRS):
                pe.wait_ge(qkv_ready, 3 * j + 2)
                for h, bank in enumerate(("SA", "S0")):
                    r = slice(HD * h, HD * h + HD)
                    claim(bank, "stick", j)
                    mm(ps[bank][:, 0:T], ks[r, 0:P], qs[r, :], start=True, stop=True)
                    mm(ps[bank][:, T:384], ks[r, P:T], qs[r, P:T], start=True, stop=True).then_inc(done[bank], 1)
                block_r("stick", 3 * j + 2, 3 * j + 2, 0)
                if j > 0:
                    for k in (2 * j - 2, 2 * j - 1):
                        ada_columns(4 + k)
                if j == SB_PAIRS - 1:
                    for e in range(4):
                        extra(e)
                else:
                    block_t("stick", 3 * j + 3, 3 * j + 3, 0)
                for h in range(2):
                    bank = f"T{h}"
                    pe.wait_ge(stick_sp, 2 * j + h + 1)
                    claim(bank, "stick", j)
                    mm(ps[bank][:, 0:384], tri, sp[:, h, :], start=True, stop=False)
                    mm(ps[bank][:, P:T], ones[:, :], sp[:, h, T:384], start=False, stop=True).then_inc(done[bank], 1)
                if j == SB_PAIRS - 1:
                    for e in range(4, 8):
                        extra(e)
                else:
                    block_t("stick", 3 * j + 4, 3 * j + 4, 0)
                pe.wait_ge(qkv_ready, 3 * j + 3)
                claim("OT", "stick", j)
                for h in range(2):
                    r = slice(HD * h, HD * h + HD)
                    pe.wait_ge(stick_p, 2 * j + h + 1)
                    mm(ps["OT"][r, 0:T], vs[:, 0, r], ez[:, h, 0:T], start=True, stop=False)
                    m = mm(ps["OT"][r, P:T], vs[:, 1, r], ez[:, h, T:384], start=False, stop=True)
                m.then_inc(done["OT"], 1)

            pe.wait_ge(free["S1"], prior("S1", "stick", 10))
            pe.wait_ge(const2_in, 5 * 16)

            with pe.Fori(0, DIL_HP) as i:
                def rotate(g):
                    for s in range(2):
                        bank = f"T{s}"
                        pe.wait_ge(qkv_ready, i * 9 + (12 + 2 * g + s + 1))
                        claim(bank, "dilated", g, i)
                        mm(ps[bank][:, 0:T], rot, raw[:, g, s, :], start=True, stop=True).then_inc(done[bank], 1)

                for t, (s, g) in enumerate(DIL_ORDER[:6]):
                    block_t("dilated", t, t, i)
                    if s == 1 and g > 0:
                        rotate(g - 1)
                rotate(DIL_G - 1)
                block_r("dilated", 6, 6, i)
                pe.wait_ge(roped_ready, i * 3 + 3)
                for h in range(2):
                    r = slice(HD * h, HD * h + HD)
                    claim("SA", "dilated", h, i)
                    for g in range(DIL_G):
                        m = mm(ps["SA"][:, g * P:(g + 1) * P], roped[r, g, 0, 0:P], roped[r, g, 1, 0:P],
                               start=True, stop=True)
                    m.then_inc(done["SA"], 1)
                    claim("S0", "dilated", h, i)
                    for g in range(DIL_G):
                        m = mm(wide[:, g * T:(g + 1) * T], roped[r, g, 0, P:T], roped[r, g, 1, :],
                               start=True, stop=True)
                    m.then_inc(done["S0"], 1)
                for t in (7, 8):
                    block_r("dilated", t, t, i)
                pe.wait_ge(qkv_ready, i * 9 + 21)
                claim("OT", "dilated", 0, i)
                for h in range(2):
                    r = slice(HD * h, HD * h + HD)
                    pe.wait_ge(soft_p, i * 4 + (2 * h + 2))
                    for g in range(DIL_G):
                        bank = f"T{g % 2}"
                        claim(bank, "dilated", 3 + 2 * h + g // 2 if g % 2 == 0 else 3 + h, i)
                        at = DIL_G * P + g * T
                        for n, lo in enumerate((g * P, at, at + P)):
                            m = nc.tensor.transpose(ps[bank][:, n * P:(n + 1) * P], sd[:, h, lo:lo + P], ident[:, :])
                        m.then_inc(done[bank], 1)
                    pe.wait_ge(pt_ready, i * 6 + (3 * h + 3))
                    for g in range(DIL_G):
                        mm(ps["OT"][r, 0:T], vd[:, g, 0, r], pt[:, h, g, 0:T], start=g == 0, stop=False)
                        m = mm(ps["OT"][r, P:T], vd[:, g, 1, r], pt[:, h, g, T:384], start=False, stop=g == 2)
                m.then_inc(done["OT"], 1)

            pe.wait_ge(free["S0"], prior("S0", "dilated", 0, DIL_HP))
            for k in range(2):
                ada_columns(10 + k)
            with pe.Fori(0, 2) as i:
                for j in range(4):
                    block_t("gates", 3 * j, 4 * j, i)
                    block_t("gates", 3 * j + 1, 4 * j + 1, i)
                    if j == 0:
                        pe.wait_ge(free["OT"], prior("OT", "dilated", 1, DIL_HP - 1))
                    block_t("gates", 3 * j + 2, 4 * j + 2, i, lambda c: osb[:, c, :], (0, 4))
                    block_t("gates", 3 * j + 2, 4 * j + 3, i, lambda c: odl[:, c - 4, :], (4, 6))
            for t in range(KC):
                block_t("out1", t, t, 0, lambda c: merged[:, c, :], fresh=(merged_ready, 0) if t == 0 else None)

            norm(2)
            def scores(h):
                bank = ("SA", "OT")[h % 2]
                for half in range(2):
                    pe.wait_ge(free[f"M{half}"], prior(f"M{half}", "query", h) + 1)
                claim(bank, "sub", h // 2)
                for tt in range(TT):
                    for half in range(2):
                        n = 2 * tt + half
                        m = mm(ps[bank][:, n * P:(n + 1) * P], qT[:, 2 * (h % 2) + half, tt * P:(tt + 1) * P],
                               keysT[:, 2 * h + half, :], start=True, stop=True)
                m.then_inc(done[bank], 1)

            pe.sem_inc(v_used, VR - 6)
            for k in range(2 * NH):
                stage, t = query_block(k)
                block_t(stage, t, t, 0, fresh=(h_ready, KC) if k == 0 else None)
                if k == RING - 1:
                    pe.wait_ge(done["M1"], prior("M1", "query2", 0))
                    pe.sem_inc(v_used, 4)
                if k == 1 or k >= 4 and k % 2 == 0:
                    scores(max(k // 2 - 1, 0))
                if k == 4:
                    for g in range(4):
                        turn("rows", g, [hT[:, 4 * (g % 2) + n, (g // 2) * P:(g // 2 + 1) * P] for n in range(4)])
            scores(NH - 1)

            for b in ("T0", "T1"):
                pe.wait_ge(free[b], prior(b, "back", 0))
            pe.sem_inc(v_used, 2)

            def expert_pair(i, first=False, last=False):
                for s in range(TT):
                    u = i * TT + s
                    acc = wide if s == 0 else twin
                    for k in range(TOPK):
                        pe.wait_ge(diag_ready, u * TOPK + (k + 1))
                        pe.wait_ge(v_in[k], (u + 1) * 16)
                        for lo in (0, 512):
                            m = mm(acc[:, lo:lo + 512], dg[:, k % 8, :], v_ring[k][:, lo:lo + 512],
                                   start=first and k == 0, stop=last and k == TOPK - 1)
                        m.then_inc(v_used, 1)

            expert_pair(0, first=True)
            with pe.Fori(1, NH - 1) as i:
                expert_pair(i)
            expert_pair(NH - 1, last=True)
            pe.wait_ge(y_ready, 3)
            for g in range(4):
                turn("back", g, [y_rows[:, tt * D + c * P:tt * D + (c + 1) * P]
                                 for c in (2 * g, 2 * g + 1) for tt in range(TT)])
            norm(3)
            norm(4)

            for t in range(8):
                block_r("sgu_v", t, t, 0, fresh=(h_ready, 2 * KC) if t == 0 else None)
            with pe.Fori(0, 4) as i:
                for j in range(2):
                    k0 = 6 * j
                    block_t("mix", k0, k0, i)
                    block_t("mix", k0 + 1, k0 + 1, i)
                    pe.wait_ge(qkv_ready, i * 6 + (30 + 3 * j + 2))
                    for h, bank in enumerate(("SA", "S0")):
                        r = slice(HD * h, HD * h + HD)
                        claim(bank, "mix", j, i)
                        mm(ps[bank][:, 0:P], q2[r, 0:P], k2[r, 0:P], start=True, stop=True)
                        mm(ps[bank][:, P:384], q2[r, P:T], k2[r, :], start=True, stop=True).then_inc(done[bank], 1)
                    block_r("mix", k0 + 2, k0 + 2, i)
                    block_t("mix", k0 + 3, k0 + 3, i)
                    for h in range(2):
                        bank = f"T{h}"
                        pe.wait_ge(soft_p, i * 8 + (8 + 4 * j + 2 * h + 2))
                        claim(bank, "mix", j, i)
                        for n in range(3):
                            m = nc.tensor.transpose(ps[bank][:, n * P:(n + 1) * P], s2[:, h, n * P:(n + 1) * P],
                                                    ident[:, :])
                        m.then_inc(done[bank], 1)
                    block_t("mix", k0 + 4, k0 + 4, i)
                    pe.wait_ge(qkv_ready, i * 6 + (30 + 3 * j + 3))
                    claim("OT", "mix", j, i)
                    for h in range(2):
                        r = slice(HD * h, HD * h + HD)
                        pe.wait_ge(pt_ready, i * 4 + (12 + 2 * j + h + 1))
                        mm(ps["OT"][r, 0:T], v2[:, 0, r], p2[:, h, 0:T], start=True, stop=False)
                        m = mm(ps["OT"][r, P:T], v2[:, 1, r], p2[:, h, T:384], start=False, stop=True)
                    m.then_inc(done["OT"], 1)
                    pe.wait_ge(vst_ready, i * 2 + (j + 1))
                    claim("S1", "mix", j, i)
                    for tt in range(TT):
                        m = mm(ps["S1"][:, tt * P:(tt + 1) * P], vst[:, tt, :],
                               sguT[:, bass.ds(i * 2 + j, 1), :].rearrange("p a b -> p (a b)"), start=True, stop=True)
                    m.then_inc(done["S1"], 1)
                    block_t("mix", k0 + 5, k0 + 5, i)
            for t in range(KC):
                block_t("out2", t, t, 0, lambda c: merged[:, c, :], fresh=(merged_ready, KC) if t == 0 else None)
            norm(5)
            with pe.Fori(0, 4) as i:
                for t in range(8):
                    block_t("ff1", t, t, i, fresh=(h_ready, 3 * KC) if t == 0 else None)
            pe.wait_ge(ff_ready, DFF // P - KC + 2)
            with pe.Fori(0, 4) as i:
                for j in range(2):
                    bank = f"M{j}"
                    claim(bank, "ff2", 0, i)
                    for q in range(4):
                        pe.wait_ge(tile_in[4 * j + q], tile_ready("ff2", 4 * j + q, i))
                        for c in range(KC):
                            if j == 0 and q == 3:
                                pe.wait_ge(ff_ready, q * KC + c + 3)
                            m = mm(ps[bank][:, 0:T], ring[:, 4 * j + q, c, :], ffT[:, q * KC + c, :],
                                   start=q + c == 0, stop=q == 3 and c == KC - 1)
                    m.then_inc(done[bank], 1)
            norm(6)
            with pe.Fori(0, 2) as i:
                for j in range(4):
                    block_t("ple", 2 * j, 2 * j, i, fresh=(h_ready, 4 * KC) if j == 0 else None)
                    block_t("ple", 2 * j + 1, 2 * j + 1, i, lambda c: pT[:, c, :], (0, 2))
            norm(7)
            for g in range(4):
                pe.wait_ge(h_ready, 5 * KC + 4 * (g // 2 + 1))
                turn("final", g, [hT[:, 4 * (g // 2) + n, (g % 2) * P:(g % 2 + 1) * P] for n in range(4)])

        @block.scalar
        def _(act):
            st = Steps(act_step)
            F = nc.scalar.activation

            def take(bank, stage, k, i=0):
                act.wait_ge(done[bank], prior(bank, stage, k, i) + 1)

            def norm(n, updated):
                F(warm[:, n:n + 1], eps[:, :], ACT.Sqrt)
                for c in range(KC if updated is not None else 0):
                    act.wait_ge(*updated(c))
                    F(tmp[:, c, :], xT[:, c, :], ACT.Square).then_inc(sq_ready, 1)
                take("SA", f"norm{n}", 0)
                F(rt[:, :], ps["SA"][:, 0:T], ACT.Sqrt, bias=eps[:, :], scale=1.0 / D).then_inc(free["SA"], 1)

            def shifted(n, shift):
                for c in range(KC):
                    act.wait_ge(scaled, KC * n + c + 1)
                    F(hT[:, c, :], tmp[:, c, :], ACT.Identity, bias=shift[:, c:c + 1]).then_inc(h_ready, 1)

            def read(bank, stage, k, i=0):
                return free[bank], prior(bank, stage, k, i) + 1

            load_vectors(act, 4, len(names))
            take("T0", "init", 0)
            F(vecT[:, :], ps["T0"][:, 0:NVEC + 6 * KC], ACT.Copy).then_inc(free["T0"], 1)
            act.wait_ge(free["T0"], 1)
            F(silu_c[:, 0, :], col["c"], ACT.Tanh, scale=0.5).then_inc(silu_half, 1)
            for g in range(4):
                bank = f"T{(1 + g) % 2}"
                take(bank, "init", (1 + g) // 2)
                F(xT[:, 2 * g:2 * g + 2, :].rearrange("p c t -> p (c t)"), ps[bank], ACT.Copy).then_inc(free[bank], 1)
            act.wait_ge(setup_done, 2)
            norm(1, lambda c: read(f"T{(1 + c // 2) % 2}", "init", (1 + c // 2) // 2))
            act.wait_ge(mod_ready, 4)
            shifted(0, mod[0])
            def stick_copy(k, dst):
                b = f"M{k % 2}"
                take(b, "stick", k // 2)
                F(dst, ps[b][:, 0:T], ACT.Copy).then_inc(free[b], 1)
                act.wait_ge(free[b], prior(b, "stick", k // 2) + 1)
                act.sem_inc(qkv_ready, 1)

            stick_copy(0, qs)
            stick_copy(1, ks)
            for j in range(SB_PAIRS):
                for h, bank in enumerate(("SA", "S0")):
                    act.wait_ge(free[bank], prior(bank, "stick", j) + 1)
                    F(ez[:, h, :], zm[:, h, :], ACT.Abs).then_inc(st.tick(), 1)
                for h in range(2):
                    act.wait_ge(st.sem, 4 * j + 1 + h)
                    F(ez[:, h, :], ez[:, h, :], ACT.Exp, scale=-1.0).then_inc(st.tick(), 1)
                for h in range(2):
                    act.wait_ge(st.sem, 4 * j + 3 + h)
                    F(ez[:, h, :], ez[:, h, :], ACT.Ln, bias=ones[:, 0:1]).then_inc(stick_ln, 1)
                if j == SB_PAIRS - 1:
                    for e in range(4):
                        bank, k = ("SA", "S1")[e % 2], (4, 6)[e % 2] + e // 2
                        take(bank, "stick", k)
                        F(keysT[:, 4 * e:4 * e + 4, :].rearrange("p a b -> p (a b)"), ps[bank], ACT.Copy)\
                            .then_inc(free[bank], 1)
                stick_copy(3 * j + 2, vs.rearrange("p t n -> p (t n)"))
                if j < SB_PAIRS - 1:
                    stick_copy(3 * j + 3, qs)
                for h in range(2):
                    act.wait_ge(free[f"T{h}"], prior(f"T{h}", "stick", j) + 1)
                    F(ez[:, h, :], zm[:, h, :], ACT.Exp).then_inc(stick_p, 1)
                if j < SB_PAIRS - 1:
                    stick_copy(3 * j + 4, ks)
                if j == SB_PAIRS - 1:
                    take("SA", "stick", 7)
                    F(pT[:, :, :].rearrange("p c t -> p (c t)"), ps["SA"], ACT.Copy).then_inc(free["SA"], 1)
                take("OT", "stick", j)
                F(osb[:, j, :], ps["OT"][:, 0:T], ACT.Copy).then_inc(free["OT"], 1)

            def soft_exp_of(buf, lo, hi, h, part, mx, sm, value):
                act.wait_ge(soft_max, value)
                F(buf[:, h, lo:hi], buf[:, h, lo:hi], ACT.Exp, bias=mx[:, h, part:part + 1],
                  accum_out=sm[:, h, part:part + 1]).then_inc(soft_exp, 1)

            with act.Fori(0, DIL_HP) as i:
                for k, (s, g) in enumerate(DIL_ORDER):
                    if k == 7:
                        for h in range(2):
                            soft_exp_of(sd, 0, 384, h, 0, sm_max, sm_sum, i * 4 + (2 * h + 1))
                            soft_exp_of(sd, 384, 1152, h, 1, sm_max, sm_sum, i * 4 + (2 * h + 2))
                    dst = raw[:, g, s, :] if s < 2 else vd[:, g].rearrange("p t n -> p (t n)")
                    b = f"M{k % 2}"
                    take(b, "dilated", k // 2, i)
                    F(dst, ps[b][:, 0:T], ACT.Copy).then_inc(free[b], 1)
                    act.wait_ge(free[b], prior(b, "dilated", k // 2, i) + 1)
                    act.sem_inc(qkv_ready, 1)
                for h in range(2):
                    for g in range(DIL_G):
                        bank = f"T{g % 2}"
                        n = 3 + 2 * h + g // 2 if g % 2 == 0 else 3 + h
                        take(bank, "dilated", n, i)
                        F(pt[:, h, g, :], ps[bank][:, 0:384], ACT.Copy).then_inc(free[bank], 1)
                        act.wait_ge(free[bank], prior(bank, "dilated", n, i) + 1)
                        act.sem_inc(pt_ready, 1)
                take("OT", "dilated", 0, i)
                F(odl[:, bass.ds(i, 1), :].rearrange("p a t -> p (a t)"), ps["OT"][:, 0:T], ACT.Copy)\
                    .then_inc(free["OT"], 1)

            with act.Fori(0, 2) as i:
                for j in range(4):
                    for s, dst in enumerate((gate_a, gate_b)):
                        take(f"M{s}", "gates", 2 * j, i)
                        F(dst, ps[f"M{s}"][:, 0:T], ACT.Tanh, scale=0.5).then_inc(free[f"M{s}"], 1)

            act.wait_ge(rel_back, 16)
            norm(2, lambda c: read(f"M{c % 2}", "out1", c // 2))
            act.wait_ge(mod_ready, 12)
            shifted(1, mod[3])
            def scores(h):
                bank = ("SA", "OT")[h % 2]
                take(bank, "sub", h // 2)
                F(sub[:, h * 512:(h + 1) * 512], ps[bank], ACT.Copy).then_inc(free[bank], 1)
                act.wait_ge(free[bank], prior(bank, "sub", h // 2) + 1)
                act.sem_inc(sub_ready, 1)

            for k in range(2 * NH):
                b = f"M{k % 2}"
                take(b, "query", k // 2)
                F(qT[:, k % 4, :], ps[b][:, 0:T], ACT.Copy).then_inc(free[b], 1)
                if k == 1 or k >= 4 and k % 2 == 0:
                    scores(max(k // 2 - 1, 0))
                if k == 4:
                    for g in range(4):
                        bank = f"T{g % 2}"
                        take(bank, "rows", g // 2)
                        F(h_rows[:, g // 2, (g % 2) * 512:(g % 2 + 1) * 512], ps[bank], ACT.Copy).then_inc(free[bank], 1)
            scores(NH - 1)

            with act.Fori(0, NU // 2) as i:
                for s in range(2):
                    u = i * 2 + s
                    act.wait_ge(best_ready, u + 1)
                    F(gate_w[:, s, :], best_2[:, s, :], ACT.Exp, bias=gate_n[:, s, :], accum_out=gate_s[:, s, :])\
                        .then_inc(gate_exp, 1)
                    act.wait_ge(act_arg, u + 1)
                    F(act_t[:, s, :], act_b[:, s, :], ACT.Tanh, scale=GELU_C).then_inc(act_tanh, 1)
                    act.wait_ge(wgt_ready, u + 1)
                    for k in range(TOPK):
                        act.wait_ge(v_used, u * TOPK + (k + 1 + VR - 8))
                        F(dg[:, k % 8, :], ident[:, :], ACT.Copy, scale=wgt[:, s, k:k + 1]).then_inc(diag_ready, 1)

            act.wait_ge(v_used, VR + TOPK * (NU - 1))
            F(y_rows[:, 0:D], wide[:, :], ACT.Copy).then_inc(y_ready, 1)
            act.wait_ge(v_used, VR + TOPK * NU)
            F(y_rows[:, D:D + 512], ps["T0"], ACT.Copy).then_inc(y_ready, 1)
            norm(3, lambda c: read(f"T{c // 2 % 2}", "back", c // 4))
            norm(4, lambda c: (x_ready, c + 1))

            def zv_tanh_of(t):
                act.wait_ge(zv_arg, t + 1)
                F(g_th[:, t % 2, :], g_sq[:, t % 2, :], ACT.Tanh, scale=GELU_C).then_inc(zv_tanh, 1)

            for t in range(8):
                b = f"M{t % 2}"
                take(b, "sgu_v", t // 2)
                if t > 1:
                    act.wait_ge(zv_ready, t - 1)
                F(g_raw[:, t % 2, :], ps[b][:, 0:T], ACT.Copy).then_inc(free[b], 1)
                act.wait_ge(free[b], prior(b, "sgu_v", t // 2) + 1)
                F(g_sq[:, t % 2, :], g_raw[:, t % 2, :], ACT.Square).then_inc(zv_raw, 1)
                if t > 0:
                    zv_tanh_of(t - 1)
            zv_tanh_of(7)
            for tt in range(TT):
                act.wait_ge(ln_c, 1)
                F(zsq[:, tt, :], zv[:, tt, :], ACT.Square, bias=ln_m[:, tt:tt + 1], accum_out=ln_q[:, tt:tt + 1])\
                    .then_inc(ln_sq, 1)
            act.wait_ge(ln_sq, TT)
            F(ln_r, ln_q, ACT.Sqrt, bias=eps[:, :], scale=1.0 / D).then_inc(ln_root, 1)

            with act.Fori(0, 4) as i:
                for j in range(2):
                    k0 = 6 * j

                    def copy(k, dst):
                        b = f"M{k % 2}"
                        take(b, "mix", k // 2, i)
                        F(dst, ps[b][:, 0:T], ACT.Copy).then_inc(free[b], 1)
                        act.wait_ge(free[b], prior(b, "mix", k // 2, i) + 1)

                    copy(k0, q2)
                    act.sem_inc(qkv_ready, 1)
                    copy(k0 + 1, k2)
                    act.sem_inc(qkv_ready, 1)
                    for h in range(2):
                        soft_exp_of(s2, 0, P, h, 0, mx2, sm2, i * 8 + (8 + 4 * j + 2 * h + 1))
                        soft_exp_of(s2, P, 384, h, 1, mx2, sm2, i * 8 + (8 + 4 * j + 2 * h + 2))
                    copy(k0 + 2, v2.rearrange("p t n -> p (t n)"))
                    act.sem_inc(qkv_ready, 1)
                    act.wait_ge(merged_ready, i * 2 + (KC + j))
                    copy(k0 + 3, g_raw[:, 0, :])
                    F(g_sq[:, 0, :], g_raw[:, 0, :], ACT.Square).then_inc(u_raw, 1)
                    for h in range(2):
                        take(f"T{h}", "mix", j, i)
                        F(p2[:, h, :], ps[f"T{h}"][:, 0:384], ACT.Copy).then_inc(free[f"T{h}"], 1)
                        act.wait_ge(free[f"T{h}"], prior(f"T{h}", "mix", j, i) + 1)
                        act.sem_inc(pt_ready, 1)
                    act.wait_ge(u_arg, i * 2 + (j + 1))
                    F(g_th[:, 0, :], g_sq[:, 0, :], ACT.Tanh, scale=GELU_C).then_inc(u_tanh, 1)
                    for s, dst in enumerate((ga, gb)):
                        b = f"M{s}"
                        take(b, "mix", (k0 + 4 + s) // 2, i)
                        F(dst, ps[b][:, 0:T], ACT.Tanh, scale=0.5).then_inc(free[b], 1)

            norm(5, lambda c: read(f"M{c % 2}", "out2", c // 2))
            with act.Fori(0, 4) as i:
                for t in range(8):
                    b = f"M{t % 2}"
                    take(b, "ff1", t // 2, i)
                    act.wait_ge(ff_ready, i * 8 + (t + 1))
                    F(relu[:, t % 2, :], ps[b][:, 0:T], ACT.Relu).then_inc(free[b], 1)
            norm(6, lambda c: read(f"M{c % 2}", "ff2", 0, c // 2))
            with act.Fori(0, 2) as i:
                for j in range(4):
                    take("M0", "ple", j, i)
                    act.wait_ge(free["M1"], prior("M1", "ple", j, i))
                    F(gate_p[:, 0, :], ps["M0"][:, 0:T], ACT.Tanh, scale=0.5).then_inc(free["M0"], 1)
                    act.wait_ge(x_ready, i * 4 + (KC + j + 1))
                    F(tmp[:, bass.ds(i * 4 + j, 1), :], xT[:, bass.ds(i * 4 + j, 1), :], ACT.Square).then_inc(sq_ready, 1)
            norm(7, None)
            for g in range(2):
                take("T0", "final", g)
                F(o_rows[:, 0, g * 512:(g + 1) * 512], ps["T0"], ACT.Copy).then_inc(free["T0"], 1)

        @block.vector
        def _(dve):
            st = Steps(dve_step)
            V = nc.vector

            def take(bank, stage, k, i=0):
                dve.wait_ge(done[bank], prior(bank, stage, k, i) + 1)

            def own():
                dve.wait_ge(st.sem, st.now())

            def inverse_root(n):
                dve.wait_ge(free["SA"], prior("SA", f"norm{n}", 0) + 1)
                V.reciprocal(rstd[:, :], rt[:, :]).then_inc(st.tick(), 1)
                own()

            def norm(n, gains, dst, signal):
                if n > 1:
                    inverse_root(n)
                for c in range(KC):
                    V.scalar_tensor_tensor(dst[:, c, :], xT[:, c, :], gains[:, c:c + 1], rstd[:, :],
                                           ALU.mult, ALU.mult).then_inc(signal, 1)

            def ada_chunk(ch):
                a = ada_sum[:, ch % 2, :]
                lo = P if ch < 4 else 0
                a = a[:, lo:]
                dve.wait_ge(ada_in[ch % 2], 16 * (ch // 2 + 1))
                if ch >= 2:
                    dve.wait_ge(mod_ready, ch - 1)
                for c in range(KC):
                    w = ada[:, ch % 2, c, lo:]
                    if c == 0:
                        m = V.tensor_scalar(a, w, silu_c[:, 1, 0:1], None, ALU.mult)
                    else:
                        own()
                        m = V.scalar_tensor_tensor(a, w, silu_c[:, 1, c:c + 1], a, ALU.mult, ALU.add)
                    if c < KC - 1:
                        m.then_inc(st.tick(), 1)
                m.then_inc(ada_ready, 1)
                if ch >= 4:
                    dve.wait_ge(ada_ready, ch + 1)
                    dve.sem_inc(ada_used, 1)

            def ada_bias(ch):
                bank, stage, k = ada_sums(ch)
                take(bank, stage, k)
                V.tensor_tensor(modT[:, 4 * ch:4 * ch + 4], ps[bank][:, 0:4], b_ada_col[:, 4 * ch:4 * ch + 4], ALU.add)\
                    .then_inc(free[bank], 1)
                dve.wait_ge(free[bank], prior(bank, stage, k) + 1)
                dve.sem_inc(mod_ready, 1)

            dve.wait_ge(silu_half, 1)
            V.tensor_scalar(silu_c[:, 0, :], silu_c[:, 0, :], 0.5, 0.5, ALU.mult, ALU.add).then_inc(st.tick(), 1)
            own()
            V.tensor_tensor(silu_c[:, 1, :], silu_c[:, 0, :], col["c"], ALU.mult).then_inc(silu_ready, 1)
            dve.wait_ge(silu_ready, 1)
            ada_chunk(0)
            for ch in range(4):
                if ch < 3:
                    ada_chunk(ch + 1)
                ada_bias(ch)
                if ch == 1:
                    inverse_root(1)
            V.scalar_tensor_tensor(gain[:, 0, :], mod[1], 1.0, col["g_mix"], ALU.add, ALU.mult).then_inc(st.tick(), 1)
            own()
            norm(1, gain[:, 0, :], tmp, scaled)
            dve.wait_ge(const_in, 2 * 16)
            for j in range(SB_PAIRS):
                for h, bank in enumerate(("SA", "S0")):
                    take(bank, "stick", j)
                    V.scalar_tensor_tensor(zm[:, h, :], ps[bank][:, 0:384], SCALE, stick_neg, ALU.mult, ALU.add)\
                        .then_inc(free[bank], 1)
                if j > 0:
                    for k in (2 * j - 2, 2 * j - 1):
                        ada_bias(4 + k)
                if j < SB_PAIRS - 1:
                    ada_chunk(4 + 2 * j)
                for h in range(2):
                    dve.wait_ge(stick_ln, 2 * j + h + 1)
                    V.scalar_tensor_tensor(sp[:, h, :], zm[:, h, :], 0.0, ez[:, h, :], ALU.max, ALU.add)\
                        .then_inc(stick_sp, 1)
                for h in range(2):
                    take(f"T{h}", "stick", j)
                    V.tensor_tensor(zm[:, h, :], zm[:, h, :], ps[f"T{h}"][:, 0:384], ALU.subtract)\
                        .then_inc(free[f"T{h}"], 1)
                if j < SB_PAIRS - 1:
                    ada_chunk(5 + 2 * j)

            for e in (4, 5):
                bank, k = ("SA", "S1")[e % 2], (4, 6)[e % 2] + e // 2
                take(bank, "stick", k)
                V.tensor_tensor(sguT[:, 4 * (e - 4):4 * (e - 3), :], ps[bank].rearrange("p (a b) -> p a b", b=P),
                                sgu_mask.unsqueeze(1).broadcast_to([P, 4, P]), ALU.mult).then_inc(free[bank], 1)
            take("S1", "stick", 9)
            V.tensor_tensor(rel_row, ps["S1"][0:AH, 0:RMAX], rel_neg, ALU.add).then_inc(free["S1"], 1)
            dve.wait_ge(free["S1"], prior("S1", "stick", 9) + 1)
            dve.sem_inc(rel_out, 1)
            for ch in (10, 11):
                ada_chunk(ch)
            dve.wait_ge(const2_in, 5 * 16)

            def soft_norm(buf, splits, h, sm, iv, value):
                dve.wait_ge(soft_exp, value)
                V.reciprocal(iv[:, h, :], sm[:, h, :]).then_inc(st.tick(), 1)
                own()
                for part, (lo, hi) in enumerate(splits):
                    V.tensor_scalar(buf[:, h, lo:hi], buf[:, h, lo:hi], iv[:, h, part:part + 1], None, ALU.mult)\
                        .then_inc(soft_p, 1)

            with dve.Fori(0, DIL_HP) as i:
                st.enter(i, 8)
                for g in range(DIL_G):
                    if g > 0:
                        dve.wait_ge(roped_ready, i * DIL_G + g)
                    for s in range(2):
                        take(f"T{s}", "dilated", g, i)
                        V.tensor_tensor(rope_b[:, s, :], ps[f"T{s}"][:, 0:T], sinT, ALU.mult).then_inc(free[f"T{s}"], 1)
                        V.tensor_tensor(rope_a[:, s, :], raw[:, g, s, :], cosT, ALU.mult).then_inc(st.tick(), 1)
                    own()
                    dve.wait_ge(free["T1"], prior("T1", "dilated", g, i) + 1)
                    V.tensor_tensor(roped[:, g], rope_a, rope_b, ALU.add).then_inc(roped_ready, 1)
                for h in range(2):
                    take("SA", "dilated", h, i)
                    V.scalar_tensor_tensor(sd[:, h, 0:384], ps["SA"][:, 0:384], SCALE, dil_neg[:, 0:384],
                                           ALU.mult, ALU.add).then_inc(free["SA"], 1)
                    take("S0", "dilated", h, i)
                    V.scalar_tensor_tensor(sd[:, h, 384:1152], wide[:, 0:768], SCALE, dil_neg[:, 384:1152],
                                           ALU.mult, ALU.add).then_inc(free["S0"], 1)
                    dve.wait_ge(free["S0"], prior("S0", "dilated", h, i) + 1)
                    V.tensor_reduce(sm_max[:, h, 0:1], sd[:, h, 0:384], AX.X, ALU.max, negate=True).then_inc(soft_max, 1)
                    V.tensor_reduce(sm_max[:, h, 1:2], sd[:, h, 384:1152], AX.X, ALU.max, negate=True)\
                        .then_inc(soft_max, 1)
                for h in range(2):
                    soft_norm(sd, ((0, 384), (384, 1152)), h, sm_sum, sm_inv, i * 4 + (2 * h + 2))
                st.leave(DIL_HP)

            for k in range(2):
                ada_bias(10 + k)
            V.scalar_tensor_tensor(gain[:, 1, :], mod[4], 1.0, col["g_ffn"], ALU.add, ALU.mult).then_inc(st.tick(), 1)
            with dve.Fori(0, 2) as i:
                st.enter(i, 8)
                for j in range(4):
                    for s, (g, br) in enumerate(((gate_a, br_a), (gate_b, br_b))):
                        dve.wait_ge(free[f"M{s}"], prior(f"M{s}", "gates", 2 * j, i) + 1)
                        V.tensor_scalar(g, g, 0.5, 0.5, ALU.mult, ALU.add).then_inc(st.tick(), 1)
                        take(f"M{s}", "gates", 2 * j + 1, i)
                        own()
                        V.tensor_tensor(br, g, ps[f"M{s}"][:, 0:T], ALU.mult).then_inc(free[f"M{s}"], 1)
                    for s in range(2):
                        dve.wait_ge(free[f"M{s}"], prior(f"M{s}", "gates", 2 * j + 1, i) + 1)
                    V.tensor_tensor(merged[:, bass.ds(i * 4 + j, 1), :].rearrange("p a t -> p (a t)"), br_a, br_b, ALU.add)\
                        .then_inc(merged_ready, 1)
                st.leave(2)
            for t in range(KC):
                b = f"M{t % 2}"
                take(b, "out1", t // 2)
                V.scalar_tensor_tensor(xT[:, t, :], ps[b][:, 0:T], mod[2][:, t:t + 1], xT[:, t, :], ALU.mult, ALU.add)\
                    .then_inc(free[b], 1)
            for b in ("M0", "M1"):
                dve.wait_ge(free[b], prior(b, "out1", 4))
            norm(2, gain[:, 1, :], tmp, scaled)

            def top16(vals, idx, src, work):
                own()
                dve.sem_inc(route_step, 1)
                V.max(vals[:, 0:8], src).then_inc(st.tick(), 1)
                own()
                dve.sem_inc(route_step, 1)
                V.max_index(idx[:, 0:8], vals[:, 0:8], src).then_inc(st.tick(), 1)
                V.match_replace(work, vals[:, 0:8], src, LOWEST).then_inc(st.tick(), 1)
                own()
                dve.sem_inc(route_step, 1)
                V.max(vals[:, 8:16], work).then_inc(st.tick(), 1)
                own()
                dve.sem_inc(route_step, 1)
                V.max_index(idx[:, 8:16], vals[:, 8:16], work).then_inc(st.tick(), 1)

            def route(u, s):
                V.tensor_copy(sub_w.rearrange("p a b -> p (a b)"), sub[:, bass.ds(u * (2 * NK), 2 * NK)])\
                    .then_inc(st.tick(), 1)
                for half in range(2):
                    top16(s16[:, half, :], i16[:, half, :], sub_w[:, half, :], cand_w[:, half * NK:(half + 1) * NK])
                own()
                V.tensor_copy(i16f, i16).then_inc(st.tick(), 1)
                V.tensor_tensor(cand, s16[:, 0, :].unsqueeze(2).broadcast_to([P, TOPK, TOPK]),
                                s16[:, 1, :].unsqueeze(1).broadcast_to([P, TOPK, TOPK]), ALU.add).then_inc(st.tick(), 1)
                best = best_2[:, s, :]
                top16(best, pos, cand.rearrange("p a b -> p (a b)"), cand_w)
                own()
                V.tensor_scalar(gate_n[:, s, :], best[:, 0:1], -1.0, None, ALU.mult).then_inc(best_ready, 1)
                V.tensor_scalar(pos_ab[:, 0, :], pos, 4, None, ALU.logical_shift_right).then_inc(st.tick(), 1)
                V.tensor_scalar(pos_ab[:, 1, :], pos, 15, None, ALU.bitwise_and).then_inc(st.tick(), 1)
                own()
                V.tensor_copy(pos_f, pos_ab).then_inc(st.tick(), 1)
                own()
                V.tensor_tensor(hot, pos_f.rearrange("p a k -> p (a k)").unsqueeze(2).broadcast_to([P, 2 * TOPK, TOPK]),
                                iota.unsqueeze(1).broadcast_to([P, 2 * TOPK, TOPK]), ALU.is_equal).then_inc(st.tick(), 1)
                own()
                for half in range(2):
                    part = hot[:, half * TOPK:(half + 1) * TOPK, :]
                    V.tensor_tensor(part, part, i16f[:, half, :].unsqueeze(1).broadcast_to([P, TOPK, TOPK]), ALU.mult)\
                        .then_inc(st.tick(), 1)
                own()
                V.tensor_reduce(pick.rearrange("p a k -> p (a k)"), hot, AX.X, ALU.add).then_inc(st.tick(), 1)
                own()
                V.scalar_tensor_tensor(expert_f, pick[:, 0, :], float(NK), pick[:, 1, :], ALU.mult, ALU.add)\
                    .then_inc(st.tick(), 1)
                own()
                V.tensor_copy(expert[:, s, :], expert_f).then_inc(idx_ready, 1)
            ROUTE_STEPS = 26

            def dots(u, s):
                for k in range(TOPK):
                    dve.wait_ge(u_in[k % 8], u * 32 + 16 * (k // 8 + 1))
                    if k >= 1 or not isinstance(u, int) or u > 0:
                        dve.wait_ge(u_used, u * TOPK + (k + 8))
                    V.scalar_tensor_tensor(dot_junk, u_ring[:, k % 8, :], 1.0, h_rows[:, s, :],
                                           ALU.mult, ALU.mult, accum_out=act_x[:, s, k:k + 1]).then_inc(u_used, 1)
                dve.wait_ge(u_used, u * TOPK + (TOPK + 8))
                x = act_x[:, s, :]
                V.tensor_tensor(act_a[:, s, :], x, x, ALU.mult).then_inc(st.tick(), 1)
                own()
                V.tensor_scalar(act_a[:, s, :], act_a[:, s, :], GELU_A, 1.0, ALU.mult, ALU.add).then_inc(st.tick(), 1)
                own()
                V.tensor_tensor(act_b[:, s, :], act_a[:, s, :], x, ALU.mult).then_inc(act_arg, 1)
                dve.wait_ge(gate_exp, u + 1)
                V.reciprocal(gate_r[:, s, :], gate_s[:, s, :]).then_inc(st.tick(), 1)
                own()
                V.tensor_scalar(gate_w[:, s, :], gate_w[:, s, :], gate_r[:, s, :], 0.5, ALU.mult, ALU.mult)\
                    .then_inc(st.tick(), 1)
                dve.wait_ge(act_tanh, u + 1)
                V.scalar_tensor_tensor(act_a[:, s, :], act_t[:, s, :], 1.0, x, ALU.add, ALU.mult).then_inc(st.tick(), 1)
                own()
                V.tensor_tensor(wgt[:, s, :], act_a[:, s, :], gate_w[:, s, :], ALU.mult).then_inc(wgt_ready, 1)

            DOT_STEPS = 5

            dve.wait_ge(sub_ready, 1)
            route(0, 0)
            dve.sem_inc(u_used, 8)
            for b in ("T0", "T1"):
                dve.wait_ge(free[b], prior(b, "back", 0))
            route(1, 1)
            dots(0, 0)

            def unit(u, s):
                dots(u, s)
                dve.wait_ge(v_used, u * TOPK + VR)
                route(u + 1, 1 - s)

            with dve.Fori(0, NU // 2 - 1) as i:
                st.enter(i, 2 * (ROUTE_STEPS + DOT_STEPS))
                dve.wait_ge(sub_ready, i + 2)
                unit(i * 2 + 1, 1)
                unit(i * 2 + 2, 0)
                st.leave(NU // 2 - 1)
            dots(NU - 1, 1)
            dve.wait_ge(v_used, VR + TOPK * NU)
            V.tensor_copy(y_rows[:, D + 512:2 * D], ps["T1"]).then_inc(y_ready, 1)
            for g in range(4):
                bank = f"T{g % 2}"
                take(bank, "back", g // 2)
                for n in range(2):
                    c = 2 * g + n
                    m = V.scalar_tensor_tensor(xT[:, c, :], ps[bank][:, n * T:(n + 1) * T], mod[5][:, c:c + 1], xT[:, c, :],
                                               ALU.mult, ALU.add)
                m.then_inc(free[bank], 1)
            for b in ("T0", "T1"):
                dve.wait_ge(free[b], prior(b, "back", 2))
            norm(3, col["g_final"], xT, x_ready)

            norm(4, col["norm_mix_g_2"], hT, h_ready)

            def gelu_arg(ready, value, signal, b):
                dve.wait_ge(ready, value)
                V.tensor_scalar(g_sq[:, b, :], g_sq[:, b, :], GELU_A, 1.0, ALU.mult, ALU.add).then_inc(st.tick(), 1)
                own()
                V.tensor_tensor(g_sq[:, b, :], g_sq[:, b, :], g_raw[:, b, :], ALU.mult).then_inc(signal, 1)

            def gelu_half(ready, value, b):
                dve.wait_ge(ready, value)
                V.tensor_scalar(g_th[:, b, :], g_th[:, b, :], 0.5, 0.5, ALU.mult, ALU.add).then_inc(st.tick(), 1)
                own()

            def zv_of(t):
                gelu_half(zv_tanh, t + 1, t % 2)
                for tt in range(TT):
                    m = V.scalar_tensor_tensor(zv[:, tt, t * P:(t + 1) * P], g_th[:, t % 2, tt * P:(tt + 1) * P], 1.0,
                                               g_raw[:, t % 2, tt * P:(tt + 1) * P], ALU.mult, ALU.mult,
                                               accum_out=ln_part[:, tt, t:t + 1])
                m.then_inc(zv_ready, 1)

            for t in range(8):
                gelu_arg(zv_raw, t + 1, zv_arg, t % 2)
                if t > 0:
                    zv_of(t - 1)
            zv_of(7)
            dve.wait_ge(zv_ready, 8)
            V.tensor_reduce(ln_s, ln_part, AX.X, ALU.add).then_inc(st.tick(), 1)
            own()
            V.tensor_scalar(ln_m, ln_s, -1.0 / D, None, ALU.mult).then_inc(ln_c, 1)
            dve.wait_ge(ln_c, 1)
            dve.wait_ge(layer2_in, 64)

            MIX_STEPS = 14
            with dve.Fori(0, 4) as i:
                st.enter(i, 2 * MIX_STEPS)
                for j in range(2):
                    jj = i * 2 + j
                    for h, bank in enumerate(("SA", "S0")):
                        take(bank, "mix", j, i)
                        V.scalar_tensor_tensor(s2[:, h, 0:P], ps[bank][:, 0:P], SCALE,
                                               rel[:, bass.ds(i * (4 * T) + ((2 * j + h) * T + P), P)], ALU.mult, ALU.add)\
                            .then_inc(st.tick(), 1)
                        V.scalar_tensor_tensor(s2[:, h, P:384], ps[bank][:, P:384], SCALE,
                                               rel[:, bass.ds(i * (4 * T) + (2 * j + h) * T, T)], ALU.mult, ALU.add)\
                            .then_inc(free[bank], 1)
                        dve.wait_ge(free[bank], prior(bank, "mix", j, i) + 1)
                        own()
                        V.tensor_reduce(mx2[:, h, 0:1], s2[:, h, 0:P], AX.X, ALU.max, negate=True).then_inc(soft_max, 1)
                        V.tensor_reduce(mx2[:, h, 1:2], s2[:, h, P:384], AX.X, ALU.max, negate=True).then_inc(soft_max, 1)
                    for h in range(2):
                        soft_norm(s2, ((0, P), (P, 384)), h, sm2, iv2, i * 8 + (8 + 4 * j + 2 * h + 2))
                    dve.wait_ge(ln_root, 1)
                    V.reciprocal(ln_i, ln_r).then_inc(st.tick(), 1)
                    own()
                    for tt in range(TT):
                        m = V.tensor_scalar(vst[:, tt, :], zv[:, tt, bass.ds(jj * P, P)], ln_m[:, tt:tt + 1],
                                            ln_i[:, tt:tt + 1], ALU.add, ALU.mult)
                    m.then_inc(st.tick(), 1)
                    own()
                    V.tensor_tensor(vst, vst, ln_g[:, bass.ds(jj * P, P)].unsqueeze(1).broadcast_to([P, TT, P]),
                                    ALU.mult).then_inc(st.tick(), 1)
                    own()
                    V.tensor_tensor(vst, vst, ln_b[:, bass.ds(jj * P, P)].unsqueeze(1).broadcast_to([P, TT, P]),
                                    ALU.add).then_inc(vst_ready, 1)
                    gelu_arg(u_raw, jj + 1, u_arg, 0)
                    gelu_half(u_tanh, jj + 1, 0)
                    V.tensor_tensor(u_act, g_th[:, 0, :], g_raw[:, 0, :], ALU.mult).then_inc(st.tick(), 1)
                    take("S1", "mix", j, i)
                    V.tensor_tensor(ya.rearrange("p (t n) -> p t n", n=P),
                                    ps["S1"][:, 0:T].rearrange("p (t n) -> p t n", n=P),
                                    bs_rows[:, bass.ds(jj * P, P)].unsqueeze(1).broadcast_to([P, TT, P]), ALU.add)\
                        .then_inc(free["S1"], 1)
                    dve.wait_ge(free["S1"], prior("S1", "mix", j, i) + 1)
                    own()
                    V.tensor_tensor(ya, ya, u_act, ALU.mult).then_inc(st.tick(), 1)
                    for s, g in enumerate((ga, gb)):
                        b = f"M{s}"
                        dve.wait_ge(free[b], prior(b, "mix", (6 * j + 4 + s) // 2, i) + 1)
                        V.tensor_scalar(g, g, 0.5, 0.5, ALU.mult, ALU.add).then_inc(st.tick(), 1)
                    own()
                    V.tensor_tensor(ya, ya, ga, ALU.mult).then_inc(st.tick(), 1)
                    take("OT", "mix", j, i)
                    V.tensor_tensor(gb, gb, ps["OT"][:, 0:T], ALU.mult).then_inc(free["OT"], 1)
                    dve.wait_ge(free["OT"], prior("OT", "mix", j, i) + 1)
                    own()
                    V.tensor_tensor(merged[:, bass.ds(jj, 1), :].rearrange("p a t -> p (a t)"), ya, gb, ALU.add)\
                        .then_inc(merged_ready, 1)
                st.leave(4)
            for t in range(KC):
                b = f"M{t % 2}"
                take(b, "out2", t // 2)
                V.tensor_tensor(xT[:, t, :], xT[:, t, :], ps[b][:, 0:T], ALU.add).then_inc(free[b], 1)
            for b in ("M0", "M1"):
                dve.wait_ge(free[b], prior(b, "out2", 4))
            norm(5, col["norm_ffn_g_2"], hT, h_ready)
            dve.sem_inc(ff_ready, 2)
            with dve.Fori(0, 4) as i:
                for t in range(8):
                    b = f"M{t % 2}"
                    dve.wait_ge(free[b], prior(b, "ff1", t // 2, i) + 1)
                    V.tensor_tensor(ffT[:, bass.ds(i * 8 + t, 1), :].rearrange("p a t -> p (a t)"), relu[:, t % 2, :],
                                    relu[:, t % 2, :], ALU.mult).then_inc(ff_ready, 1)
            with dve.Fori(0, 4) as i:
                for j in range(2):
                    b = f"M{j}"
                    take(b, "ff2", 0, i)
                    xs = xT[:, bass.ds(i * 2 + j, 1), :].rearrange("p a t -> p (a t)")
                    V.tensor_tensor(xs, xs, ps[b][:, 0:T], ALU.add).then_inc(free[b], 1)
            for b in ("M0", "M1"):
                dve.wait_ge(free[b], prior(b, "ff2", 1, 3))
            norm(6, col["norm_ple_g_2"], hT, h_ready)
            with dve.Fori(0, 2) as i:
                st.enter(i, 4)
                for j in range(4):
                    dve.wait_ge(free["M0"], prior("M0", "ple", j, i) + 1)
                    V.tensor_scalar(gate_p[:, 1, :], gate_p[:, 0, :], 0.5, 0.5, ALU.mult, ALU.add).then_inc(st.tick(), 1)
                    take("M1", "ple", j, i)
                    own()
                    V.tensor_tensor(prod_p[:, j % 2, :], gate_p[:, 1, :], ps["M1"][:, 0:T], ALU.mult)\
                        .then_inc(free["M1"], 1)
                    dve.wait_ge(free["M1"], prior("M1", "ple", j, i) + 1)
                    xs = xT[:, bass.ds(i * 4 + j, 1), :].rearrange("p a t -> p (a t)")
                    V.tensor_tensor(xs, xs, prod_p[:, j % 2, :], ALU.add).then_inc(x_ready, 1)
                st.leave(2)
            dve.wait_ge(x_ready, 2 * KC)
            norm(7, col["norm_final_g_2"], hT, h_ready)
            for g in range(2):
                take("T1", "final", g)
                V.tensor_copy(o_rows[:, 1, g * 512:(g + 1) * 512], ps["T1"]).then_inc(free["T1"], 1)


def shape_constants():
    f = np.float32
    p, t = np.arange(P), np.arange(T)
    half = HD // 2
    inv = (f(10000.0) ** (-np.arange(half, dtype=f) / f(half))).astype(f)
    ang = (t.astype(f)[:, None] * inv[None, :]).astype(f)
    K = {"ident": np.eye(P, dtype=f), "tri": (p[:, None] >= p[None, :]).astype(f),
         "cos": np.cos(ang).astype(f).T[p % half], "sin": np.sin(ang).astype(f).T[p % half]}
    rot = np.zeros((P, P), f)
    for j in range(P):
        if j % HD < half:
            rot[j + half, j] = -1
        else:
            rot[j - half, j] = 1
    K["rot"] = rot
    before = np.where(p[:, None] < p[None, :], 0, NEG)
    K["stick_neg"] = np.concatenate([before, np.zeros((P, P)), before], 1).astype(f)
    dist0, dist1 = p[:, None] - p[None, :], P + p[:, None] - t[None, :]
    ok = [[(d >= 0) & (d <= w) & (d % r == 0) for w, r in zip(DIL_WIN, DIL_RATE)] for d in (dist0, dist1)]
    K["dil_neg"] = np.concatenate([np.where(m, 0, NEG) for part in ok for m in part], 1).astype(f)
    K["sgu_mask"] = (p[:, None] <= p[None, :]).astype(f)
    n = np.maximum((T - 1) - np.arange(RMAX), 0)
    exact = NBUCK // 2
    large = exact + (np.log(np.maximum(n, exact).astype(f) / f(exact)) / f(np.log(1024 / exact)) * f(exact)).astype(np.int32)
    bucket = np.where(n < exact, n, np.minimum(large, NBUCK - 1))
    causal = np.arange(RMAX) <= T - 1
    K["rel_hot"] = ((np.arange(NBUCK)[:, None] == bucket[None, :]) & causal[None, :]).astype(f)
    K["rel_neg"] = np.broadcast_to(np.where(causal, 0, NEG), (AH, RMAX)).astype(f)
    K["iota"] = np.broadcast_to(np.arange(TOPK), (P, TOPK)).astype(f)
    return {n: np.ascontiguousarray(a) for n, a in K.items()}


def kernel(**inputs):
    import concourse.bacc as bacc
    from concourse.bass_utils import run_bass_kernel_spmd as run

    nc = bacc.Bacc("TRN2", target_bir_lowering=False, num_devices=1)
    arrays, A, K = {}, {}, {}
    for name, value in inputs.items():
        arrays[f"in_{name}"] = np.ascontiguousarray(value)
        A[name] = nc.dram_tensor(f"in_{name}", arrays[f"in_{name}"].shape, F32, kind="ExternalInput").ap()
    for name, value in shape_constants().items():
        arrays[f"const_{name}"] = value
        K[name] = nc.dram_tensor(f"const_{name}", value.shape, F32, kind="ExternalInput").ap()
    rel_rows = nc.dram_tensor("rel_rows", (AH, P, RMAX), F32).ap()
    out = nc.dram_tensor("out", (1, T, D), F32, kind="ExternalOutput").ap()
    build(nc, A, K, rel_rows, out)
    r = run(nc, [arrays], core_ids=[0])
    return r.results[0]["out"]
```

```python
from contextlib import ExitStack

import numpy as np

import concourse.bass as bass
from concourse import mybir

F32 = mybir.dt.float32
U32 = mybir.dt.uint32
ALU = mybir.AluOpType
ACT = mybir.ActivationFunctionType
AX = mybir.AxisListType

P = 128
T, D = 256, 1024
TT, KC = T // P, D // P
HD = 64
SBW, DILW = 512, 768
SB_PAIRS = SBW // P
DIL_G, DIL_HP = 3, 2
DIL_RATE = (1, 4, 16)
DIL_WIN = (128, 512, 2048)
LAST_ROWS = 5
FIRST_HEADS = 5
NH, NK, TOPK = 8, 128, 16
NU = TT * NH
DFF = 4096
AH = 16
NBUCK = 32
PLE = 256
EPS = 1e-6
SCALE = HD ** -0.5
GELU_A, GELU_C = 0.044715, float(np.sqrt(2.0 / np.pi))
NEG = -1e30
LOWEST = -3.0e38
RMAX = 512

RING = 12
TILES = {
    "stick": (12, 1, list(range(12)), [1] * 12),
    "dilated": (9, 2, list(range(9)), [1] * 9),
    "gates": (12, 2, [4 * j + b for j in range(4) for b in (0, 1, 3)], [1, 1, 2] * 4),
    "out1": (8, 1, list(range(8, 16)), [1] * 8),
    "query": (12, 1, [0] * 8 + [0, 0, 0, 1], [0] * 8 + [1] * 4),
    "query2": (12, 1, [0] * 8 + list(range(4)), [0] * 8 + [1] * 4),
    "sgu_v": (8, 1, list(range(8)), [1] * 8),
    "mix": (12, 4, list(range(12)), [1] * 12),
    "out2": (8, 1, list(range(8)), [1] * 8),
    "ff1": (8, 4, list(range(8)), [1] * 8),
    "ff2": (8, 4, [0] * 4 + [1] * 4, [1] * 8),
    "ple": (8, 2, list(range(8)), [1] * 8),
}
USES = {
    "init": (1, {"T0": 3, "T1": 2, "S0": 2, "S1": 2}),
    "norm1": (1, {"SA": 1}),
    "stick": (1, {"M0": 6, "M1": 6, "SA": 8, "S0": 4, "S1": 9, "T0": 4, "T1": 4, "OT": 4}),
    "dilated": (2, {"M0": 5, "M1": 4, "T0": 7, "T1": 5, "SA": 2, "S0": 2, "OT": 1}),
    "ada": (1, {"S1": 3}),
    "gates": (2, {"M0": 8, "M1": 8}),
    "out1": (1, {"M0": 8, "M1": 8}),
    "norm2": (1, {"SA": 2}),
    "early": (1, {"S0": 2, "S1": 2, "OT": 2}),
    "query": (1, {"M0": 5, "M1": 5}),
    "query2": (1, {"M0": 2, "M1": 2}),
    "rows": (1, {"T0": 2, "T1": 2}),
    "sub": (1, {"SA": 3, "OT": 4}),
    "back": (1, {"T0": 2, "T1": 2}),
    "norm3": (1, {"SA": 1}),
    "norm4": (1, {"SA": 1}),
    "sgu_v": (1, {"M0": 4, "M1": 4}),
    "mix": (4, {"M0": 6, "M1": 6, "SA": 2, "S0": 2, "S1": 2, "T0": 2, "T1": 2, "OT": 2}),
    "out2": (1, {"M0": 4, "M1": 4}),
    "norm5": (1, {"SA": 1}),
    "ff1": (4, {"M0": 4, "M1": 4}),
    "ff2": (4, {"M0": 1, "M1": 1}),
    "norm6": (1, {"SA": 1}),
    "ple": (2, {"M0": 4, "M1": 4}),
    "norm7": (1, {"SA": 1}),
    "final": (1, {"T0": 2, "T1": 2}),
}
DIL_ORDER = [(s, g) for g in range(DIL_G) for s in (0, 1)] + [(2, g) for g in range(DIL_G)]
BANKS = ("M0", "M1", "SA", "S0", "S1", "T0", "T1", "OT")


def prior(bank, stage, k, i=0):
    n = 0
    for name, (bodies, per) in USES.items():
        if name == stage:
            return i * per[bank] + (n + k)
        n += bodies * per.get(bank, 0)
    raise KeyError(stage)


def tile_loads(slot, stage):
    n = 0
    for name, (tiles, bodies, _, dmas) in TILES.items():
        if name == stage:
            return n
        if slot < tiles:
            n += bodies * dmas[slot]
    raise KeyError(stage)


def tile_ready(stage, t, i=0):
    dmas = TILES[stage][3][t]
    return i * (16 * dmas) + 16 * (tile_loads(t, stage) + dmas)


def last_user(slot, stage):
    found = None
    for name, (tiles, bodies, free_after, dmas) in TILES.items():
        if name == stage:
            return found
        if slot < tiles and dmas[slot]:
            k = free_after[slot]
            found = (f"M{k % 2}", prior(f"M{k % 2}", name, k // 2, bodies - 1) + 1)
    raise KeyError(stage)


def query_block(k):
    return ("query", (k + 8) % RING, k - 2) if k < RING else ("query2", k - 4, k - RING)


class Steps:

    def __init__(self, sem):
        self.sem, self.n, self.reg, self.per, self.at = sem, 0, None, 0, 0

    def tick(self):
        self.n += 1
        return self.sem

    def now(self):
        return self.n if self.reg is None else self.reg * self.per + self.n

    def enter(self, reg, per):
        self.reg, self.per, self.at = reg, per, self.n

    def leave(self, bodies):
        assert self.n - self.at == self.per, (self.n - self.at, self.per)
        self.n, self.reg = self.at + bodies * self.per, None


def build(nc, A, K, rel_rows, out):
    with ExitStack() as ctx:
        def sb(name, shape, dt=F32):
            return ctx.enter_context(nc.sbuf_tensor(name, shape, dt))

        def sem(name):
            return ctx.enter_context(nc.semaphore(name))

        ident = sb("ident", [P, P])
        ones = sb("ones", [P, P])
        eps = sb("eps", [P, 1])
        xT = sb("xT", [P, KC, T])
        hT = sb("hT", [P, KC, T])
        tmp = sb("tmp", [P, KC, T])
        merged = sb("merged", [P, KC, T])
        rt = sb("rt", [P, T])
        rstd = sb("rstd", [P, T])
        warm = sb("warm", [P, 8])
        ring = sb("ring", [P, RING, KC, P])
        NVEC = 8 * KC
        vec_rows = sb("vec_rows", [NVEC + 6 * KC, P])
        vecT = sb("vecT", [P, NVEC + 6 * KC])
        names = ("c", "g_mix", "g_ffn", "g_final", "norm_mix_g_2", "norm_ffn_g_2", "norm_ple_g_2",
                 "norm_final_g_2")
        col = {n: vecT[:, KC * i:KC * (i + 1)] for i, n in enumerate(names)}
        b_ada_col = vecT[:, NVEC:NVEC + 6 * KC]
        silu_c = sb("silu_c", [P, 2, KC])
        modT = sb("modT", [P, 6 * KC])
        mod = [modT[:, KC * i:KC * (i + 1)] for i in range(6)]
        gain = sb("gain", [P, 2, KC])
        keysT = sb("keysT", [P, 2 * NH, NK])
        sguT = sb("sguT", [P, KC, P])
        pT = sb("pT", [P, 2, T])
        iota = sb("iota", [P, TOPK])[:, :]
        arena = sb("arena", [P, 27300])
        carved = [0]

        def carve(*shape, dt=F32, parts=P):
            n = int(np.prod(shape))
            ap = arena[0:parts, carved[0]:carved[0] + n]
            carved[0] += n
            assert carved[0] <= 27300, carved[0]
            if dt is not F32:
                ap = ap.bitcast(dt)
            if len(shape) == 2:
                ap = ap.rearrange("p (a b) -> p a b", b=shape[1])
            elif len(shape) == 3:
                ap = ap.rearrange("p (a b c) -> p a b c", b=shape[1], c=shape[2])
            return ap

        ada_ring = carve(2, KC, 512)
        ada_sum = carve(3, 512)
        tri = carve(P)
        rot = carve(P)
        cosT, sinT = carve(T), carve(T)
        stick_neg = carve(384)
        dil_neg = carve(DIL_G * 384)
        osb = carve(SB_PAIRS, T)
        odl = carve(DIL_HP, T)
        qs, ks, vs = carve(T), carve(T), carve(TT, P)
        zm, ez, sp = carve(2, 384), carve(2, 384), carve(2, 384)
        gate_a, gate_b, br_a, br_b = carve(T), carve(T), carve(T), carve(T)
        mark = carved[0]
        ada_third = carve(KC, 512)
        carved[0] = mark
        x_rows = carve(TT, D)
        key_rows = carve(2 * NH, P)
        sgu_rows = carve(KC, P)
        sgu_mask = carve(P)
        p_rows = carve(TT, PLE)
        rel_tab = carve(AH, parts=NBUCK)
        rel_hot = carve(RMAX, parts=NBUCK)
        rel_neg = carve(RMAX, parts=AH)
        rel_row = tmp[0:AH, 0:2, :].rearrange("p a t -> p (a t)")
        carved[0] = mark
        raw = carve(DIL_G, 2, T)
        roped = carve(DIL_G, 2, T)
        rope_a, rope_b = carve(2, T), carve(2, T)
        vd = carve(DIL_G, TT, P)
        sd = carve(2, DIL_G * 384)
        pt = carve(2, DIL_G, 384)
        sm_max, sm_sum, sm_inv = carve(2, 2), carve(2, 2), carve(2, 2)
        carved[0] = 0
        sub = carve(TT * 2 * NH * NK)
        y_rows = sub[:, 0:TT * D]
        h_rows = carve(TT, D)
        v_first = carve(8, D)
        qT = carve(4, T)
        u_ring = carve(8, D)
        dg = carve(8, P)
        dot_junk = tmp[:, 0:4, :].rearrange("p a t -> p (a t)")
        v_ring = [ring[:, n, :, :].rearrange("p c n -> p (c n)") for n in range(8)] + \
            [b.rearrange("p a t -> p (a t)") for b in (tmp[:, 4:8, :], merged[:, 4:8, :])] + \
            [v_first[:, n, :] for n in range(6)]
        q_tiles = [v_first[:, n, :].rearrange("p (c n) -> p c n", n=P) for n in range(8)]
        VR = len(v_ring)
        s16 = carve(2, TOPK)
        i16 = carve(2, TOPK, dt=U32)
        i16f = carve(2, TOPK)
        mark = carved[0]
        sub_w = carve(2, NK)
        cand, cand_w = carve(TOPK, TOPK), carve(TOPK * TOPK)
        best_2 = carve(2, TOPK)
        pos = carve(TOPK, dt=U32)
        pos_ab = carve(2, TOPK, dt=U32)
        pos_f = carve(2, TOPK)
        hot = arena[:, mark:mark + 2 * TOPK * TOPK].rearrange("p (k a) -> p k a", a=TOPK)
        pick = carve(2, TOPK)
        expert_f = carve(TOPK)
        expert = carve(2, TOPK, dt=U32)
        gate_w, gate_n = carve(2, TOPK), carve(2, 1)
        gate_s, gate_r = carve(2, 1), carve(2, 1)
        act_x, act_a, act_b, act_t = carve(2, TOPK), carve(2, TOPK), carve(2, TOPK), carve(2, TOPK)
        wgt = carve(2, TOPK)
        carved[0] = 0
        rel = carve(AH * T)
        bs_rows = carve(KC * P)
        ln_g, ln_b = carve(D), carve(D)
        zv = carve(TT, D)
        zsq = carve(TT, D)
        ln_part = carve(TT, KC)
        ln_s, ln_m, ln_q, ln_r, ln_i = carve(TT), carve(TT), carve(TT), carve(TT), carve(TT)
        g_raw, g_sq, g_th, u_act = carve(2, T), carve(2, T), carve(2, T), carve(T)
        vst = carve(TT, P)
        q2, k2, v2 = carve(T), carve(T), carve(TT, P)
        s2, p2 = carve(2, 384), carve(2, 384)
        ga, gb, ya = carve(T), carve(T), carve(T)
        mx2, sm2, iv2 = carve(2, 2), carve(2, 2), carve(2, 2)
        mark = carved[0]
        carved[0] = 0
        ffT = carve(DFF // P, T)
        relu = carve(2, T)
        gate_p, prod_p = carve(2, T), carve(2, T)
        o_rows = carve(TT, D)

        ps = {b: None for b in BANKS}
        for b in ("M0", "M1", "SA"):
            ps[b] = ctx.enter_context(nc.psum_tensor(f"ps_{b}", [P, 512], F32))[:, :]
        wide = ctx.enter_context(nc.psum_tensor("ps_S", [P, 1024], F32))
        ps["S0"], ps["S1"] = wide[:, 0:512], wide[:, 512:1024]
        twin = ctx.enter_context(nc.psum_tensor("ps_T", [P, 1024], F32))
        ps["T0"], ps["T1"] = twin[:, 0:512], twin[:, 512:1024]
        ps["OT"] = ctx.enter_context(nc.psum_tensor("ps_OT", [P, 512], F32))[:, :]

        done = {b: sem(f"done_{b}") for b in BANKS}
        free = {b: sem(f"free_{b}") for b in BANKS}
        tile_in = [sem(f"tile_in{s}") for s in range(RING)]
        vec_in, ident_in, x_in, key_in, sgu_in, p_in, rel_in, const_in, const2_in = (
            sem(n) for n in ("vec_in", "ident_in", "x_in", "key_in", "sgu_in", "p_in", "rel_in", "const_in",
                             "const2_in"))
        ada_in = [sem(f"ada_in{s}") for s in range(3)]
        ada_used, ada_ready, mod_ready = sem("ada_used"), sem("ada_ready"), sem("mod_ready")
        setup_done, silu_half, silu_ready = sem("setup_done"), sem("silu_half"), sem("silu_ready")
        rel_out, rel_back, layer2_in = sem("rel_out"), sem("rel_back"), sem("layer2_in")
        x_ready = sem("x_ready")
        sq_ready, scaled, h_ready = sem("sq_ready"), sem("scaled"), sem("h_ready")
        stick_sp, stick_ln, stick_p = sem("stick_sp"), sem("stick_ln"), sem("stick_p")
        qkv_ready = sem("qkv_ready")
        roped_ready = sem("roped_ready")
        soft_max, soft_exp, soft_p, pt_ready = sem("soft_max"), sem("soft_exp"), sem("soft_p"), sem("pt_ready")
        merged_ready = sem("merged_ready")
        sub_ready = sem("sub_ready")
        idx_ready, best_ready, gate_exp = sem("idx_ready"), sem("best_ready"), sem("gate_exp")
        q_in = [sem(f"q_in{s}") for s in range(8)]
        u_in = [sem(f"u_in{s}") for s in range(8)]
        v_in = [sem(f"v_in{s}") for s in range(VR)]
        u_used, v_used, issued = sem("u_used"), sem("v_used"), sem("issued")
        act_arg, act_tanh, wgt_ready, diag_ready = sem("act_arg"), sem("act_tanh"), sem("wgt_ready"), sem("diag_ready")
        y_ready = sem("y_ready")
        zv_raw, zv_arg, zv_tanh, zv_ready = sem("zv_raw"), sem("zv_arg"), sem("zv_tanh"), sem("zv_ready")
        ln_c, ln_sq, ln_root, vst_ready = sem("ln_c"), sem("ln_sq"), sem("ln_root"), sem("vst_ready")
        u_raw, u_arg, u_tanh = sem("u_raw"), sem("u_arg"), sem("u_tanh")
        ff_ready = sem("ff_ready")
        out_done = sem("out_done")
        dve_step, act_step = sem("dve_step"), sem("act_step")
        slots_freed, route_step = sem("slots_freed"), sem("route_step")

        block = ctx.enter_context(nc.Block())

        w_in, w_in2 = A["w_in"][0], A["w_in_2"][0]

        def rows8(w):
            return w.rearrange("(c p) n -> p c n", p=P)

        w_in_v, w_in2_v = rows8(w_in), rows8(w_in2)
        w_ada_v = rows8(A["w_ada"][0])
        w_sbo_v, w_dlo_v = rows8(A["w_sb_o"][0]), rows8(A["w_dil_o"][0])
        w_out_v, w_pq_v, w_out2_v = rows8(A["w_out"][0]), rows8(A["w_pq"][0]), rows8(A["w_out_2"][0])
        w_ff1_v = rows8(A["w_ff1_2"][0])
        w_ff2_v = A["w_ff2_2"][0].rearrange("(q c p) n -> q p c n", p=P, c=KC)
        w_plg_v, w_plp_v = rows8(A["w_ple_gate_2"][0]), rows8(A["w_ple_proj_2"][0])

        def load_vectors(eng, lo, hi):
            for i in range(lo, hi):
                src = A[names[i]] if len(A[names[i]].shape) == 1 else A[names[i]][0]
                eng.dma_start(vec_rows[KC * i:KC * (i + 1), :],
                              src.rearrange("(c p) -> c p", p=P)).then_inc(vec_in, 16)

        def ada_slot(ch):
            if ch == 2:
                return ada_in[2], 16, ada_third
            n = ch if ch < 2 else ch - 1
            return ada_in[n % 2], 16 * (n // 2 + 1), ada_ring[:, n % 2]

        def ada_sums(ch):
            if ch < 4:
                return ("S0", "S1")[ch % 2], "init", ch // 2
            return ("S1", "stick", ch - 4) if ch < 9 else ("S1", "ada", ch - 9)

        @block.sync
        def _(eng):
            load_vectors(eng, 0, 4)
            eng.dma_start(vec_rows[NVEC:NVEC + 6 * KC, :],
                          A["b_ada"][0].rearrange("(c p) -> c p", p=P)).then_inc(vec_in, 16)
            eng.dma_start(ident[:, :], K["ident"]).then_inc(ident_in, 16)
            eng.dma_start(x_rows, A["x"][0].rearrange("(t p) d -> p t d", p=P)).then_inc(x_in, 16)

            def tile(stage, t, i, *parts):
                if isinstance(i, int) and i == 0:
                    user = last_user(t, stage)
                    if user is not None:
                        eng.wait_ge(done[user[0]], user[1])
                else:
                    k = TILES[stage][2][t]
                    b = f"M{k % 2}"
                    eng.wait_ge(done[b], prior(b, stage, k // 2, i - 1) + 1)
                    eng.sem_inc(slots_freed, 1)
                for lo, hi, src in parts:
                    eng.dma_start(ring[:, t, lo:hi, :], src).then_inc(tile_in[t], 16)

            def cols(view, start):
                return (0, KC, view[:, :, bass.ds(start, P)])

            def stick_tiles(i):
                for j in range(SB_PAIRS):
                    for s in range(3):
                        tile("stick", 3 * j + s, i, cols(w_in_v, s * SBW + j * P))

            def dilated_tiles(i):
                for t, (s, g) in enumerate(DIL_ORDER):
                    tile("dilated", t, i, cols(w_in_v, i * P + (3 * SBW + s * DILW + g * 256)))

            def gate_tiles(i):
                for j in range(4):
                    n = i * (4 * P) + j * P
                    g0 = 3 * SBW + 3 * DILW
                    tile("gates", 3 * j, i, cols(w_in_v, n + g0))
                    tile("gates", 3 * j + 1, i, cols(w_in_v, n + (g0 + D)))
                    tile("gates", 3 * j + 2, i, (0, 4, w_sbo_v[:, :, bass.ds(n, P)]),
                         (4, 6, w_dlo_v[:, :, bass.ds(n, P)]))

            def plain_tiles(stage, view, base=0):
                def body(i):
                    for t in range(8):
                        tile(stage, t, i, cols(view, i * (8 * P) + (base + t * P)))
                return body

            def mix_tiles(i):
                for j in range(2):
                    for t, base in enumerate((2 * D, 3 * D, 4 * D, 0, 5 * D, 6 * D)):
                        tile("mix", 6 * j + t, i, cols(w_in2_v, i * (2 * P) + (base + j * P)))

            def ff2_tiles(i):
                for j in range(2):
                    for q in range(4):
                        tile("ff2", 4 * j + q, i, (0, KC, w_ff2_v[q][:, :, bass.ds(i * (2 * P) + j * P, P)]))

            def ple_tiles(i):
                for j in range(4):
                    n = i * (4 * P) + j * P
                    tile("ple", 2 * j, i, cols(w_plg_v, n))
                    tile("ple", 2 * j + 1, i, (0, 2, w_plp_v[:, :, bass.ds(n, P)]))

            def stream(stage, body):
                body(0)
                bodies = TILES[stage][1]
                if bodies > 1:
                    with eng.Fori(1, bodies) as i:
                        body(i)

            for dst, n in ((tri, "tri"), (stick_neg, "stick_neg")):
                eng.dma_start(dst, K[n]).then_inc(const_in, 16)
            eng.wait_ge(ada_in[2], 16)
            stream("stick", stick_tiles)
            landed, value, _ = ada_slot(8)
            eng.wait_ge(landed, value)
            for dst, n in ((rot, "rot"), (cosT, "cos"), (sinT, "sin"), (dil_neg, "dil_neg"), (iota[:, :], "iota")):
                eng.dma_start(dst, K[n]).then_inc(const2_in, 16)
            bank, stage, k = ada_sums(2)
            eng.wait_ge(done[bank], prior(bank, stage, k) + 1)
            eng.dma_start(key_rows, A["peer_keys"][0].rearrange("h s n c -> n (h s) c")).then_inc(key_in, 16)
            eng.dma_start(sgu_rows, A["w_sgu_spatial_2"][0].rearrange("g t s -> t g s")).then_inc(sgu_in, 16)
            eng.dma_start(sgu_mask, K["sgu_mask"]).then_inc(sgu_in, 16)
            eng.dma_start(p_rows, A["p_2"][0, 0].rearrange("(t p) d -> p t d", p=P)).then_inc(p_in, 16)
            eng.dma_start(rel_tab, A["rel_bias_2"]).then_inc(rel_in, 16)
            eng.dma_start(rel_hot, K["rel_hot"]).then_inc(rel_in, 16)
            eng.dma_start(rel_neg, K["rel_neg"]).then_inc(rel_in, 16)
            stream("dilated", dilated_tiles)
            stream("gates", gate_tiles)
            stream("out1", plain_tiles("out1", w_out_v))
            for k in range(2 * NH):
                if k == 4:
                    for b in ("M0", "M1"):
                        eng.wait_ge(done[b], prior(b, "out1", 0))
                if 4 <= k < RING:
                    eng.dma_start(q_tiles[k - 4], cols(w_pq_v, k * P)[2]).then_inc(q_in[k - 4], 16)
                else:
                    stage, t, _ = query_block(k)
                    tile(stage, t, 0, cols(w_pq_v, k * P))
            eng.wait_ge(y_ready, 4)
            stream("sgu_v", plain_tiles("sgu_v", w_in2_v, D))
            stream("mix", mix_tiles)
            stream("out2", plain_tiles("out2", w_out2_v))
            stream("ff1", plain_tiles("ff1", w_ff1_v))
            stream("ff2", ff2_tiles)
            stream("ple", ple_tiles)
            for g in range(4):
                b, t, n = f"T{g % 2}", g % 2, g // 2 * 512
                eng.wait_ge(free[b], prior(b, "final", g // 2) + 1)
                eng.dma_start(out[0, t * P:(t + 1) * P, n:n + 512], o_rows[:, t, n:n + 512]).then_inc(out_done, 16)
            eng.wait_ge(out_done, 16 * 4)

        @block.gpsimd
        def _(pool):
            nc.gpsimd.memset(ones[:, :], 1.0).then_inc(setup_done, 1)
            nc.gpsimd.memset(eps[:, :], EPS).then_inc(setup_done, 1)
            for ch in range(12):
                if ch == 1:
                    pool.wait_ge(vec_in, 9 * 16)
                elif ch == 2:
                    pool.wait_ge(done["T0"], prior("T0", "init", 2) + 1)
                    pool.wait_ge(done["T1"], prior("T1", "init", 1) + 1)
                elif 3 <= ch < 6:
                    bank, stage, k = ada_sums((0, 1, 3)[ch - 3])
                    pool.wait_ge(done[bank], prior(bank, stage, k) + 1)
                elif ch >= 6:
                    pool.wait_ge(ada_used, ch - 5)
                landed, _, slot = ada_slot(ch)
                pool.dma_start(slot, w_ada_v[:, :, ch * 512:(ch + 1) * 512]).then_inc(landed, 16)

            pool.wait_ge(rel_out, 1)
            pool.dma_start(rel_rows, rel_row.unsqueeze(1).broadcast_to([AH, P, RMAX])).then_inc(rel_back, 16)

            def gather(slots, table, sems, used, s, u):
                for k in range(TOPK):
                    pool.wait_ge(used, u * TOPK + (k + 1))
                    pool.sem_inc(issued, 1)
                    pool.indirect_dma_start(slots[k % len(slots)], None, table,
                                            bass.IndirectOffsetOnAxis(ap=expert[:, s, k:k + 1], axis=0))\
                        .then_inc(sems[k % len(slots)], 16)

            with pool.Fori(0, NU // 2) as i:
                for s in range(2):
                    u = i * 2 + s
                    pool.wait_ge(idx_ready, u + 1)
                    gather([u_ring[:, n, :] for n in range(8)], A["peer_u"][0], u_in, u_used, s, u)
                    gather(v_ring, A["peer_v"][0], v_in, v_used, s, u)
            pool.wait_ge(done["T0"], prior("T0", "back", 2))
            pool.wait_ge(done["T1"], prior("T1", "back", 2))
            pool.wait_ge(rel_back, 16)
            pool.dma_start(rel.rearrange("p (h k) -> p h k", k=T),
                           bass.AP(rel_rows.tensor, P - 1, [[RMAX - 1, P], [P * RMAX, AH], [1, T]])).then_inc(layer2_in, 16)
            pool.dma_start(bs_rows, A["b_sgu_spatial_2"][0].rearrange("g t -> (g t)").partition_broadcast(P))\
                .then_inc(layer2_in, 16)
            pool.dma_start(ln_g, A["ln_v_g_2"][0].partition_broadcast(P)).then_inc(layer2_in, 16)
            pool.dma_start(ln_b, A["ln_v_b_2"][0].partition_broadcast(P)).then_inc(layer2_in, 16)

        @block.tensor
        def _(pe):
            mm = nc.tensor.matmul

            def claim(bank, stage, k, i=0):
                n = prior(bank, stage, k, i)
                if not isinstance(n, int) or n > 0:
                    pe.wait_ge(free[bank], n)

            def norm(n):
                claim("SA", f"norm{n}", 0)
                for c in range(KC):
                    pe.wait_ge(sq_ready, KC * (n if n > 2 else n - 1) + c + 1)
                    m = mm(ps["SA"][:, 0:T], ones[:, :], tmp[:, c, :], start=c == 0, stop=c == KC - 1)
                m.then_inc(done["SA"], 1)

            def block_t(stage, t, k, i, src=None, chunks=(0, KC), fresh=None, aside=None):
                bank = f"M{k % 2}"
                claim(bank, stage, k // 2, i)
                if aside is None:
                    w = ring[:, t]
                    pe.wait_ge(tile_in[t], tile_ready(stage, t, i))
                else:
                    landed, w = aside
                    pe.wait_ge(landed, 16)
                lo, hi = chunks
                for c in range(lo, hi):
                    if fresh is not None:
                        pe.wait_ge(fresh[0], fresh[1] + c + 1)
                    rhs = hT[:, c, :] if src is None else src(c)
                    m = mm(ps[bank][:, 0:T], w[:, c, :], rhs, start=c == lo, stop=c == hi - 1)
                m.then_inc(done[bank], 1)

            def block_r(stage, t, k, i, fresh=None):
                bank = f"M{k % 2}"
                claim(bank, stage, k // 2, i)
                pe.wait_ge(tile_in[t], tile_ready(stage, t, i))
                for tt in range(TT):
                    for c in range(KC):
                        if fresh is not None and tt == 0:
                            pe.wait_ge(fresh[0], fresh[1] + c + 1)
                        m = mm(ps[bank][:, tt * P:(tt + 1) * P], hT[:, c, tt * P:(tt + 1) * P], ring[:, t, c, :],
                               start=c == 0, stop=c == KC - 1)
                m.then_inc(done[bank], 1)

            def turn(stage, group, sources, width=P):
                bank = f"T{group % 2}"
                claim(bank, stage, group // 2)
                for n, src in enumerate(sources):
                    m = nc.tensor.transpose(ps[bank][:, n * P:n * P + width], src, ident[0:width, 0:width])
                m.then_inc(done[bank], 1)

            def ada_columns(ch):
                bank, stage, k = ada_sums(ch)
                claim(bank, stage, k)
                if ch < 4:
                    landed, value, slot = ada_slot(ch)
                    pe.wait_ge(landed, value)
                    for c in range(KC):
                        mm(ps[bank][:, 0:1], slot[:, c, 0:P], silu_c[:, 1, c:c + 1],
                           start=c == 0, stop=c == KC - 1)
                pe.wait_ge(ada_ready, ch + 1)
                for b in range(1 if ch < 4 else 0, 4):
                    m = mm(ps[bank][:, b:b + 1], ada_sum[:, ch % 3, b * P:(b + 1) * P], ones[:, 0:1],
                           start=True, stop=True)
                m.then_inc(done[bank], 1)

            def extra(e):
                bank, k = ("SA", "S1")[e % 2], (4, 5)[e % 2] + e // 2
                if e < 4:
                    pe.wait_ge(key_in, 16)
                    sources = [key_rows[:, 4 * e + n, :] for n in range(4)]
                elif e < 6:
                    pe.wait_ge(sgu_in, 32)
                    sources = [sgu_rows[:, 4 * (e - 4) + n, :] for n in range(4)]
                elif e == 6:
                    pe.wait_ge(p_in, 16)
                    sources = [p_rows[:, tt, c * P:(c + 1) * P] for c in range(2) for tt in range(TT)]
                claim(bank, "stick", k)
                if e < 7:
                    for n, src in enumerate(sources):
                        m = nc.tensor.transpose(ps[bank][:, n * P:(n + 1) * P], src, ident[:, :])
                else:
                    pe.wait_ge(rel_in, 48)
                    m = mm(ps[bank][0:AH, 0:RMAX], rel_tab, rel_hot, start=True, stop=True)
                m.then_inc(done[bank], 1)

            pe.wait_ge(setup_done, 2)
            pe.wait_ge(ident_in, 16)
            pe.wait_ge(vec_in, 9 * 16)
            turn("init", 0, [vec_rows[:, :]], width=NVEC + 6 * KC)
            pe.wait_ge(x_in, 16)
            for g in range(4):
                turn("init", 1 + g, [x_rows[:, tt, c * P:(c + 1) * P] for c in (2 * g, 2 * g + 1) for tt in range(TT)])
            pe.wait_ge(silu_ready, 1)
            ada_columns(0)
            norm(1)
            for ch in range(1, 4):
                ada_columns(ch)
            pe.wait_ge(const_in, 2 * 16)
            block_t("stick", 0, 0, 0, fresh=(h_ready, 0))
            block_t("stick", 1, 1, 0)
            for j in range(SB_PAIRS):
                pe.wait_ge(qkv_ready, 3 * j + 2)
                for h, bank in enumerate(("SA", "S0")):
                    r = slice(HD * h, HD * h + HD)
                    claim(bank, "stick", j)
                    mm(ps[bank][:, 0:T], ks[r, 0:P], qs[r, :], start=True, stop=True)
                    mm(ps[bank][:, T:384], ks[r, P:T], qs[r, P:T], start=True, stop=True).then_inc(done[bank], 1)
                if 0 < j < 3:
                    ada_columns(3 + 2 * j)
                block_r("stick", 3 * j + 2, 3 * j + 2, 0)
                if j == SB_PAIRS - 1:
                    for e in range(4):
                        extra(e)
                else:
                    block_t("stick", 3 * j + 3, 3 * j + 3, 0)
                for h in range(2):
                    bank = f"T{h}"
                    pe.wait_ge(stick_sp, 2 * j + h + 1)
                    claim(bank, "stick", j)
                    mm(ps[bank][:, 0:384], tri, sp[:, h, :], start=True, stop=False)
                    mm(ps[bank][:, P:T], ones[:, :], sp[:, h, T:384], start=False, stop=True).then_inc(done[bank], 1)
                if j == SB_PAIRS - 1:
                    for e in range(4, 8):
                        extra(e)
                else:
                    ada_columns(4 + 2 * j)
                    block_t("stick", 3 * j + 4, 3 * j + 4, 0)
                pe.wait_ge(qkv_ready, 3 * j + 3)
                claim("OT", "stick", j)
                for h in range(2):
                    r = slice(HD * h, HD * h + HD)
                    pe.wait_ge(stick_p, 2 * j + h + 1)
                    mm(ps["OT"][r, 0:T], vs[:, 0, r], ez[:, h, 0:T], start=True, stop=False)
                    m = mm(ps["OT"][r, P:T], vs[:, 1, r], ez[:, h, T:384], start=False, stop=True)
                m.then_inc(done["OT"], 1)

            pe.wait_ge(free["S1"], prior("S1", "stick", 9))
            pe.wait_ge(const2_in, 5 * 16)

            with pe.Fori(0, DIL_HP) as i:
                def rotate(g):
                    for s in range(2):
                        bank = f"T{s}"
                        pe.wait_ge(qkv_ready, i * 9 + (12 + 2 * g + s + 1))
                        claim(bank, "dilated", g, i)
                        mm(ps[bank][:, 0:T], rot, raw[:, g, s, :], start=True, stop=True).then_inc(done[bank], 1)

                for t, (s, g) in enumerate(DIL_ORDER[:6]):
                    block_t("dilated", t, t, i)
                    if s == 1 and g > 0:
                        rotate(g - 1)
                rotate(DIL_G - 1)
                block_r("dilated", 6, 6, i)
                pe.wait_ge(roped_ready, i * 3 + 3)
                for h in range(2):
                    r = slice(HD * h, HD * h + HD)
                    claim("SA", "dilated", h, i)
                    for g in range(DIL_G):
                        m = mm(ps["SA"][:, g * P:(g + 1) * P], roped[r, g, 0, 0:P], roped[r, g, 1, 0:P],
                               start=True, stop=True)
                    m.then_inc(done["SA"], 1)
                    claim("S0", "dilated", h, i)
                    for g in range(DIL_G):
                        m = mm(wide[:, g * T:(g + 1) * T], roped[r, g, 0, P:T], roped[r, g, 1, :],
                               start=True, stop=True)
                    m.then_inc(done["S0"], 1)
                for t in (7, 8):
                    block_r("dilated", t, t, i)
                pe.wait_ge(qkv_ready, i * 9 + 21)
                claim("OT", "dilated", 0, i)
                for h in range(2):
                    r = slice(HD * h, HD * h + HD)
                    pe.wait_ge(soft_p, i * 4 + (2 * h + 2))
                    for g in range(DIL_G):
                        bank = f"T{g % 2}"
                        claim(bank, "dilated", 3 + 2 * h + g // 2 if g % 2 == 0 else 3 + h, i)
                        at = DIL_G * P + g * T
                        for n, lo in enumerate((g * P, at, at + P)):
                            m = nc.tensor.transpose(ps[bank][:, n * P:(n + 1) * P], sd[:, h, lo:lo + P], ident[:, :])
                        m.then_inc(done[bank], 1)
                    pe.wait_ge(pt_ready, i * 6 + (3 * h + 3))
                    for g in range(DIL_G):
                        mm(ps["OT"][r, 0:T], vd[:, g, 0, r], pt[:, h, g, 0:T], start=g == 0, stop=False)
                        m = mm(ps["OT"][r, P:T], vd[:, g, 1, r], pt[:, h, g, T:384], start=False, stop=g == 2)
                m.then_inc(done["OT"], 1)

            pe.wait_ge(free["S0"], prior("S0", "dilated", 0, DIL_HP))
            for ch in (9, 10, 11):
                ada_columns(ch)
            with pe.Fori(0, 2) as i:
                for j in range(4):
                    block_t("gates", 3 * j, 4 * j, i)
                    block_t("gates", 3 * j + 1, 4 * j + 1, i)
                    if j == 0:
                        pe.wait_ge(free["OT"], prior("OT", "dilated", 1, DIL_HP - 1))
                    block_t("gates", 3 * j + 2, 4 * j + 2, i, lambda c: osb[:, c, :], (0, 4))
                    block_t("gates", 3 * j + 2, 4 * j + 3, i, lambda c: odl[:, c - 4, :], (4, 6))
            def out1_block(tt, t):
                bank = f"M{t % 2}"
                claim(bank, "out1", 4 * tt + t // 2)
                pe.wait_ge(tile_in[t], tile_ready("out1", t))
                for c in range(KC):
                    if tt == 0 and t == 0:
                        pe.wait_ge(merged_ready, c + 1)
                    m = mm(ps[bank][:, 0:P], ring[:, t, c, :], merged[:, c, tt * P:(tt + 1) * P],
                           start=c == 0, stop=c == KC - 1)
                m.then_inc(done[bank], 1)

            def norm2(tt):
                claim("SA", "norm2", tt)
                for c in range(KC):
                    pe.wait_ge(sq_ready, KC * (1 + tt) + c + 1)
                    m = mm(ps["SA"][:, 0:P], ones[:, :], tmp[:, c, tt * P:(tt + 1) * P], start=c == 0, stop=c == KC - 1)
                m.then_inc(done["SA"], 1)

            def early_route(tt):
                for half, bank in enumerate(("S0", "S1")):
                    claim(bank, "early", tt)
                    stage, t, _ = query_block(half)
                    pe.wait_ge(tile_in[t], tile_ready(stage, t))
                    for c in range(KC):
                        if half == 0:
                            pe.wait_ge(h_ready, KC * (1 + tt) + c + 1)
                        m = mm(ps[bank][:, 0:P], ring[:, t, c, :], hT[:, c, tt * P:(tt + 1) * P],
                               start=c == 0, stop=c == KC - 1)
                    m.then_inc(done[bank], 1)
                for bank in ("S0", "S1"):
                    pe.wait_ge(free[bank], prior(bank, "early", tt) + 1)
                claim("OT", "early", tt)
                for half in range(2):
                    m = mm(ps["OT"][:, half * P:(half + 1) * P], qT[:, half, tt * P:(tt + 1) * P], keysT[:, half, :],
                           start=True, stop=True)
                m.then_inc(done["OT"], 1)
                for g in (2 * tt, 2 * tt + 1):
                    turn("rows", g, [hT[:, 4 * (g % 2) + n, tt * P:(tt + 1) * P] for n in range(4)])

            for t in range(KC):
                out1_block(0, t)
            norm2(0)
            for t in range(3):
                out1_block(1, t)
            early_route(0)
            for t in range(3, KC):
                out1_block(1, t)
            norm2(1)
            early_route(1)
            pe.sem_inc(v_used, 10)

            def scores(h):
                bank = ("SA", "OT")[h % 2]
                for half in range(2):
                    pe.wait_ge(free[f"M{half}"], prior(f"M{half}", "query", h - 1) + 1)
                claim(bank, "sub", (h - 1) // 2)
                for tt in range(TT):
                    for half in range(2):
                        n = 2 * tt + half
                        m = mm(ps[bank][:, n * P:(n + 1) * P], qT[:, 2 * (h % 2) + half, tt * P:(tt + 1) * P],
                               keysT[:, 2 * h + half, :], start=True, stop=True)
                m.then_inc(done[bank], 1)

            def queries(lo, hi):
                for k in range(lo, hi):
                    stage, t, n = query_block(k)
                    block_t(stage, t, n, 0, aside=(q_in[k - 4], q_tiles[k - 4]) if 4 <= k < RING else None)
                    if k > lo and k % 2 == 0:
                        scores(k // 2 - 1)
                    if k in (5, 7, 9):
                        pe.wait_ge(done["M1"], prior("M1", "query", n // 2) + 1)
                        pe.sem_inc(v_used, 2)
                scores(hi // 2 - 1)

            queries(2, 2 * FIRST_HEADS)

            for b in ("T0", "T1"):
                pe.wait_ge(free[b], prior(b, "back", 0))
            def expert_pair(i, first=False, last=False):
                for s in range(TT):
                    u = i * TT + s
                    acc = wide if s == 0 else twin
                    rows = TOPK - LAST_ROWS if last and s == TT - 1 else TOPK
                    for k in range(rows):
                        pe.wait_ge(diag_ready, u * TOPK + (k + 1))
                        pe.wait_ge(v_in[k], (u + 1) * 16)
                        for lo in (0, 512):
                            m = mm(acc[:, lo:lo + 512], dg[:, k % 8, :], v_ring[k][:, lo:lo + 512],
                                   start=first and k == 0, stop=last and k == rows - 1)
                        m.then_inc(v_used, 1)

            expert_pair(0, first=True)
            queries(2 * FIRST_HEADS, 2 * NH)
            with pe.Fori(1, NH - 1) as i:
                expert_pair(i)
            expert_pair(NH - 1, last=True)
            pe.wait_ge(y_ready, 4)
            for g in range(4):
                turn("back", g, [y_rows[:, tt * D + c * P:tt * D + (c + 1) * P]
                                 for c in (2 * g, 2 * g + 1) for tt in range(TT)])
            norm(3)
            norm(4)

            for t in range(8):
                block_r("sgu_v", t, t, 0, fresh=(h_ready, 3 * KC) if t == 0 else None)
            with pe.Fori(0, 4) as i:
                for j in range(2):
                    k0 = 6 * j
                    block_t("mix", k0, k0, i)
                    block_t("mix", k0 + 1, k0 + 1, i)
                    pe.wait_ge(qkv_ready, i * 6 + (30 + 3 * j + 2))
                    for h, bank in enumerate(("SA", "S0")):
                        r = slice(HD * h, HD * h + HD)
                        claim(bank, "mix", j, i)
                        mm(ps[bank][:, 0:P], q2[r, 0:P], k2[r, 0:P], start=True, stop=True)
                        mm(ps[bank][:, P:384], q2[r, P:T], k2[r, :], start=True, stop=True).then_inc(done[bank], 1)
                    block_r("mix", k0 + 2, k0 + 2, i)
                    block_t("mix", k0 + 3, k0 + 3, i)
                    for h in range(2):
                        bank = f"T{h}"
                        pe.wait_ge(soft_p, i * 8 + (8 + 4 * j + 2 * h + 2))
                        claim(bank, "mix", j, i)
                        for n in range(3):
                            m = nc.tensor.transpose(ps[bank][:, n * P:(n + 1) * P], s2[:, h, n * P:(n + 1) * P],
                                                    ident[:, :])
                        m.then_inc(done[bank], 1)
                    block_t("mix", k0 + 4, k0 + 4, i)
                    pe.wait_ge(qkv_ready, i * 6 + (30 + 3 * j + 3))
                    claim("OT", "mix", j, i)
                    for h in range(2):
                        r = slice(HD * h, HD * h + HD)
                        pe.wait_ge(pt_ready, i * 4 + (12 + 2 * j + h + 1))
                        mm(ps["OT"][r, 0:T], v2[:, 0, r], p2[:, h, 0:T], start=True, stop=False)
                        m = mm(ps["OT"][r, P:T], v2[:, 1, r], p2[:, h, T:384], start=False, stop=True)
                    m.then_inc(done["OT"], 1)
                    pe.wait_ge(vst_ready, i * 2 + (j + 1))
                    claim("S1", "mix", j, i)
                    for tt in range(TT):
                        m = mm(ps["S1"][:, tt * P:(tt + 1) * P], vst[:, tt, :],
                               sguT[:, bass.ds(i * 2 + j, 1), :].rearrange("p a b -> p (a b)"), start=True, stop=True)
                    m.then_inc(done["S1"], 1)
                    block_t("mix", k0 + 5, k0 + 5, i)
            for t in range(KC):
                block_t("out2", t, t, 0, lambda c: merged[:, c, :], fresh=(merged_ready, KC) if t == 0 else None)
            norm(5)
            with pe.Fori(0, 4) as i:
                for t in range(8):
                    block_t("ff1", t, t, i, fresh=(h_ready, 4 * KC) if t == 0 else None)
            pe.wait_ge(ff_ready, DFF // P - KC + 2)
            with pe.Fori(0, 4) as i:
                for j in range(2):
                    bank = f"M{j}"
                    claim(bank, "ff2", 0, i)
                    for q in range(4):
                        pe.wait_ge(tile_in[4 * j + q], tile_ready("ff2", 4 * j + q, i))
                        for c in range(KC):
                            if j == 0 and q == 3:
                                pe.wait_ge(ff_ready, q * KC + c + 3)
                            m = mm(ps[bank][:, 0:T], ring[:, 4 * j + q, c, :], ffT[:, q * KC + c, :],
                                   start=q + c == 0, stop=q == 3 and c == KC - 1)
                    m.then_inc(done[bank], 1)
            norm(6)
            with pe.Fori(0, 2) as i:
                for j in range(4):
                    block_t("ple", 2 * j, 2 * j, i, fresh=(h_ready, 5 * KC) if j == 0 else None)
                    block_t("ple", 2 * j + 1, 2 * j + 1, i, lambda c: pT[:, c, :], (0, 2))
            norm(7)
            for g in range(4):
                pe.wait_ge(h_ready, 6 * KC + 4 * (g // 2 + 1))
                turn("final", g, [hT[:, 4 * (g // 2) + n, (g % 2) * P:(g % 2 + 1) * P] for n in range(4)])

        @block.scalar
        def _(act):
            st = Steps(act_step)
            F = nc.scalar.activation

            def take(bank, stage, k, i=0):
                act.wait_ge(done[bank], prior(bank, stage, k, i) + 1)

            def norm(n, updated):
                F(warm[:, n:n + 1], eps[:, :], ACT.Sqrt)
                for c in range(KC if updated is not None else 0):
                    act.wait_ge(*updated(c))
                    F(tmp[:, c, :], xT[:, c, :], ACT.Square).then_inc(sq_ready, 1)
                take("SA", f"norm{n}", 0)
                F(rt[:, :], ps["SA"][:, 0:T], ACT.Sqrt, bias=eps[:, :], scale=1.0 / D).then_inc(free["SA"], 1)

            def shifted(shift):
                for c in range(KC):
                    act.wait_ge(scaled, c + 1)
                    F(hT[:, c, :], tmp[:, c, :], ACT.Identity, bias=shift[:, c:c + 1]).then_inc(h_ready, 1)

            def read(bank, stage, k, i=0):
                return free[bank], prior(bank, stage, k, i) + 1

            load_vectors(act, 4, len(names))
            take("T0", "init", 0)
            F(vecT[:, :], ps["T0"][:, 0:NVEC + 6 * KC], ACT.Copy).then_inc(free["T0"], 1)
            act.wait_ge(free["T0"], 1)
            F(silu_c[:, 0, :], col["c"], ACT.Tanh, scale=0.5).then_inc(silu_half, 1)
            for g in range(4):
                bank = f"T{(1 + g) % 2}"
                take(bank, "init", (1 + g) // 2)
                F(xT[:, 2 * g:2 * g + 2, :].rearrange("p c t -> p (c t)"), ps[bank], ACT.Copy).then_inc(free[bank], 1)
            act.wait_ge(setup_done, 2)
            norm(1, lambda c: read(f"T{(1 + c // 2) % 2}", "init", (1 + c // 2) // 2))
            act.wait_ge(mod_ready, 4)
            shifted(mod[0])
            def stick_copy(k, dst):
                b = f"M{k % 2}"
                take(b, "stick", k // 2)
                F(dst, ps[b][:, 0:T], ACT.Copy).then_inc(free[b], 1)
                act.wait_ge(free[b], prior(b, "stick", k // 2) + 1)
                act.sem_inc(qkv_ready, 1)

            stick_copy(0, qs)
            stick_copy(1, ks)
            for j in range(SB_PAIRS):
                for h, bank in enumerate(("SA", "S0")):
                    act.wait_ge(free[bank], prior(bank, "stick", j) + 1)
                    F(ez[:, h, :], zm[:, h, :], ACT.Abs).then_inc(st.tick(), 1)
                for h in range(2):
                    act.wait_ge(st.sem, 4 * j + 1 + h)
                    F(ez[:, h, :], ez[:, h, :], ACT.Exp, scale=-1.0).then_inc(st.tick(), 1)
                for h in range(2):
                    act.wait_ge(st.sem, 4 * j + 3 + h)
                    F(ez[:, h, :], ez[:, h, :], ACT.Ln, bias=ones[:, 0:1]).then_inc(stick_ln, 1)
                if j == SB_PAIRS - 1:
                    for e in range(4):
                        bank, k = ("SA", "S1")[e % 2], (4, 5)[e % 2] + e // 2
                        take(bank, "stick", k)
                        F(keysT[:, 4 * e:4 * e + 4, :].rearrange("p a b -> p (a b)"), ps[bank], ACT.Copy)\
                            .then_inc(free[bank], 1)
                stick_copy(3 * j + 2, vs.rearrange("p t n -> p (t n)"))
                if j < SB_PAIRS - 1:
                    stick_copy(3 * j + 3, qs)
                for h in range(2):
                    act.wait_ge(free[f"T{h}"], prior(f"T{h}", "stick", j) + 1)
                    F(ez[:, h, :], zm[:, h, :], ACT.Exp).then_inc(stick_p, 1)
                if j < SB_PAIRS - 1:
                    stick_copy(3 * j + 4, ks)
                if j == SB_PAIRS - 1:
                    take("SA", "stick", 7)
                    F(pT[:, :, :].rearrange("p c t -> p (c t)"), ps["SA"], ACT.Copy).then_inc(free["SA"], 1)
                take("OT", "stick", j)
                F(osb[:, j, :], ps["OT"][:, 0:T], ACT.Copy).then_inc(free["OT"], 1)

            def soft_exp_of(buf, lo, hi, h, part, mx, sm, value):
                act.wait_ge(soft_max, value)
                F(buf[:, h, lo:hi], buf[:, h, lo:hi], ACT.Exp, bias=mx[:, h, part:part + 1],
                  accum_out=sm[:, h, part:part + 1]).then_inc(soft_exp, 1)

            with act.Fori(0, DIL_HP) as i:
                for k, (s, g) in enumerate(DIL_ORDER):
                    if k == 7:
                        for h in range(2):
                            soft_exp_of(sd, 0, 384, h, 0, sm_max, sm_sum, i * 4 + (2 * h + 1))
                            soft_exp_of(sd, 384, 1152, h, 1, sm_max, sm_sum, i * 4 + (2 * h + 2))
                    dst = raw[:, g, s, :] if s < 2 else vd[:, g].rearrange("p t n -> p (t n)")
                    b = f"M{k % 2}"
                    take(b, "dilated", k // 2, i)
                    F(dst, ps[b][:, 0:T], ACT.Copy).then_inc(free[b], 1)
                    act.wait_ge(free[b], prior(b, "dilated", k // 2, i) + 1)
                    act.sem_inc(qkv_ready, 1)
                for h in range(2):
                    for g in range(DIL_G):
                        bank = f"T{g % 2}"
                        n = 3 + 2 * h + g // 2 if g % 2 == 0 else 3 + h
                        take(bank, "dilated", n, i)
                        F(pt[:, h, g, :], ps[bank][:, 0:384], ACT.Copy).then_inc(free[bank], 1)
                        act.wait_ge(free[bank], prior(bank, "dilated", n, i) + 1)
                        act.sem_inc(pt_ready, 1)
                take("OT", "dilated", 0, i)
                F(odl[:, bass.ds(i, 1), :].rearrange("p a t -> p (a t)"), ps["OT"][:, 0:T], ACT.Copy)\
                    .then_inc(free["OT"], 1)

            with act.Fori(0, 2) as i:
                for j in range(4):
                    for s, dst in enumerate((gate_a, gate_b)):
                        take(f"M{s}", "gates", 2 * j, i)
                        F(dst, ps[f"M{s}"][:, 0:T], ACT.Tanh, scale=0.5).then_inc(free[f"M{s}"], 1)

            act.wait_ge(rel_back, 16)
            F(warm[:, 2:3], eps[:, :], ACT.Sqrt)
            for tt in range(TT):
                tok = slice(tt * P, (tt + 1) * P)
                for c in range(KC):
                    act.wait_ge(*read(f"M{c % 2}", "out1", 4 * tt + c // 2))
                    F(tmp[:, c, tok], xT[:, c, tok], ACT.Square).then_inc(sq_ready, 1)
                take("SA", "norm2", tt)
                F(rt[:, tok], ps["SA"][:, 0:P], ACT.Sqrt, bias=eps[:, :], scale=1.0 / D).then_inc(free["SA"], 1)
                act.wait_ge(mod_ready, 12)
                for c in range(KC):
                    act.wait_ge(scaled, KC * (1 + tt) + c + 1)
                    F(hT[:, c, tok], tmp[:, c, tok], ACT.Identity, bias=mod[3][:, c:c + 1]).then_inc(h_ready, 1)
                for half, bank in enumerate(("S0", "S1")):
                    take(bank, "early", tt)
                    F(qT[:, half, tok], ps[bank][:, 0:P], ACT.Copy).then_inc(free[bank], 1)
                take("OT", "early", tt)
                F(sub[:, 2 * NK * tt:2 * NK * (tt + 1)], ps["OT"][:, 0:2 * NK], ACT.Copy).then_inc(free["OT"], 1)
                act.wait_ge(free["OT"], prior("OT", "early", tt) + 1)
                act.sem_inc(sub_ready, 1)
                for half in range(2):
                    take(f"T{half}", "rows", tt)
                    F(h_rows[:, tt, half * 512:(half + 1) * 512], ps[f"T{half}"], ACT.Copy).then_inc(free[f"T{half}"], 1)

            def scores(h):
                bank = ("SA", "OT")[h % 2]
                take(bank, "sub", (h - 1) // 2)
                F(sub[:, h * 512:(h + 1) * 512], ps[bank], ACT.Copy).then_inc(free[bank], 1)
                act.wait_ge(free[bank], prior(bank, "sub", (h - 1) // 2) + 1)
                act.sem_inc(sub_ready, 1)

            def queries(lo, hi):
                for k in range(lo, hi):
                    b = f"M{k % 2}"
                    take(b, "query", (k - 2) // 2)
                    F(qT[:, k % 4, :], ps[b][:, 0:T], ACT.Copy).then_inc(free[b], 1)
                    if k > lo and k % 2 == 0:
                        scores(k // 2 - 1)
                scores(hi // 2 - 1)

            def expert_weights(i, last=False):
                for s in range(2):
                    u = i * 2 + s
                    act.wait_ge(best_ready, u + 1)
                    F(gate_w[:, s, :], best_2[:, s, :], ACT.Exp, bias=gate_n[:, s, :], accum_out=gate_s[:, s, :])\
                        .then_inc(gate_exp, 1)
                    act.wait_ge(act_arg, u + 1)
                    F(act_t[:, s, :], act_b[:, s, :], ACT.Tanh, scale=GELU_C).then_inc(act_tanh, 1)
                    act.wait_ge(wgt_ready, u + 1)
                    for k in range(TOPK - LAST_ROWS if last and s == TT - 1 else TOPK):
                        act.wait_ge(v_used, u * TOPK + (k + 1 + VR - 8))
                        F(dg[:, k % 8, :], ident[:, :], ACT.Copy, scale=wgt[:, s, k:k + 1]).then_inc(diag_ready, 1)

            queries(2, 2 * FIRST_HEADS)
            expert_weights(0)
            queries(2 * FIRST_HEADS, 2 * NH)
            with act.Fori(1, NU // 2 - 1) as i:
                expert_weights(i)
            expert_weights(NU // 2 - 1, last=True)

            act.wait_ge(v_used, VR + TOPK * (NU - 1))
            F(y_rows[:, 0:D], wide[:, :], ACT.Copy).then_inc(y_ready, 1)
            norm(3, lambda c: read(f"T{c // 2 % 2}", "back", c // 4))
            norm(4, lambda c: (x_ready, c + 1))

            def zv_tanh_of(t):
                act.wait_ge(zv_arg, t + 1)
                F(g_th[:, t % 2, :], g_sq[:, t % 2, :], ACT.Tanh, scale=GELU_C).then_inc(zv_tanh, 1)

            for t in range(8):
                b = f"M{t % 2}"
                take(b, "sgu_v", t // 2)
                if t > 1:
                    act.wait_ge(zv_ready, t - 1)
                F(g_raw[:, t % 2, :], ps[b][:, 0:T], ACT.Copy).then_inc(free[b], 1)
                act.wait_ge(free[b], prior(b, "sgu_v", t // 2) + 1)
                F(g_sq[:, t % 2, :], g_raw[:, t % 2, :], ACT.Square).then_inc(zv_raw, 1)
                if t > 0:
                    zv_tanh_of(t - 1)
            zv_tanh_of(7)
            for tt in range(TT):
                act.wait_ge(ln_c, 1)
                F(zsq[:, tt, :], zv[:, tt, :], ACT.Square, bias=ln_m[:, tt:tt + 1], accum_out=ln_q[:, tt:tt + 1])\
                    .then_inc(ln_sq, 1)
            act.wait_ge(ln_sq, TT)
            F(ln_r, ln_q, ACT.Sqrt, bias=eps[:, :], scale=1.0 / D).then_inc(ln_root, 1)

            with act.Fori(0, 4) as i:
                for j in range(2):
                    k0 = 6 * j

                    def copy(k, dst):
                        b = f"M{k % 2}"
                        take(b, "mix", k // 2, i)
                        F(dst, ps[b][:, 0:T], ACT.Copy).then_inc(free[b], 1)
                        act.wait_ge(free[b], prior(b, "mix", k // 2, i) + 1)

                    copy(k0, q2)
                    act.sem_inc(qkv_ready, 1)
                    copy(k0 + 1, k2)
                    act.sem_inc(qkv_ready, 1)
                    for h in range(2):
                        soft_exp_of(s2, 0, P, h, 0, mx2, sm2, i * 8 + (8 + 4 * j + 2 * h + 1))
                        soft_exp_of(s2, P, 384, h, 1, mx2, sm2, i * 8 + (8 + 4 * j + 2 * h + 2))
                    copy(k0 + 2, v2.rearrange("p t n -> p (t n)"))
                    act.sem_inc(qkv_ready, 1)
                    act.wait_ge(merged_ready, i * 2 + (KC + j))
                    copy(k0 + 3, g_raw[:, 0, :])
                    F(g_sq[:, 0, :], g_raw[:, 0, :], ACT.Square).then_inc(u_raw, 1)
                    for h in range(2):
                        take(f"T{h}", "mix", j, i)
                        F(p2[:, h, :], ps[f"T{h}"][:, 0:384], ACT.Copy).then_inc(free[f"T{h}"], 1)
                        act.wait_ge(free[f"T{h}"], prior(f"T{h}", "mix", j, i) + 1)
                        act.sem_inc(pt_ready, 1)
                    act.wait_ge(u_arg, i * 2 + (j + 1))
                    F(g_th[:, 0, :], g_sq[:, 0, :], ACT.Tanh, scale=GELU_C).then_inc(u_tanh, 1)
                    for s, dst in enumerate((ga, gb)):
                        b = f"M{s}"
                        take(b, "mix", (k0 + 4 + s) // 2, i)
                        F(dst, ps[b][:, 0:T], ACT.Tanh, scale=0.5).then_inc(free[b], 1)

            norm(5, lambda c: read(f"M{c % 2}", "out2", c // 2))
            with act.Fori(0, 4) as i:
                for t in range(8):
                    b = f"M{t % 2}"
                    take(b, "ff1", t // 2, i)
                    act.wait_ge(ff_ready, i * 8 + (t + 1))
                    F(relu[:, t % 2, :], ps[b][:, 0:T], ACT.Relu).then_inc(free[b], 1)
            norm(6, lambda c: read(f"M{c % 2}", "ff2", 0, c // 2))
            with act.Fori(0, 2) as i:
                for j in range(4):
                    take("M0", "ple", j, i)
                    act.wait_ge(free["M1"], prior("M1", "ple", j, i))
                    F(gate_p[:, 0, :], ps["M0"][:, 0:T], ACT.Tanh, scale=0.5).then_inc(free["M0"], 1)
                    act.wait_ge(x_ready, i * 4 + (KC + j + 1))
                    F(tmp[:, bass.ds(i * 4 + j, 1), :], xT[:, bass.ds(i * 4 + j, 1), :], ACT.Square).then_inc(sq_ready, 1)
            norm(7, None)
            for g in range(2):
                take("T0", "final", g)
                F(o_rows[:, 0, g * 512:(g + 1) * 512], ps["T0"], ACT.Copy).then_inc(free["T0"], 1)

        @block.vector
        def _(dve):
            st = Steps(dve_step)
            V = nc.vector

            def take(bank, stage, k, i=0):
                dve.wait_ge(done[bank], prior(bank, stage, k, i) + 1)

            def own():
                dve.wait_ge(st.sem, st.now())

            def inverse_root(n):
                dve.wait_ge(free["SA"], prior("SA", f"norm{n}", 0) + 1)
                V.reciprocal(rstd[:, :], rt[:, :]).then_inc(st.tick(), 1)
                own()

            def norm(n, gains, dst, signal):
                if n > 1:
                    inverse_root(n)
                for c in range(KC):
                    V.scalar_tensor_tensor(dst[:, c, :], xT[:, c, :], gains[:, c:c + 1], rstd[:, :],
                                           ALU.mult, ALU.mult).then_inc(signal, 1)

            def ada_chunk(ch):
                a = ada_sum[:, ch % 3, :]
                lo = P if ch < 4 else 0
                a = a[:, lo:]
                landed, value, slot = ada_slot(ch)
                dve.wait_ge(landed, value)
                if ch >= 3:
                    dve.wait_ge(mod_ready, ch - 2)
                for c in range(KC):
                    w = slot[:, c, lo:]
                    if c == 0:
                        m = V.tensor_scalar(a, w, silu_c[:, 1, 0:1], None, ALU.mult)
                    else:
                        own()
                        m = V.scalar_tensor_tensor(a, w, silu_c[:, 1, c:c + 1], a, ALU.mult, ALU.add)
                    if c < KC - 1:
                        m.then_inc(st.tick(), 1)
                m.then_inc(ada_ready, 1)
                if ch >= 4:
                    dve.wait_ge(ada_ready, ch + 1)
                    dve.sem_inc(ada_used, 1)

            def ada_bias(ch):
                bank, stage, k = ada_sums(ch)
                take(bank, stage, k)
                V.tensor_tensor(modT[:, 4 * ch:4 * ch + 4], ps[bank][:, 0:4], b_ada_col[:, 4 * ch:4 * ch + 4], ALU.add)\
                    .then_inc(free[bank], 1)
                dve.wait_ge(free[bank], prior(bank, stage, k) + 1)
                dve.sem_inc(mod_ready, 1)

            dve.wait_ge(silu_half, 1)
            V.tensor_scalar(silu_c[:, 0, :], silu_c[:, 0, :], 0.5, 0.5, ALU.mult, ALU.add).then_inc(st.tick(), 1)
            own()
            V.tensor_tensor(silu_c[:, 1, :], silu_c[:, 0, :], col["c"], ALU.mult).then_inc(silu_ready, 1)
            dve.wait_ge(silu_ready, 1)
            ada_chunk(0)
            for ch in range(4):
                if ch < 3:
                    ada_chunk(ch + 1)
                ada_bias(ch)
                if ch == 1:
                    inverse_root(1)
            V.scalar_tensor_tensor(gain[:, 0, :], mod[1], 1.0, col["g_mix"], ALU.add, ALU.mult).then_inc(st.tick(), 1)
            own()
            norm(1, gain[:, 0, :], tmp, scaled)
            dve.wait_ge(const_in, 2 * 16)
            for j in range(SB_PAIRS):
                for h, bank in enumerate(("SA", "S0")):
                    take(bank, "stick", j)
                    V.scalar_tensor_tensor(zm[:, h, :], ps[bank][:, 0:384], SCALE, stick_neg, ALU.mult, ALU.add)\
                        .then_inc(free[bank], 1)
                if j < SB_PAIRS - 1:
                    ada_chunk(4 + 2 * j)
                if 0 < j < 3:
                    ada_bias(3 + 2 * j)
                for h in range(2):
                    dve.wait_ge(stick_ln, 2 * j + h + 1)
                    V.scalar_tensor_tensor(sp[:, h, :], zm[:, h, :], 0.0, ez[:, h, :], ALU.max, ALU.add)\
                        .then_inc(stick_sp, 1)
                for h in range(2):
                    take(f"T{h}", "stick", j)
                    V.tensor_tensor(zm[:, h, :], zm[:, h, :], ps[f"T{h}"][:, 0:384], ALU.subtract)\
                        .then_inc(free[f"T{h}"], 1)
                if j < SB_PAIRS - 1:
                    ada_bias(4 + 2 * j)
                if j < 2:
                    ada_chunk(5 + 2 * j)

            for e in (4, 5):
                bank, k = ("SA", "S1")[e % 2], (4, 5)[e % 2] + e // 2
                take(bank, "stick", k)
                V.tensor_tensor(sguT[:, 4 * (e - 4):4 * (e - 3), :], ps[bank].rearrange("p (a b) -> p a b", b=P),
                                sgu_mask.unsqueeze(1).broadcast_to([P, 4, P]), ALU.mult).then_inc(free[bank], 1)
            take("S1", "stick", 8)
            V.tensor_tensor(rel_row, ps["S1"][0:AH, 0:RMAX], rel_neg, ALU.add).then_inc(free["S1"], 1)
            dve.wait_ge(free["S1"], prior("S1", "stick", 8) + 1)
            dve.sem_inc(rel_out, 1)
            for ch in (9, 10, 11):
                ada_chunk(ch)
            dve.wait_ge(const2_in, 5 * 16)

            def soft_norm(buf, splits, h, sm, iv, value):
                dve.wait_ge(soft_exp, value)
                V.reciprocal(iv[:, h, :], sm[:, h, :]).then_inc(st.tick(), 1)
                own()
                for part, (lo, hi) in enumerate(splits):
                    V.tensor_scalar(buf[:, h, lo:hi], buf[:, h, lo:hi], iv[:, h, part:part + 1], None, ALU.mult)\
                        .then_inc(soft_p, 1)

            with dve.Fori(0, DIL_HP) as i:
                st.enter(i, 8)
                for g in range(DIL_G):
                    if g > 0:
                        dve.wait_ge(roped_ready, i * DIL_G + g)
                    for s in range(2):
                        take(f"T{s}", "dilated", g, i)
                        V.tensor_tensor(rope_b[:, s, :], ps[f"T{s}"][:, 0:T], sinT, ALU.mult).then_inc(free[f"T{s}"], 1)
                        V.tensor_tensor(rope_a[:, s, :], raw[:, g, s, :], cosT, ALU.mult).then_inc(st.tick(), 1)
                    own()
                    dve.wait_ge(free["T1"], prior("T1", "dilated", g, i) + 1)
                    V.tensor_tensor(roped[:, g], rope_a, rope_b, ALU.add).then_inc(roped_ready, 1)
                for h in range(2):
                    take("SA", "dilated", h, i)
                    V.scalar_tensor_tensor(sd[:, h, 0:384], ps["SA"][:, 0:384], SCALE, dil_neg[:, 0:384],
                                           ALU.mult, ALU.add).then_inc(free["SA"], 1)
                    take("S0", "dilated", h, i)
                    V.scalar_tensor_tensor(sd[:, h, 384:1152], wide[:, 0:768], SCALE, dil_neg[:, 384:1152],
                                           ALU.mult, ALU.add).then_inc(free["S0"], 1)
                    dve.wait_ge(free["S0"], prior("S0", "dilated", h, i) + 1)
                    V.tensor_reduce(sm_max[:, h, 0:1], sd[:, h, 0:384], AX.X, ALU.max, negate=True).then_inc(soft_max, 1)
                    V.tensor_reduce(sm_max[:, h, 1:2], sd[:, h, 384:1152], AX.X, ALU.max, negate=True)\
                        .then_inc(soft_max, 1)
                for h in range(2):
                    soft_norm(sd, ((0, 384), (384, 1152)), h, sm_sum, sm_inv, i * 4 + (2 * h + 2))
                st.leave(DIL_HP)

            for ch in (9, 10, 11):
                ada_bias(ch)
            V.scalar_tensor_tensor(gain[:, 1, :], mod[4], 1.0, col["g_ffn"], ALU.add, ALU.mult).then_inc(st.tick(), 1)
            with dve.Fori(0, 2) as i:
                st.enter(i, 8)
                for j in range(4):
                    for s, (g, br) in enumerate(((gate_a, br_a), (gate_b, br_b))):
                        dve.wait_ge(free[f"M{s}"], prior(f"M{s}", "gates", 2 * j, i) + 1)
                        V.tensor_scalar(g, g, 0.5, 0.5, ALU.mult, ALU.add).then_inc(st.tick(), 1)
                        take(f"M{s}", "gates", 2 * j + 1, i)
                        own()
                        V.tensor_tensor(br, g, ps[f"M{s}"][:, 0:T], ALU.mult).then_inc(free[f"M{s}"], 1)
                    for s in range(2):
                        dve.wait_ge(free[f"M{s}"], prior(f"M{s}", "gates", 2 * j + 1, i) + 1)
                    V.tensor_tensor(merged[:, bass.ds(i * 4 + j, 1), :].rearrange("p a t -> p (a t)"), br_a, br_b, ALU.add)\
                        .then_inc(merged_ready, 1)
                st.leave(2)
            def top16(vals, idx, src, work):
                own()
                dve.sem_inc(route_step, 1)
                V.max(vals[:, 0:8], src).then_inc(st.tick(), 1)
                own()
                dve.sem_inc(route_step, 1)
                V.max_index(idx[:, 0:8], vals[:, 0:8], src).then_inc(st.tick(), 1)
                V.match_replace(work, vals[:, 0:8], src, LOWEST).then_inc(st.tick(), 1)
                own()
                dve.sem_inc(route_step, 1)
                V.max(vals[:, 8:16], work).then_inc(st.tick(), 1)
                own()
                dve.sem_inc(route_step, 1)
                V.max_index(idx[:, 8:16], vals[:, 8:16], work).then_inc(st.tick(), 1)

            def route(u, s):
                V.tensor_copy(sub_w.rearrange("p a b -> p (a b)"), sub[:, bass.ds(u * (2 * NK), 2 * NK)])\
                    .then_inc(st.tick(), 1)
                for half in range(2):
                    top16(s16[:, half, :], i16[:, half, :], sub_w[:, half, :], cand_w[:, half * NK:(half + 1) * NK])
                own()
                V.tensor_copy(i16f, i16).then_inc(st.tick(), 1)
                V.tensor_tensor(cand, s16[:, 0, :].unsqueeze(2).broadcast_to([P, TOPK, TOPK]),
                                s16[:, 1, :].unsqueeze(1).broadcast_to([P, TOPK, TOPK]), ALU.add).then_inc(st.tick(), 1)
                best = best_2[:, s, :]
                top16(best, pos, cand.rearrange("p a b -> p (a b)"), cand_w)
                own()
                V.tensor_scalar(gate_n[:, s, :], best[:, 0:1], -1.0, None, ALU.mult).then_inc(best_ready, 1)
                V.tensor_scalar(pos_ab[:, 0, :], pos, 4, None, ALU.logical_shift_right).then_inc(st.tick(), 1)
                V.tensor_scalar(pos_ab[:, 1, :], pos, 15, None, ALU.bitwise_and).then_inc(st.tick(), 1)
                own()
                V.tensor_copy(pos_f, pos_ab).then_inc(st.tick(), 1)
                own()
                V.tensor_tensor(hot, pos_f.rearrange("p a k -> p (a k)").unsqueeze(2).broadcast_to([P, 2 * TOPK, TOPK]),
                                iota.unsqueeze(1).broadcast_to([P, 2 * TOPK, TOPK]), ALU.is_equal).then_inc(st.tick(), 1)
                own()
                for half in range(2):
                    part = hot[:, half * TOPK:(half + 1) * TOPK, :]
                    V.tensor_tensor(part, part, i16f[:, half, :].unsqueeze(1).broadcast_to([P, TOPK, TOPK]), ALU.mult)\
                        .then_inc(st.tick(), 1)
                own()
                V.tensor_reduce(pick.rearrange("p a k -> p (a k)"), hot, AX.X, ALU.add).then_inc(st.tick(), 1)
                own()
                V.scalar_tensor_tensor(expert_f, pick[:, 0, :], float(NK), pick[:, 1, :], ALU.mult, ALU.add)\
                    .then_inc(st.tick(), 1)
                own()
                V.tensor_copy(expert[:, s, :], expert_f).then_inc(idx_ready, 1)
            ROUTE_STEPS = 26

            def dots(u, s):
                for k in range(TOPK):
                    dve.wait_ge(u_in[k % 8], u * 32 + 16 * (k // 8 + 1))
                    if k >= 1 or not isinstance(u, int) or u > 0:
                        dve.wait_ge(u_used, u * TOPK + (k + 8))
                    V.scalar_tensor_tensor(dot_junk, u_ring[:, k % 8, :], 1.0, h_rows[:, s, :],
                                           ALU.mult, ALU.mult, accum_out=act_x[:, s, k:k + 1]).then_inc(u_used, 1)

            def weights(u, s):
                dve.wait_ge(u_used, u * TOPK + (TOPK + 8))
                x = act_x[:, s, :]
                V.tensor_tensor(act_a[:, s, :], x, x, ALU.mult).then_inc(st.tick(), 1)
                own()
                V.tensor_scalar(act_a[:, s, :], act_a[:, s, :], GELU_A, 1.0, ALU.mult, ALU.add).then_inc(st.tick(), 1)
                own()
                V.tensor_tensor(act_b[:, s, :], act_a[:, s, :], x, ALU.mult).then_inc(act_arg, 1)
                dve.wait_ge(gate_exp, u + 1)
                V.reciprocal(gate_r[:, s, :], gate_s[:, s, :]).then_inc(st.tick(), 1)
                own()
                V.tensor_scalar(gate_w[:, s, :], gate_w[:, s, :], gate_r[:, s, :], 0.5, ALU.mult, ALU.mult)\
                    .then_inc(st.tick(), 1)
                dve.wait_ge(act_tanh, u + 1)
                V.scalar_tensor_tensor(act_a[:, s, :], act_t[:, s, :], 1.0, x, ALU.add, ALU.mult).then_inc(st.tick(), 1)
                own()
                V.tensor_tensor(wgt[:, s, :], act_a[:, s, :], gate_w[:, s, :], ALU.mult).then_inc(wgt_ready, 1)

            DOT_STEPS = 5

            def out1_update(tt, blocks):
                tok = slice(tt * P, (tt + 1) * P)
                for t in blocks:
                    b = f"M{t % 2}"
                    take(b, "out1", 4 * tt + t // 2)
                    V.scalar_tensor_tensor(xT[:, t, tok], ps[b][:, 0:P], mod[2][:, t:t + 1], xT[:, t, tok],
                                           ALU.mult, ALU.add).then_inc(free[b], 1)

            def norm2(tt):
                tok = slice(tt * P, (tt + 1) * P)
                dve.wait_ge(free["SA"], prior("SA", "norm2", tt) + 1)
                V.reciprocal(rstd[:, tok], rt[:, tok]).then_inc(st.tick(), 1)
                own()
                for b in ("M0", "M1"):
                    dve.wait_ge(free[b], prior(b, "out1", 4 * tt + 4))
                for c in range(KC):
                    V.scalar_tensor_tensor(tmp[:, c, tok], xT[:, c, tok], gain[:, 1, c:c + 1], rstd[:, tok],
                                           ALU.mult, ALU.mult).then_inc(scaled, 1)

            out1_update(0, range(KC))
            out1_update(1, range(2))
            norm2(0)
            out1_update(1, range(2, 3))
            dve.wait_ge(sub_ready, 1)
            route(0, 0)
            dve.sem_inc(u_used, 8)
            out1_update(1, range(3, KC))
            norm2(1)
            for b in ("T0", "T1"):
                dve.wait_ge(free[b], prior(b, "rows", 0) + 1)
            dve.wait_ge(h_ready, 3 * KC)
            dots(0, 0)
            dve.wait_ge(sub_ready, 2)
            route(1, 1)
            weights(0, 0)
            for b in ("T0", "T1"):
                dve.wait_ge(free[b], prior(b, "back", 0))

            def unit(u, s):
                dots(u, s)
                weights(u, s)
                dve.wait_ge(v_used, u * TOPK + VR)
                route(u + 1, 1 - s)

            with dve.Fori(0, NU // 2 - 1) as i:
                st.enter(i, 2 * (ROUTE_STEPS + DOT_STEPS))
                dve.wait_ge(sub_ready, i + 3)
                unit(i * 2 + 1, 1)
                unit(i * 2 + 2, 0)
                st.leave(NU // 2 - 1)
            dots(NU - 1, 1)
            weights(NU - 1, 1)
            y_last = y_rows[:, D:2 * D]
            dve.wait_ge(wgt_ready, NU)
            for n in range(LAST_ROWS):
                k = TOPK - LAST_ROWS + n
                dve.wait_ge(v_in[k], 16 * NU)
                if n == 0:
                    m = V.tensor_scalar(y_last, v_ring[k], wgt[:, 1, k:k + 1], None, ALU.mult)
                else:
                    own()
                    m = V.scalar_tensor_tensor(y_last, v_ring[k], wgt[:, 1, k:k + 1], y_last, ALU.mult, ALU.add)
                m.then_inc(st.tick(), 1)
            own()
            dve.wait_ge(v_used, VR + TOPK * NU - LAST_ROWS)
            for n, b in enumerate(("T0", "T1")):
                half = y_last[:, n * 512:(n + 1) * 512]
                V.tensor_tensor(half, half, ps[b], ALU.add).then_inc(y_ready, 1)
            dve.sem_inc(y_ready, 1)
            for g in range(4):
                bank = f"T{g % 2}"
                take(bank, "back", g // 2)
                for n in range(2):
                    c = 2 * g + n
                    m = V.scalar_tensor_tensor(xT[:, c, :], ps[bank][:, n * T:(n + 1) * T], mod[5][:, c:c + 1], xT[:, c, :],
                                               ALU.mult, ALU.add)
                m.then_inc(free[bank], 1)
            for b in ("T0", "T1"):
                dve.wait_ge(free[b], prior(b, "back", 2))
            norm(3, col["g_final"], xT, x_ready)

            norm(4, col["norm_mix_g_2"], hT, h_ready)

            def gelu_arg(ready, value, signal, b):
                dve.wait_ge(ready, value)
                V.tensor_scalar(g_sq[:, b, :], g_sq[:, b, :], GELU_A, 1.0, ALU.mult, ALU.add).then_inc(st.tick(), 1)
                own()
                V.tensor_tensor(g_sq[:, b, :], g_sq[:, b, :], g_raw[:, b, :], ALU.mult).then_inc(signal, 1)

            def gelu_half(ready, value, b):
                dve.wait_ge(ready, value)
                V.tensor_scalar(g_th[:, b, :], g_th[:, b, :], 0.5, 0.5, ALU.mult, ALU.add).then_inc(st.tick(), 1)
                own()

            def zv_of(t):
                gelu_half(zv_tanh, t + 1, t % 2)
                for tt in range(TT):
                    m = V.scalar_tensor_tensor(zv[:, tt, t * P:(t + 1) * P], g_th[:, t % 2, tt * P:(tt + 1) * P], 1.0,
                                               g_raw[:, t % 2, tt * P:(tt + 1) * P], ALU.mult, ALU.mult,
                                               accum_out=ln_part[:, tt, t:t + 1])
                m.then_inc(zv_ready, 1)

            for t in range(8):
                gelu_arg(zv_raw, t + 1, zv_arg, t % 2)
                if t > 0:
                    zv_of(t - 1)
            zv_of(7)
            dve.wait_ge(zv_ready, 8)
            V.tensor_reduce(ln_s, ln_part, AX.X, ALU.add).then_inc(st.tick(), 1)
            own()
            V.tensor_scalar(ln_m, ln_s, -1.0 / D, None, ALU.mult).then_inc(ln_c, 1)
            dve.wait_ge(ln_c, 1)
            dve.wait_ge(layer2_in, 64)

            MIX_STEPS = 14
            with dve.Fori(0, 4) as i:
                st.enter(i, 2 * MIX_STEPS)
                for j in range(2):
                    jj = i * 2 + j
                    for h, bank in enumerate(("SA", "S0")):
                        take(bank, "mix", j, i)
                        V.scalar_tensor_tensor(s2[:, h, 0:P], ps[bank][:, 0:P], SCALE,
                                               rel[:, bass.ds(i * (4 * T) + ((2 * j + h) * T + P), P)], ALU.mult, ALU.add)\
                            .then_inc(st.tick(), 1)
                        V.scalar_tensor_tensor(s2[:, h, P:384], ps[bank][:, P:384], SCALE,
                                               rel[:, bass.ds(i * (4 * T) + (2 * j + h) * T, T)], ALU.mult, ALU.add)\
                            .then_inc(free[bank], 1)
                        dve.wait_ge(free[bank], prior(bank, "mix", j, i) + 1)
                        own()
                        V.tensor_reduce(mx2[:, h, 0:1], s2[:, h, 0:P], AX.X, ALU.max, negate=True).then_inc(soft_max, 1)
                        V.tensor_reduce(mx2[:, h, 1:2], s2[:, h, P:384], AX.X, ALU.max, negate=True).then_inc(soft_max, 1)
                    for h in range(2):
                        soft_norm(s2, ((0, P), (P, 384)), h, sm2, iv2, i * 8 + (8 + 4 * j + 2 * h + 2))
                    dve.wait_ge(ln_root, 1)
                    V.reciprocal(ln_i, ln_r).then_inc(st.tick(), 1)
                    own()
                    for tt in range(TT):
                        m = V.tensor_scalar(vst[:, tt, :], zv[:, tt, bass.ds(jj * P, P)], ln_m[:, tt:tt + 1],
                                            ln_i[:, tt:tt + 1], ALU.add, ALU.mult)
                    m.then_inc(st.tick(), 1)
                    own()
                    V.tensor_tensor(vst, vst, ln_g[:, bass.ds(jj * P, P)].unsqueeze(1).broadcast_to([P, TT, P]),
                                    ALU.mult).then_inc(st.tick(), 1)
                    own()
                    V.tensor_tensor(vst, vst, ln_b[:, bass.ds(jj * P, P)].unsqueeze(1).broadcast_to([P, TT, P]),
                                    ALU.add).then_inc(vst_ready, 1)
                    gelu_arg(u_raw, jj + 1, u_arg, 0)
                    gelu_half(u_tanh, jj + 1, 0)
                    V.tensor_tensor(u_act, g_th[:, 0, :], g_raw[:, 0, :], ALU.mult).then_inc(st.tick(), 1)
                    take("S1", "mix", j, i)
                    V.tensor_tensor(ya.rearrange("p (t n) -> p t n", n=P),
                                    ps["S1"][:, 0:T].rearrange("p (t n) -> p t n", n=P),
                                    bs_rows[:, bass.ds(jj * P, P)].unsqueeze(1).broadcast_to([P, TT, P]), ALU.add)\
                        .then_inc(free["S1"], 1)
                    dve.wait_ge(free["S1"], prior("S1", "mix", j, i) + 1)
                    own()
                    V.tensor_tensor(ya, ya, u_act, ALU.mult).then_inc(st.tick(), 1)
                    for s, g in enumerate((ga, gb)):
                        b = f"M{s}"
                        dve.wait_ge(free[b], prior(b, "mix", (6 * j + 4 + s) // 2, i) + 1)
                        V.tensor_scalar(g, g, 0.5, 0.5, ALU.mult, ALU.add).then_inc(st.tick(), 1)
                    own()
                    V.tensor_tensor(ya, ya, ga, ALU.mult).then_inc(st.tick(), 1)
                    take("OT", "mix", j, i)
                    V.tensor_tensor(gb, gb, ps["OT"][:, 0:T], ALU.mult).then_inc(free["OT"], 1)
                    dve.wait_ge(free["OT"], prior("OT", "mix", j, i) + 1)
                    own()
                    V.tensor_tensor(merged[:, bass.ds(jj, 1), :].rearrange("p a t -> p (a t)"), ya, gb, ALU.add)\
                        .then_inc(merged_ready, 1)
                st.leave(4)
            for t in range(KC):
                b = f"M{t % 2}"
                take(b, "out2", t // 2)
                V.tensor_tensor(xT[:, t, :], xT[:, t, :], ps[b][:, 0:T], ALU.add).then_inc(free[b], 1)
            for b in ("M0", "M1"):
                dve.wait_ge(free[b], prior(b, "out2", 4))
            norm(5, col["norm_ffn_g_2"], hT, h_ready)
            dve.sem_inc(ff_ready, 2)
            with dve.Fori(0, 4) as i:
                for t in range(8):
                    b = f"M{t % 2}"
                    dve.wait_ge(free[b], prior(b, "ff1", t // 2, i) + 1)
                    V.tensor_tensor(ffT[:, bass.ds(i * 8 + t, 1), :].rearrange("p a t -> p (a t)"), relu[:, t % 2, :],
                                    relu[:, t % 2, :], ALU.mult).then_inc(ff_ready, 1)
            with dve.Fori(0, 4) as i:
                for j in range(2):
                    b = f"M{j}"
                    take(b, "ff2", 0, i)
                    xs = xT[:, bass.ds(i * 2 + j, 1), :].rearrange("p a t -> p (a t)")
                    V.tensor_tensor(xs, xs, ps[b][:, 0:T], ALU.add).then_inc(free[b], 1)
            for b in ("M0", "M1"):
                dve.wait_ge(free[b], prior(b, "ff2", 1, 3))
            norm(6, col["norm_ple_g_2"], hT, h_ready)
            with dve.Fori(0, 2) as i:
                st.enter(i, 4)
                for j in range(4):
                    dve.wait_ge(free["M0"], prior("M0", "ple", j, i) + 1)
                    V.tensor_scalar(gate_p[:, 1, :], gate_p[:, 0, :], 0.5, 0.5, ALU.mult, ALU.add).then_inc(st.tick(), 1)
                    take("M1", "ple", j, i)
                    own()
                    V.tensor_tensor(prod_p[:, j % 2, :], gate_p[:, 1, :], ps["M1"][:, 0:T], ALU.mult)\
                        .then_inc(free["M1"], 1)
                    dve.wait_ge(free["M1"], prior("M1", "ple", j, i) + 1)
                    xs = xT[:, bass.ds(i * 4 + j, 1), :].rearrange("p a t -> p (a t)")
                    V.tensor_tensor(xs, xs, prod_p[:, j % 2, :], ALU.add).then_inc(x_ready, 1)
                st.leave(2)
            dve.wait_ge(x_ready, 2 * KC)
            norm(7, col["norm_final_g_2"], hT, h_ready)
            for g in range(2):
                take("T1", "final", g)
                V.tensor_copy(o_rows[:, 1, g * 512:(g + 1) * 512], ps["T1"]).then_inc(free["T1"], 1)


def shape_constants():
    f = np.float32
    p, t = np.arange(P), np.arange(T)
    half = HD // 2
    inv = (f(10000.0) ** (-np.arange(half, dtype=f) / f(half))).astype(f)
    ang = (t.astype(f)[:, None] * inv[None, :]).astype(f)
    K = {"ident": np.eye(P, dtype=f), "tri": (p[:, None] >= p[None, :]).astype(f),
         "cos": np.cos(ang).astype(f).T[p % half], "sin": np.sin(ang).astype(f).T[p % half]}
    rot = np.zeros((P, P), f)
    for j in range(P):
        if j % HD < half:
            rot[j + half, j] = -1
        else:
            rot[j - half, j] = 1
    K["rot"] = rot
    before = np.where(p[:, None] < p[None, :], 0, NEG)
    K["stick_neg"] = np.concatenate([before, np.zeros((P, P)), before], 1).astype(f)
    dist0, dist1 = p[:, None] - p[None, :], P + p[:, None] - t[None, :]
    ok = [[(d >= 0) & (d <= w) & (d % r == 0) for w, r in zip(DIL_WIN, DIL_RATE)] for d in (dist0, dist1)]
    K["dil_neg"] = np.concatenate([np.where(m, 0, NEG) for part in ok for m in part], 1).astype(f)
    K["sgu_mask"] = (p[:, None] <= p[None, :]).astype(f)
    n = np.maximum((T - 1) - np.arange(RMAX), 0)
    exact = NBUCK // 2
    large = exact + (np.log(np.maximum(n, exact).astype(f) / f(exact)) / f(np.log(1024 / exact)) * f(exact)).astype(np.int32)
    bucket = np.where(n < exact, n, np.minimum(large, NBUCK - 1))
    causal = np.arange(RMAX) <= T - 1
    K["rel_hot"] = ((np.arange(NBUCK)[:, None] == bucket[None, :]) & causal[None, :]).astype(f)
    K["rel_neg"] = np.broadcast_to(np.where(causal, 0, NEG), (AH, RMAX)).astype(f)
    K["iota"] = np.broadcast_to(np.arange(TOPK), (P, TOPK)).astype(f)
    return {n: np.ascontiguousarray(a) for n, a in K.items()}


def kernel(**inputs):
    import concourse.bacc as bacc
    from concourse.bass_utils import run_bass_kernel_spmd as run

    nc = bacc.Bacc("TRN2", target_bir_lowering=False, num_devices=1)
    arrays, A, K = {}, {}, {}
    for name, value in inputs.items():
        arrays[f"in_{name}"] = np.ascontiguousarray(value)
        A[name] = nc.dram_tensor(f"in_{name}", arrays[f"in_{name}"].shape, F32, kind="ExternalInput").ap()
    for name, value in shape_constants().items():
        arrays[f"const_{name}"] = value
        K[name] = nc.dram_tensor(f"const_{name}", value.shape, F32, kind="ExternalInput").ap()
    rel_rows = nc.dram_tensor("rel_rows", (AH, P, RMAX), F32).ap()
    out = nc.dram_tensor("out", (1, T, D), F32, kind="ExternalOutput").ap()
    build(nc, A, K, rel_rows, out)
    r = run(nc, [arrays], core_ids=[0])
    return r.results[0]["out"]
```
